# Optimizing a Trainium2 kernel written in Bass

```python
import jax, jax.numpy as jnp
from jax import lax
import numpy as np
import math

D_MODEL = 1024
BATCH = 1
SEQ = 1024
DEPTH = 2

CHUNK = 64
Q_BLOCK = 128
FOX_HEADS = 8
FOX_HEAD_DIM = 64
FOX_WIDTH = FOX_HEADS * FOX_HEAD_DIM
POOL_WINDOWS = (2, 4, 8, 16)
POOL_GROUPS = len(POOL_WINDOWS)
POOL_WIDTH = D_MODEL - FOX_WIDTH
POOL_GROUP_DIM = POOL_WIDTH // POOL_GROUPS
EVEN_IN_WIDTH = 3 * FOX_WIDTH + FOX_HEADS + POOL_WIDTH
LRU_WIDTH = D_MODEL
LRU_HEADS = 4
LRU_HEAD_DIM = LRU_WIDTH // LRU_HEADS
CONV_WIDTH = 4
LRU_C = 8.0
D_FF = -(-8 * D_MODEL // (3 * 256)) * 256
RMS_EPS = 1e-6


def rmsnorm(x, g):
    xf = x.astype(jnp.float32)
    y = xf * lax.rsqrt(jnp.mean(xf * xf, axis=-1, keepdims=True) + RMS_EPS)
    return (y * g.astype(jnp.float32)).astype(x.dtype)

def swiglu(h, w_gate, w_up, w_down):
    return (jax.nn.silu(h @ w_gate) * (h @ w_up)) @ w_down

def forgetting_attention(q, k, v, log_f):
    B, S, H, Dh = q.shape
    n_blk = S // Q_BLOCK
    scale = Dh ** -0.5
    c = jnp.cumsum(log_f, axis=1).transpose(0, 2, 1)
    q_blocks = q.reshape(B, n_blk, Q_BLOCK, H, Dh).transpose(1, 0, 3, 2, 4)
    c_blocks = c.reshape(B, H, n_blk, Q_BLOCK).transpose(2, 0, 1, 3)
    k_pos = jnp.arange(S, dtype=jnp.int32)

    def one_block(args):
        qb, cb, i = args
        s = jnp.einsum('bhqd,bshd->bhqs', qb, k, preferred_element_type=jnp.float32)
        s = s * scale + cb[..., None] - c[:, :, None, :]
        q_pos = i * Q_BLOCK + jnp.arange(Q_BLOCK, dtype=jnp.int32)
        mask = k_pos[None, :] <= q_pos[:, None]
        s = jnp.where(mask, s, -jnp.inf)
        p = jax.nn.softmax(s, axis=-1)
        return jnp.einsum('bhqs,bshd->bqhd', p.astype(v.dtype), v)

    out = lax.map(one_block, (q_blocks, c_blocks, jnp.arange(n_blk, dtype=jnp.int32)))
    return out.transpose(1, 0, 2, 3, 4).reshape(B, S, H * Dh)

def multiscale_pool(u, pool_w, pool_scale):
    B, S, _ = u.shape
    uf = u.astype(jnp.float32).reshape(B, S, POOL_GROUPS, POOL_GROUP_DIM)
    cs = jnp.cumsum(uf, axis=1)
    t1 = jnp.arange(1, S + 1, dtype=jnp.float32)
    pooled = []
    for g, w in enumerate(POOL_WINDOWS):
        cg = cs[:, :, g]
        lagged = jnp.pad(cg, ((0, 0), (w, 0), (0, 0)))[:, :S]
        mean = (cg - lagged) / jnp.minimum(t1, float(w))[None, :, None]
        pooled.append(mean - uf[:, :, g])
    pooled = jnp.stack(pooled, axis=2)
    mixed = jnp.einsum('bsgd,gde->bsge', pooled, pool_w.astype(jnp.float32))
    return (mixed.reshape(B, S, POOL_WIDTH) * pool_scale.astype(jnp.float32)).astype(u.dtype)

def even_mixer(h, w_in, b_f, pool_w, pool_scale, w_out):
    B, S, _ = h.shape
    proj = h @ w_in
    q, k, v, f_logit, u = jnp.split(
        proj, [FOX_WIDTH, 2 * FOX_WIDTH, 3 * FOX_WIDTH, 3 * FOX_WIDTH + FOX_HEADS], axis=-1)
    q = q.reshape(B, S, FOX_HEADS, FOX_HEAD_DIM)
    k = k.reshape(B, S, FOX_HEADS, FOX_HEAD_DIM)
    v = v.reshape(B, S, FOX_HEADS, FOX_HEAD_DIM)
    log_f = jax.nn.log_sigmoid(f_logit.astype(jnp.float32) + b_f.astype(jnp.float32))
    attn = forgetting_attention(q, k, v, log_f)
    pool = multiscale_pool(u, pool_w, pool_scale)
    return jnp.concatenate([attn, pool.astype(attn.dtype)], axis=-1) @ w_out

def causal_depthwise_conv(x, conv_w, conv_b):
    C = x.shape[-1]
    y = lax.conv_general_dilated(
        x, conv_w[:, None, :], window_strides=(1,), padding=[(CONV_WIDTH - 1, 0)],
        dimension_numbers=('NWC', 'WIO', 'NWC'), feature_group_count=C)
    return y + conv_b

def rg_lru(x, w_a, b_a, w_x, b_x, lam):
    B, S, W = x.shape
    xf = x.astype(jnp.float32)
    xh = xf.reshape(B, S, LRU_HEADS, LRU_HEAD_DIM)
    r = jax.nn.sigmoid(jnp.einsum('bshd,hde->bshe', xh, w_a.astype(jnp.float32)).reshape(B, S, W)
                       + b_a.astype(jnp.float32))
    i = jax.nn.sigmoid(jnp.einsum('bshd,hde->bshe', xh, w_x.astype(jnp.float32)).reshape(B, S, W)
                       + b_x.astype(jnp.float32))
    log_a = -LRU_C * r * jax.nn.softplus(-lam.astype(jnp.float32))
    a = jnp.exp(log_a)
    b = jnp.sqrt(-jnp.expm1(2.0 * log_a)) * (i * xf)

    def combine(c1, c2):
        a1, b1 = c1
        a2, b2 = c2
        return a1 * a2, a2 * b1 + b2

    _, hs = lax.associative_scan(combine, (a, b), axis=1)
    return hs.astype(x.dtype)

def odd_mixer(h, w_in, conv_w, conv_b, w_a, b_a, w_x, b_x, lam, w_out):
    proj = h @ w_in
    gate, xr = jnp.split(proj, 2, axis=-1)
    xr = causal_depthwise_conv(xr, conv_w, conv_b)
    y = rg_lru(xr, w_a, b_a, w_x, b_x, lam)
    return (jax.nn.gelu(gate) * y) @ w_out

def first_inputs(seed: int = 0) -> dict:
    key = jax.random.key(seed)
    ks = jax.random.split(key, 32)
    f32 = jnp.float32
    ne = (DEPTH + 1) // 2
    no = DEPTH // 2

    def nrm(k, shape, scale):
        return jax.random.normal(k, shape, f32) * scale

    def gain(k, shape):
        return 1.0 + 0.05 * jax.random.normal(k, shape, f32)

    u = jax.random.uniform(ks[24], (no, LRU_WIDTH), f32, minval=0.9, maxval=0.999)
    s = u ** (1.0 / LRU_C)
    lam = jnp.log(s) - jnp.log1p(-s)
    return {
        "x": jax.random.normal(ks[0], (BATCH, SEQ, D_MODEL), f32),
        "mix_pre_g": gain(ks[1], (DEPTH, D_MODEL)),
        "mix_post_g": gain(ks[2], (DEPTH, D_MODEL)),
        "ffn_pre_g": gain(ks[3], (DEPTH, D_MODEL)),
        "ffn_post_g": gain(ks[4], (DEPTH, D_MODEL)),
        "ffn_w_gate": nrm(ks[5], (DEPTH, D_MODEL, D_FF), D_MODEL ** -0.5),
        "ffn_w_up": nrm(ks[6], (DEPTH, D_MODEL, D_FF), D_MODEL ** -0.5),
        "ffn_w_down": nrm(ks[7], (DEPTH, D_FF, D_MODEL), D_FF ** -0.5),
        "ev_w_in": nrm(ks[8], (ne, D_MODEL, EVEN_IN_WIDTH), D_MODEL ** -0.5),
        "ev_b_f": jax.random.uniform(ks[9], (ne, FOX_HEADS), f32, minval=1.0, maxval=6.0),
        "ev_pool_w": nrm(ks[10], (ne, POOL_GROUPS, POOL_GROUP_DIM, POOL_GROUP_DIM), POOL_GROUP_DIM ** -0.5),
        "ev_pool_scale": 1.0 + 0.1 * jax.random.normal(ks[11], (ne, POOL_WIDTH), f32),
        "ev_w_out": nrm(ks[12], (ne, D_MODEL, D_MODEL), D_MODEL ** -0.5),
        "od_w_in": nrm(ks[13], (no, D_MODEL, 2 * LRU_WIDTH), D_MODEL ** -0.5),
        "od_conv_w": nrm(ks[14], (no, CONV_WIDTH, LRU_WIDTH), CONV_WIDTH ** -0.5),
        "od_conv_b": nrm(ks[15], (no, LRU_WIDTH), 0.01),
        "od_w_a": nrm(ks[16], (no, LRU_HEADS, LRU_HEAD_DIM, LRU_HEAD_DIM), LRU_HEAD_DIM ** -0.5),
        "od_b_a": nrm(ks[17], (no, LRU_WIDTH), 0.01),
        "od_w_x": nrm(ks[18], (no, LRU_HEADS, LRU_HEAD_DIM, LRU_HEAD_DIM), LRU_HEAD_DIM ** -0.5),
        "od_b_x": nrm(ks[19], (no, LRU_WIDTH), 0.01),
        "od_lam": lam,
        "od_w_out": nrm(ks[20], (no, LRU_WIDTH, D_MODEL), LRU_WIDTH ** -0.5),
    }

def first_block(x, mix_pre_g, mix_post_g, ffn_pre_g, ffn_post_g, ffn_w_gate, ffn_w_up, ffn_w_down,
              ev_w_in, ev_b_f, ev_pool_w, ev_pool_scale, ev_w_out,
              od_w_in, od_conv_w, od_conv_b, od_w_a, od_b_a, od_w_x, od_b_x, od_lam, od_w_out):
    for layer in range(DEPTH):
        h = rmsnorm(x, mix_pre_g[layer])
        if layer % 2 == 0:
            e = layer // 2
            m = even_mixer(h, ev_w_in[e], ev_b_f[e], ev_pool_w[e], ev_pool_scale[e], ev_w_out[e])
        else:
            o = layer // 2
            m = odd_mixer(h, od_w_in[o], od_conv_w[o], od_conv_b[o], od_w_a[o], od_b_a[o],
                          od_w_x[o], od_b_x[o], od_lam[o], od_w_out[o])
        x = x + rmsnorm(m, mix_post_g[layer])
        h = rmsnorm(x, ffn_pre_g[layer])
        x = x + rmsnorm(swiglu(h, ffn_w_gate[layer], ffn_w_up[layer], ffn_w_down[layer]), ffn_post_g[layer])
    return x


DEPTH_2 = 1

MLSTM_HEADS = 4
MLSTM_WIDTH = D_MODEL
MLSTM_HEAD_DIM = MLSTM_WIDTH // MLSTM_HEADS
MLSTM_CHUNK = 128
S5_WIDTH = D_MODEL // 2
S5_GROUP = 16
S5_GROUPS = S5_WIDTH // S5_GROUP
S5_STATE = 64
DT_MIN = 0.001
DT_MAX = 0.1
N_BRANCHES = 2
NORM_EPS = 1e-6
IN_TOTAL = 3 * MLSTM_WIDTH + 2 * MLSTM_HEADS + 2 * S5_WIDTH + N_BRANCHES * D_MODEL


def _split_points():
    sizes = (MLSTM_WIDTH, MLSTM_WIDTH, MLSTM_WIDTH, MLSTM_HEADS, MLSTM_HEADS,
             S5_WIDTH, S5_WIDTH, N_BRANCHES * D_MODEL)
    return [int(s) for s in np.cumsum(sizes)[:-1]]

def rmsnorm_2(x, g):
    xf = x.astype(jnp.float32)
    y = xf * lax.rsqrt(jnp.mean(xf * xf, axis=-1, keepdims=True) + NORM_EPS)
    return (y * g.astype(jnp.float32)).astype(x.dtype)

def causal_dwconv(u, w, b):
    K, C = w.shape
    y = lax.conv_general_dilated(u, w[:, None, :].astype(u.dtype), window_strides=(1,),
                                 padding=[(K - 1, 0)], dimension_numbers=('NWC', 'WIO', 'NWC'),
                                 feature_group_count=C)
    return y + b.astype(u.dtype)

def mlstm_chunkwise(q, k, v, ig, lf):
    Bsz, H, L, dh = q.shape
    Lc = MLSTM_CHUNK
    NC = L // Lc
    q = q.reshape(Bsz, H, NC, Lc, dh)
    k = k.reshape(Bsz, H, NC, Lc, dh) * (dh ** -0.5)
    v = v.reshape(Bsz, H, NC, Lc, dh)
    ig = ig.reshape(Bsz, H, NC, Lc)
    b = jnp.cumsum(lf.reshape(Bsz, H, NC, Lc), axis=-1)
    b_last = b[..., -1]
    w_end = b_last[..., None] - b + ig
    m_loc = jnp.max(w_end, axis=-1)
    e_end = jnp.exp(w_end - m_loc[..., None])
    C_loc = jnp.einsum('bhcs,bhcsd,bhcse->bhcde', e_end, v, k)
    n_loc = jnp.einsum('bhcs,bhcse->bhce', e_end, k)

    def step(carry, inp):
        C, n, m = carry
        C_l, n_l, m_l, bl = inp
        m_new = jnp.maximum(bl + m, m_l)
        a = jnp.exp(bl + m - m_new)
        s = jnp.exp(m_l - m_new)
        C_new = a[..., None, None] * C + s[..., None, None] * C_l
        n_new = a[..., None] * n + s[..., None] * n_l
        return (C_new, n_new, m_new), (C, n, m)

    init = (jnp.zeros((Bsz, H, dh, dh), jnp.float32), jnp.zeros((Bsz, H, dh), jnp.float32),
            jnp.full((Bsz, H), -jnp.inf, jnp.float32))
    xs = (jnp.moveaxis(C_loc, 2, 0), jnp.moveaxis(n_loc, 2, 0),
          jnp.moveaxis(m_loc, 2, 0), jnp.moveaxis(b_last, 2, 0))
    _, (C_prev, n_prev, m_prev) = lax.scan(step, init, xs)
    C_prev = jnp.moveaxis(C_prev, 0, 2)
    n_prev = jnp.moveaxis(n_prev, 0, 2)
    m_prev = jnp.moveaxis(m_prev, 0, 2)

    causal = jnp.tril(jnp.ones((Lc, Lc), dtype=bool))
    log_d = jnp.where(causal, b[..., :, None] - b[..., None, :] + ig[..., None, :], -jnp.inf)
    log_inter = b + m_prev[..., None]
    m_t = jnp.maximum(log_inter, jnp.max(log_d, axis=-1))
    dmat = jnp.exp(log_d - m_t[..., None])
    inter = jnp.exp(log_inter - m_t)
    s = jnp.einsum('bhctd,bhcsd->bhcts', q, k) * dmat
    num = jnp.einsum('bhcts,bhcsd->bhctd', s, v) + inter[..., None] * jnp.einsum('bhcde,bhcte->bhctd', C_prev, q)
    den = jnp.sum(s, axis=-1) + inter * jnp.einsum('bhce,bhcte->bhct', n_prev, q)
    h = num / jnp.maximum(jnp.abs(den), jnp.exp(-m_t))[..., None]
    return h.reshape(Bsz, H, L, dh)

def mlstm_branch(u_a, z_a, o_pre, i_pre, f_pre, conv_w, conv_b, w_q, w_k, w_v, b_i, b_f, head_g, skip):
    Bsz, L, _ = u_a.shape
    H, dh = MLSTM_HEADS, MLSTM_HEAD_DIM
    c = jax.nn.silu(causal_dwconv(u_a, conv_w, conv_b))
    ch = c.reshape(Bsz, L, H, dh)
    uh = u_a.reshape(Bsz, L, H, dh)
    q = jnp.einsum('blhd,hde->bhle', ch, w_q).astype(jnp.float32)
    k = jnp.einsum('blhd,hde->bhle', ch, w_k).astype(jnp.float32)
    v = jnp.einsum('blhd,hde->bhle', uh, w_v).astype(jnp.float32)
    ig = jnp.transpose(i_pre.astype(jnp.float32) + b_i.astype(jnp.float32), (0, 2, 1))
    lf = jax.nn.log_sigmoid(jnp.transpose(f_pre.astype(jnp.float32) + b_f.astype(jnp.float32), (0, 2, 1)))
    h = mlstm_chunkwise(q, k, v, ig, lf)
    o = jnp.transpose(jax.nn.sigmoid(o_pre.astype(jnp.float32)).reshape(Bsz, L, H, dh), (0, 2, 1, 3))
    h = o * h
    h = h * lax.rsqrt(jnp.mean(h * h, axis=-1, keepdims=True) + NORM_EPS)
    h = jnp.transpose(h, (0, 2, 1, 3)).reshape(Bsz, L, MLSTM_WIDTH) * head_g.astype(jnp.float32)
    h = h.astype(u_a.dtype) + skip * c
    return h * jax.nn.silu(z_a)

def s5_branch(u_b, z_b, lam_re, lam_im, log_dt, B_re, B_im, C_re, C_im, D_skip, w_glu, b_glu):
    Bsz, L, _ = u_b.shape
    u = u_b.astype(jnp.float32).reshape(Bsz, L, S5_GROUPS, S5_GROUP)
    dt = jnp.exp(log_dt.astype(jnp.float32))[:, None]
    lr = lam_re.astype(jnp.float32)
    li = lam_im.astype(jnp.float32)
    mag = jnp.exp(lr * dt)
    a_re = mag * jnp.cos(li * dt)
    a_im = mag * jnp.sin(li * dt)
    den = lr * lr + li * li
    nr = a_re - 1.0
    q_re = (nr * lr + a_im * li) / den
    q_im = (a_im * lr - nr * li) / den
    Br = B_re.astype(jnp.float32)
    Bi = B_im.astype(jnp.float32)
    bb_re = q_re[..., None] * Br - q_im[..., None] * Bi
    bb_im = q_re[..., None] * Bi + q_im[..., None] * Br
    bu_re = jnp.einsum('blgn,gpn->blgp', u, bb_re)
    bu_im = jnp.einsum('blgn,gpn->blgp', u, bb_im)
    a_re_b = jnp.broadcast_to(a_re, bu_re.shape)
    a_im_b = jnp.broadcast_to(a_im, bu_re.shape)

    def combine(e1, e2):
        a1r, a1i, b1r, b1i = e1
        a2r, a2i, b2r, b2i = e2
        return (a2r * a1r - a2i * a1i, a2r * a1i + a2i * a1r,
                a2r * b1r - a2i * b1i + b2r, a2r * b1i + a2i * b1r + b2i)

    _, _, s_re, s_im = lax.associative_scan(combine, (a_re_b, a_im_b, bu_re, bu_im), axis=1)
    y = (jnp.einsum('blgp,gnp->blgn', s_re, C_re.astype(jnp.float32))
         - jnp.einsum('blgp,gnp->blgn', s_im, C_im.astype(jnp.float32))
         + D_skip.astype(jnp.float32) * u)
    y = jax.nn.gelu(y.reshape(Bsz, L, S5_WIDTH)).astype(u_b.dtype)
    y = y * jax.nn.sigmoid(y @ w_glu + b_glu)
    return y * jax.nn.silu(z_b)

def second_inputs(seed: int = 0) -> dict:
    key = jax.random.key(seed)
    ks = jax.random.split(key, 32)
    f32 = jnp.float32
    nrm = lambda k, shape, scale: scale * jax.random.normal(k, shape, f32)
    H, dh, P, G, N = MLSTM_HEADS, MLSTM_HEAD_DIM, S5_STATE, S5_GROUPS, S5_GROUP
    x = jax.random.normal(ks[0], (BATCH, SEQ, D_MODEL), f32)
    norm_pre_g = 1.0 + nrm(ks[1], (DEPTH_2, D_MODEL), 0.02)
    w_in = nrm(ks[2], (DEPTH_2, D_MODEL, IN_TOTAL), D_MODEL ** -0.5)
    conv_w = nrm(ks[3], (DEPTH_2, CONV_WIDTH, MLSTM_WIDTH), CONV_WIDTH ** -0.5)
    conv_b = nrm(ks[4], (DEPTH_2, MLSTM_WIDTH), 0.01)
    w_q = nrm(ks[5], (DEPTH_2, H, dh, dh), dh ** -0.5)
    w_k = nrm(ks[6], (DEPTH_2, H, dh, dh), dh ** -0.5)
    w_v = nrm(ks[7], (DEPTH_2, H, dh, dh), dh ** -0.5)
    b_i = nrm(ks[8], (DEPTH_2, H), 0.1)
    b_f = 3.0 + 3.0 * jax.random.uniform(ks[9], (DEPTH_2, H), f32)
    head_g = 1.0 + nrm(ks[10], (DEPTH_2, MLSTM_WIDTH), 0.02)
    skip_a = 1.0 + nrm(ks[11], (DEPTH_2, MLSTM_WIDTH), 0.02)
    w_a_out = nrm(ks[12], (DEPTH_2, MLSTM_WIDTH, D_MODEL), MLSTM_WIDTH ** -0.5)
    lam_re = -0.5 + nrm(ks[13], (DEPTH_2, G, P), 0.01)
    lam_im = math.pi * jnp.arange(P, dtype=f32)[None, None, :] + nrm(ks[14], (DEPTH_2, G, P), 0.01)
    log_dt = math.log(DT_MIN) + (math.log(DT_MAX) - math.log(DT_MIN)) * jax.random.uniform(ks[15], (DEPTH_2, G), f32)
    B_re = nrm(ks[16], (DEPTH_2, G, P, N), (2.0 * N) ** -0.5)
    B_im = nrm(ks[17], (DEPTH_2, G, P, N), (2.0 * N) ** -0.5)
    C_re = nrm(ks[18], (DEPTH_2, G, N, P), P ** -0.5)
    C_im = nrm(ks[19], (DEPTH_2, G, N, P), P ** -0.5)
    D_skip = nrm(ks[20], (DEPTH_2, G, N), 1.0)
    w_glu = nrm(ks[21], (DEPTH_2, S5_WIDTH, S5_WIDTH), S5_WIDTH ** -0.5)
    b_glu = nrm(ks[22], (DEPTH_2, S5_WIDTH), 0.01)
    w_b_out = nrm(ks[23], (DEPTH_2, S5_WIDTH, D_MODEL), S5_WIDTH ** -0.5)
    w_o = nrm(ks[24], (DEPTH_2, D_MODEL, D_MODEL), D_MODEL ** -0.5)
    norm_post_g = 1.0 + nrm(ks[25], (DEPTH_2, D_MODEL), 0.02)
    return {"x": x, "norm_pre_g": norm_pre_g, "w_in": w_in, "conv_w": conv_w, "conv_b": conv_b,
            "w_q": w_q, "w_k": w_k, "w_v": w_v, "b_i": b_i, "b_f": b_f, "head_g": head_g,
            "skip_a": skip_a, "w_a_out": w_a_out, "lam_re": lam_re, "lam_im": lam_im,
            "log_dt": log_dt, "B_re": B_re, "B_im": B_im, "C_re": C_re, "C_im": C_im,
            "D_skip": D_skip, "w_glu": w_glu, "b_glu": b_glu, "w_b_out": w_b_out,
            "w_o": w_o, "norm_post_g": norm_post_g}

def second_block(x, norm_pre_g, w_in, conv_w, conv_b, w_q, w_k, w_v, b_i, b_f, head_g, skip_a,
              w_a_out, lam_re, lam_im, log_dt, B_re, B_im, C_re, C_im, D_skip, w_glu, b_glu,
              w_b_out, w_o, norm_post_g):
    h = x
    split_points = _split_points()
    for l in range(DEPTH_2):
        xn = rmsnorm_2(h, norm_pre_g[l])
        proj = xn @ w_in[l]
        u_a, z_a, o_a, i_a, f_a, u_b, z_b, g_pre = jnp.split(proj, split_points, axis=-1)
        y_a = mlstm_branch(u_a, z_a, o_a, i_a, f_a, conv_w[l], conv_b[l], w_q[l], w_k[l], w_v[l],
                           b_i[l], b_f[l], head_g[l], skip_a[l]) @ w_a_out[l]
        y_b = s5_branch(u_b, z_b, lam_re[l], lam_im[l], log_dt[l], B_re[l], B_im[l], C_re[l],
                        C_im[l], D_skip[l], w_glu[l], b_glu[l]) @ w_b_out[l]
        g = jax.nn.sigmoid(g_pre.astype(jnp.float32)).astype(h.dtype)
        merged = g[..., :D_MODEL] * y_a + g[..., D_MODEL:] * y_b
        h = h + rmsnorm_2(merged @ w_o[l], norm_post_g[l])
    return h


_first_inputs = second_inputs


def second_inputs(seed=0):
    import zlib

    import numpy as np

    out = dict(_first_inputs(seed))
    spreads = {}
    factors = {'conv_b': 5.774,
     'b_i': 64.0,
     'head_g': 106.726,
     'skip_a': 122.374,
     'lam_re': 64.0,
     'lam_im': 24.944,
     'log_dt': 25.152,
     'B_re': 35.128,
     'B_im': 34.912,
     'C_re': 35.144,
     'C_im': 35.192,
     'b_glu': 200.0,
     'norm_post_g': 32.216,
     'w_glu': 26.66,
     'D_skip': 3.917,
     'w_b_out': 3.627}
    for name, (base, spread) in spreads.items():
        noise = np.random.default_rng([zlib.crc32(name.encode()), seed]).standard_normal(out[name].shape)
        drawn = base * np.exp(spread * noise) if base else spread * noise
        out[name] = __import__('jax').numpy.asarray(drawn.astype(out[name].dtype))
    for name, factor in factors.items():
        out[name] = (out[name] * factor).astype(out[name].dtype)
    return out


_narrow_inputs = second_inputs


def second_inputs(seed=0):
    out = dict(_narrow_inputs(seed))
    wider = {'head_g': 4.75, 'skip_a': 4.66, 'b_glu': 11.17, 'norm_post_g': 3.15}
    for name, times in wider.items():
        mean = out[name].mean()
        out[name] = (mean + times * (out[name] - mean)).astype(out[name].dtype)
    return out


def setup_inputs(seed=0):
    out = dict(first_inputs(seed))
    for name, value in second_inputs(seed + 1).items():
        if name != "x":
            out[name + "_2"] = value
    return out


def reference(
    x, mix_pre_g, mix_post_g, ffn_pre_g, ffn_post_g, ffn_w_gate, ffn_w_up, ffn_w_down, ev_w_in,
    ev_b_f, ev_pool_w, ev_pool_scale, ev_w_out, od_w_in, od_conv_w, od_conv_b, od_w_a, od_b_a,
    od_w_x, od_b_x, od_lam, od_w_out, norm_pre_g_2, w_in_2, conv_w_2, conv_b_2, w_q_2, w_k_2,
    w_v_2, b_i_2, b_f_2, head_g_2, skip_a_2, w_a_out_2, lam_re_2, lam_im_2, log_dt_2, B_re_2,
    B_im_2, C_re_2, C_im_2, D_skip_2, w_glu_2, b_glu_2, w_b_out_2, w_o_2, norm_post_g_2,
):
    x = first_block(
        x, mix_pre_g, mix_post_g, ffn_pre_g, ffn_post_g, ffn_w_gate, ffn_w_up, ffn_w_down,
        ev_w_in, ev_b_f, ev_pool_w, ev_pool_scale, ev_w_out, od_w_in, od_conv_w, od_conv_b,
        od_w_a, od_b_a, od_w_x, od_b_x, od_lam, od_w_out,
    )
    return second_block(
        x, norm_pre_g_2, w_in_2, conv_w_2, conv_b_2, w_q_2, w_k_2, w_v_2, b_i_2, b_f_2,
        head_g_2, skip_a_2, w_a_out_2, lam_re_2, lam_im_2, log_dt_2, B_re_2, B_im_2, C_re_2,
        C_im_2, D_skip_2, w_glu_2, b_glu_2, w_b_out_2, w_o_2, norm_post_g_2,
    )


_drawn_inputs = setup_inputs


def setup_inputs(seed=0):
    import zlib

    import numpy as np

    out = dict(_drawn_inputs(seed))
    spreads = {}
    factors = {'od_b_a': 22.238, 'od_b_x': 8.0, 'b_i_2': 3.681, 'b_glu_2': 2.885}
    for name, (base, spread) in spreads.items():
        noise = np.random.default_rng([zlib.crc32(name.encode()), seed]).standard_normal(out[name].shape)
        drawn = base * np.exp(spread * noise) if base else spread * noise
        out[name] = __import__('jax').numpy.asarray(drawn.astype(out[name].dtype))
    for name, factor in factors.items():
        out[name] = (out[name] * factor).astype(out[name].dtype)
    return out
```

```python
import concourse.bass as bass
from concourse import mybir
import numpy as np

F32 = mybir.dt.float32
F32R = mybir.dt.float32r
BF16 = mybir.dt.bfloat16
ACT = mybir.ActivationFunctionType
ALU = mybir.AluOpType

P = 128
S = 1024
D = 1024
HALF = 512
KT = D // P
D_FF = 2816
FF_BLOCKS = D_FF // (2 * P)
FOX_WIDTH = 512
FOX_PAIRS = 4
LRU_HEADS = 4
MLSTM_HEADS = 4
POOL_WINDOWS = (2, 4, 8, 16)
PAD = 16
S5_TILES = 4
STATE_TILES = 16
POWERS = 10
LOW_POWERS = 5
LOW = 1 << LOW_POWERS
PRELUDE_ACT = 6
EPS = 1e-6
FILL = -3.0e38
GELU_C = 0.7978845608028654
GELU_A = 0.044715
SLOTS = 3

VECTORS = [("mix_pre0", 8), ("mix_pre1", 8), ("mix_post0", 8), ("mix_post1", 8),
           ("ffn_pre0", 8), ("ffn_pre1", 8), ("ffn_post0", 8), ("ffn_post1", 8),
           ("od_conv0", 8), ("od_conv1", 8), ("od_conv2", 8), ("od_conv3", 8), ("od_conv_b", 8),
           ("od_b_a", 8), ("od_b_x", 8), ("od_lam", 8), ("norm_pre", 8),
           ("ml_conv0", 8), ("ml_conv1", 8), ("ml_conv2", 8), ("ml_conv3", 8), ("ml_conv_b", 8),
           ("head_g", 8), ("skip", 8), ("norm_post", 8),
           ("pool_scale", 4), ("d_skip", 4), ("b_glu", 4),
           ("lam_re", 16), ("lam_im", 16), ("log_dt", 16), ("row_bias", 3), ("inv_count", 64)]
COLUMN, n_columns = {}, 0
for _name, _n in VECTORS:
    COLUMN[_name] = n_columns
    n_columns += _n


def column_chunk(w, c0, step=0):
    return [(w, 8, 128, 0, 0, c0, step, 0)]


def block_chunk(w, kt, n, r0, rstep, c0, cstep=0, at=0):
    return [(w, kt, n, r0, rstep, c0, cstep, at)]


def phases_of_the_stream(A):
    ev, od, w2 = A["ev_w_in"], A["od_w_in"], A["w_in_2"]

    def gate_up(l, b0, step):
        return [column_chunk(A["ffn_w_gate"][l], b0, step), column_chunk(A["ffn_w_up"][l], b0, step),
                column_chunk(A["ffn_w_gate"][l], b0 + P, step), column_chunk(A["ffn_w_up"][l], b0 + P, step)]

    def down(l, r0, step):
        return [block_chunk(A["ffn_w_down"][l], 2, HALF, r0, step, c) for c in (0, HALF)]

    def ffn(l):
        return [(f"ffn{l}_first", 1, gate_up(l, 0, 0)),
                (f"ffn{l}", (FF_BLOCKS - 1) // 2, gate_up(l, 256, 512) + down(l, 0, 512) + gate_up(l, 512, 512) + down(l, 256, 512)),
                (f"ffn{l}_last", 1, down(l, D_FF - 256, 0))]

    def lru_in(c0, step):
        return [column_chunk(od, D + c0, step), column_chunk(od, D + c0 + P, step),
                column_chunk(od, c0, step), column_chunk(od, c0 + P, step)]

    def lru_gates(r0, step):
        return [block_chunk(A["od_w_a"], 2, 256, r0, step, 0) + block_chunk(A["od_w_x"], 2, 256, r0, step, 0, 0, 512)]

    def lru_out(r0, step):
        return [block_chunk(A["od_w_out"], 2, HALF, r0, step, c) for c in (0, HALF)]

    def mlstm(step):
        return ([column_chunk(w2, 0, step), column_chunk(w2, P, step),
                 column_chunk(w2, 2048, step), column_chunk(w2, 2048 + P, step),
                 block_chunk(A["w_v_2"], 2, 256, 0, step, 0),
                 block_chunk(A["w_q_2"], 2, 256, 0, step, 0) + block_chunk(A["w_k_2"], 2, 256, 0, step, 0, 0, 512),
                 column_chunk(w2, 1024, step), column_chunk(w2, 1024 + P, step)]
                + [block_chunk(A["w_a_out_2"], 2, HALF, 0, step, c) for c in (0, HALF)])

    listed = ([("fox_pre", 1, [column_chunk(ev, 1536)] + [column_chunk(ev, 1544 + g * P) for g in range(4)]
                + [block_chunk(A["ev_pool_w"], 4, P, 0, 0, 0)]),
               ("fox", FOX_PAIRS, [column_chunk(ev, c, P) for c in (0, 512, 1024)]),
               ("fox_out", 2, [column_chunk(A["ev_w_out"], c * P, 512) for c in range(4)])]
              + ffn(0)
              + [("lru_first", 1, lru_in(0, 0) + lru_gates(0, 0)),
                 ("lru", LRU_HEADS - 1, lru_in(256, 256) + lru_out(0, 256) + lru_gates(256, 256)),
                 ("lru_last", 1, lru_out(768, 0))]
              + ffn(1)
              + [("s5_u", 1, [column_chunk(w2, 3080 + c * P) for c in range(S5_TILES)]),
                 ("glu", 1, [block_chunk(A["w_glu_2"], 4, 256, 0, 0, c) for c in (0, 256)]
                  + [column_chunk(w2, 3592 + c * P) for c in range(4)]),
                 ("ml_pre", 1, [column_chunk(w2, 3072), column_chunk(w2, 3076)]),
                 ("s5_out", 4, [block_chunk(A["w_b_out_2"], 4, 256, 0, 0, 0, 256),
                                column_chunk(w2, 4104 + D, 256), column_chunk(w2, 4104 + D + P, 256)]),
                 ("ml", MLSTM_HEADS, mlstm(256)),
                 ("merge", 2, [column_chunk(w2, 4104 + c * P, 512) for c in range(4)]),
                 ("final_out", 2, [column_chunk(A["w_o_2"], c * P, 512) for c in range(4)])])
    slots, out = {3: (0, 1, 2), 2: (0, 1), 4: (0, 1, 2, 1), 5: (0, 1, 2, 0, 1), 6: (0, 1, 2) * 2,
                  7: (0, 1, 2, 0, 1, 2, 1), 10: (0, 1, 2) * 3 + (1,), 12: (0, 1, 2) * 4}, []
    for name, count, body in listed:
        out.append((name, count, body, slots[len(body)]))
    return out


class Stream:

    def __init__(self, listed):
        self.of, self.body, self.count, uses, last, n = {}, {}, {}, [0] * SLOTS, [None] * SLOTS, 0
        for name, count, body, slots in listed:
            m = len(body)
            distance = [10 ** 6] * m
            first, start = n, list(uses)
            for i in range(count):
                for j, s in enumerate(slots):
                    if last[s] is not None:
                        distance[j] = min(distance[j], n - last[s])
                    last[s] = n
                    uses[s] += 1
                    n += 1
            per = [slots.count(s) for s in range(SLOTS)]
            rank = [slots[:j].count(s) for j, s in enumerate(slots)]
            self.of[name] = (first, m, slots, distance, start, per, rank)
            self.body[name], self.count[name] = body, count

    def slot(self, name, j):
        return self.of[name][2][j]

    def number(self, name, j, i=0):
        first, m = self.of[name][:2]
        return first + j + 1 + i * m

    def before(self, name, j, i=0):
        d = self.of[name][3][j]
        return None if d == 10 ** 6 else self.number(name, j, i) - d

    def loads(self, name, j, i=0):
        first, m, slots, _, start, per, rank = self.of[name]
        s = slots[j]
        return start[s] + rank[j] + 1 + i * per[s]


class Order:

    def __init__(self, engine, sem):
        self.engine, self.sem, self.n, self.i, self.per = engine, sem, 0, 0, 0

    def step(self, ins):
        ins.then_inc(self.sem, 1)
        self.n += 1
        return self.n

    def after(self, n):
        self.engine.wait_ge(self.sem, n + self.i * self.per if self.per else n)

    def __call__(self, ins):
        self.after(self.step(ins))

    def enter(self, i, per):
        self.i, self.per, self.entered = i, per, self.n

    def leave(self, count):
        assert self.n - self.entered == self.per, (self.n - self.entered, self.per)
        self.n, self.per = self.entered + count * self.per, 0


def block_program(nc, A, out_x):
    listed = phases_of_the_stream(A)
    stream = Stream(listed)

    place = [-(-nc.sbuf_base // 32) * 32]

    def fixed(name, shape, dt=F32):
        size = int(np.prod(shape[1:])) * (2 if dt == BF16 else 4)
        t = nc.alloc_sbuf_tensor_at(name, shape, dt, offset=place[0])
        place[0] += -(-size // 32) * 32
        return t

    H_hi, H_lo = fixed("H_hi", [P, KT, S], F32R), fixed("H_lo", [P, KT, S], F32R)
    y_at = place[0]
    Y = fixed("Y", [P, KT, S])
    raw = [fixed(f"raw{s}", [P, 1024]) for s in range(SLOTS)]
    w_hi = [fixed(f"w_hi{s}", [P, 1024], F32R) for s in range(SLOTS)]
    w_lo = [fixed(f"w_lo{s}", [P, 1024], F32R) for s in range(SLOTS)]
    par = fixed("par", [P, n_columns])
    ident = fixed("ident", [P, P])
    ident_b = fixed("ident_b", [P, P], BF16)
    causal_b = fixed("causal_b", [P, P], BF16)
    cap = fixed("cap", [P, P])
    ones = fixed("ones", [P, P])
    ones_r = fixed("ones_r", [P, P], F32R)
    eps_col = fixed("eps_col", [P, 1])
    one_col = fixed("one_col", [P, 1])
    half_bias = fixed("half_bias", [P, 20])
    decay4 = fixed("decay4", [P, 8])
    rot_re, rot_im = fixed("rot_re", [P, POWERS, 16]), fixed("rot_im", [P, POWERS, 16])
    gate_cols = fixed("gate_cols", [P, KT, 4])
    mag, q_re, q_im = (fixed(n, [P, 16]) for n in ("mag", "q_re", "q_im"))
    tmp_at = place[0]

    def carve(*wanted, keep=0):
        at, out = tmp_at + keep, []
        for name, shape, dt in wanted:
            size = int(np.prod(shape[1:])) * (2 if dt == BF16 else 4)
            out.append(nc.alloc_sbuf_tensor_at(name, shape, dt, offset=at))
            at += -(-size // 32) * 32
        assert at <= nc.sbuf_usable_end, (wanted[0][0], at - nc.sbuf_usable_end)
        return out

    ps = nc.alloc_psum_tensor("ps", [P, 8, HALF], F32)

    def pair(b):
        return ps[:, 2 * b:2 * b + 2, :].rearrange("p b n -> p (b n)")

    def tile(t, k, parts=slice(0, P)):
        if isinstance(k, int):
            return t[parts, k, :]
        return t[parts, bass.ds(k, 1), :].rearrange("p o n -> p (o n)")

    def col(name, k=0):
        return par[:, bass.ds(COLUMN[name] + k, 1)]

    def f32(ap):
        return ap.bitcast(F32)

    x_dram = nc.dram_tensor("x_dram", [KT, P, S], F32, kind="Internal").ap()
    rows_dram = nc.dram_tensor("rows_dram", [16, S], F32, kind="Internal").ap()
    part_dram = nc.dram_tensor("part_dram", [KT, P, S], F32, kind="Internal").ap()

    x_dram_t = x_dram.rearrange("k p n -> p k n")
    credits = []
    sems = {}

    def sem(name):
        if name not in sems:
            sems[name] = nc.alloc_semaphore(name)
        return sems[name]

    own_steps = {}

    def steps_of(e, name):
        if name not in own_steps:
            own_steps[name] = Order(e, sem(f"{name}_order"))
        return own_steps[name]

    def dve_steps(e):
        return steps_of(e, "dve")

    params_loaded, consts = sem("params_loaded"), sem("constants_made")

    loaded = [sem(f"chunk_loaded{s}") for s in range(SLOTS)]
    split_hi, split = sem("chunk_hi"), sem("chunk_split")
    multiplied = sem("chunk_multiplied")

    def chunks_once(sp, name, i):
        for j, parts in enumerate(stream.body[name]):
            s, before = stream.slot(name, j), stream.before(name, j, i)
            if before is not None:
                sp.wait_ge(split, before)
            for w, kt, n, r0, rstep, c0, cstep, at in parts:
                rows = bass.ds(r0 + rstep * i, kt * P) if rstep else slice(r0, r0 + kt * P)
                cols = bass.ds(c0 + cstep * i, n) if cstep else slice(c0, c0 + n)
                sp.dma_start(raw[s][:, at:at + kt * n].rearrange("p (k n) -> p k n", k=kt),
                             w[rows, cols].rearrange("(k p) n -> p k n", p=P)).then_inc(loaded[s], 32 // len(parts))

    def load_chunks(sp, name):
        if stream.count[name] == 1:
            chunks_once(sp, name, 0)
        else:
            with sp.Fori(0, stream.count[name]) as i:
                chunks_once(sp, name, i)

    def split_chunks(pool, name):
        count = stream.count[name]

        def once(i):
            for j, parts in enumerate(stream.body[name]):
                s, before = stream.slot(name, j), stream.before(name, j, i)
                n = sum(p[1] * p[2] for p in parts)
                pool.wait_ge(loaded[s], 32 * stream.loads(name, j, i))
                if before is not None:
                    pool.wait_ge(multiplied, before)
                pool.tensor_tensor(w_hi[s][:, :n], raw[s][:, :n], one_col[:, :].broadcast_to([P, n]), ALU.mult).then_inc(split_hi, 1)
                pool.wait_ge(split_hi, stream.number(name, j, i))
                pool.tensor_tensor(w_lo[s][:, :n], raw[s][:, :n], f32(w_hi[s][:, :n]), ALU.subtract).then_inc(split, 1)

        if count == 1:
            once(0)
        else:
            with pool.Fori(0, count) as i:
                once(i)

    def product(pe, o, l_hi, l_lo, r_hi, r_lo, first, last):
        pe.matmul(o, l_hi, r_hi, start=first, stop=False)
        pe.matmul(o, l_hi, r_lo, start=False, stop=False)
        return pe.matmul(o, l_lo, r_hi, start=False, stop=last)

    def columns(pe, s, bank, r_hi, r_lo, kt=KT, at=0, step=P, ready=None):
        for k in range(kt):
            if ready is not None:
                pe.wait_ge(ready[0], ready[1] + k + 1)
            w = slice(at + k * step, at + k * step + P)
            for h in range(2):
                t = slice(h * HALF, (h + 1) * HALF)
                last = product(pe, ps[:, 2 * bank + h, :], w_hi[s][:, w], w_lo[s][:, w],
                               r_hi[:, k, t], r_lo[:, k, t], k == 0, k == kt - 1)
        return last

    boundary_counts = {}

    def boundary(tag, post, pre, src, y_ready, tmp_free):
        n_post = KT if post else 0
        X, sq0, sq1, rstd, t0, t1 = carve(*[(f"{tag}_{n}", s, F32) for n, s in (
            ("X", [P, KT, S]), ("sq0", [P, S]), ("sq1", [P, S]), ("rstd", [P, S]), ("t0", [P, S]), ("t1", [P, S]))])
        sq, tmp = (sq0, sq1), (t0, t1)
        stats = int(bool(post)) + int(bool(pre))
        totals = dict(x_loaded=16, x_new=n_post, x_stored=16 * n_post, squared=KT * stats, summed=(KT - 1) * stats, all_summed=stats,
                      rooted=stats, h_full=KT if pre else 0, h_hi=KT if pre else 0, h_ready=KT if pre else 0)
        b = {n: boundary_counts.get(n, 0) for n in totals}
        for n in totals:
            boundary_counts[n] = b[n] + totals[n]
        x_loaded, x_new, x_stored, squared, summed, all_summed, rooted, h_full, h_hi, h_ready = (sem(f"boundary_{n}") for n in totals)

        def act(e):
            def squares(of, base, ready):
                with e.Fori(0, KT // 2) as i:
                    for t in range(2):
                        k = 2 * i + t
                        if ready is not None:
                            e.wait_ge(ready, b["x_new"] + k + 1)
                        e.wait_ge(summed, b["summed"] + base + k + 1)
                        e.activation(sq[t][:, :], tile(of, k), ACT.Square).then_inc(squared, 1)
                        if ready is not None:
                            e.dma_start(tile(x_dram_t, k), tile(X, k)).then_inc(x_stored, 16)

            for s, v in tmp_free:
                e.wait_ge(s, v)
            e.dma_start(X[:, :, :], src.rearrange("k p n -> p k n")).then_inc(x_loaded, 16)
            if post:
                for s, v in y_ready:
                    e.wait_ge(s, v)
                squares(Y, 0, None)
                e.wait_ge(all_summed, b["all_summed"] + 1)
                e.activation(rstd[:, :], pair(0), ACT.Sqrt, scale=1.0 / D, bias=eps_col[:, :]).then_inc(rooted, 1)
            if pre:
                if not post:
                    e.wait_ge(x_loaded, b["x_loaded"] + 16)
                squares(X, KT - 1 if post else 0, x_new if post else None)
                e.wait_ge(all_summed, b["all_summed"] + stats)
                if post:
                    e.wait_ge(x_new, b["x_new"] + KT)
                e.activation(rstd[:, :], pair(1), ACT.Sqrt, scale=1.0 / D, bias=eps_col[:, :]).then_inc(rooted, 1)
                with e.Fori(0, KT // 2) as i:
                    for t in range(2):
                        e.wait_ge(h_full, b["h_full"] + 2 * i + t + 1)
                        e.activation(tile(H_hi, 2 * i + t), tmp[t][:, :], ACT.Copy).then_inc(h_hi, 1)
            else:
                with e.Fori(0, KT) as k:
                    e.wait_ge(x_new, b["x_new"] + k + 1)
                    e.dma_start(tile(out_x.rearrange("k p n -> p k n"), k), tile(X, k)).then_inc(x_stored, 16)
                e.wait_ge(x_stored, b["x_stored"] + 16 * KT)

        def pe(e):
            def sums(bank, base, stat):
                def one(k, t, first, last):
                    e.wait_ge(squared, b["squared"] + base + k + 1)
                    for h in range(2):
                        ins = e.matmul(ps[:, 2 * bank + h, :], ones[:, :], sq[t][:, h * HALF:(h + 1) * HALF], start=first, stop=last)
                    return ins
                for k in range(KT):
                    ins = one(k, k % 2, k == 0, k == KT - 1)
                    ins.then_inc(all_summed if k == KT - 1 else summed, 1)

            if post:
                sums(0, 0, 1)
            if pre:
                sums(1, n_post, stats)

        def dve(e):
            o = dve_steps(e)
            if post:
                e.wait_ge(x_loaded, b["x_loaded"] + 16)
                e.wait_ge(rooted, b["rooted"] + 1)
                o(e.reciprocal(rstd[:, :], rstd[:, :]))
                with e.Fori(0, KT // 2) as i:
                    o.enter(i, 2)
                    for t in range(2):
                        k = 2 * i + t
                        o(e.scalar_tensor_tensor(tmp[t][:, :], tile(Y, k), col(post, k), rstd[:, :], ALU.mult, ALU.mult))
                        e.tensor_tensor(tile(X, k), tile(X, k), tmp[t][:, :], ALU.add).then_inc(x_new, 1)
                    e.wait_ge(x_new, b["x_new"] + 2 * i + 2)
                o.leave(KT // 2)
            if pre:
                e.wait_ge(rooted, b["rooted"] + stats)
                o(e.reciprocal(rstd[:, :], rstd[:, :]))

                def full(i, t):
                    e.scalar_tensor_tensor(tmp[t][:, :], tile(X, 2 * i + t), col(pre, 2 * i + t), rstd[:, :], ALU.mult, ALU.mult).then_inc(h_full, 1)

                def low(i, t):
                    e.wait_ge(h_hi, b["h_hi"] + 2 * i + t + 1)
                    k = 2 * i + t
                    e.tensor_tensor(tile(H_lo, k), tmp[t][:, :], f32(tile(H_hi, k)), ALU.subtract).then_inc(h_ready, 1)

                with e.Fori(0, KT // 2) as i:
                    full(i, 0)
                    full(i, 1)
                    low(i, 0)
                    low(i, 1)
                    e.wait_ge(h_ready, b["h_ready"] + 2 * i + 2)

        if b["summed"] == 0:
            credits.append((summed, 2))
        free = [(h_ready, b["h_ready"] + KT)] + ([(x_stored, b["x_stored"] + 16 * KT)] if post else [])
        return dict(act=act, pe=pe, dve=dve, h_ready=(h_ready, b["h_ready"]), tmp_free=free)

    def fox(h_ready, tmp_free):
        u0, u1, sum0, sum1, mixed, mix_hi, mix_lo, f_abs, f_min, negc_rows, ones_rows = carve(
            ("pool_u0", [P, PAD + S], F32), ("pool_u1", [P, PAD + S], F32), ("pool_sum0", [P, PAD + S], F32), ("pool_sum1", [P, PAD + S], F32),
            ("pool_mixed", [P, S], F32), ("pool_hi", [P, S], F32R), ("pool_lo", [P, S], F32R),
            ("f_abs", [8, S], F32), ("f_min", [8, S], F32), ("negc_rows", [8, S], F32), ("ones_rows", [8, S], F32))
        uu = (u0, u1)
        f_ln, negc_ready, negc_stored = (sem(f"fox_{n}") for n in ("f_ln", "negc_ready", "negc_stored"))
        u_ready, pool_mixed, pool_hi_done, pool_ready, pool_done, padded = (sem(f"fox_{n}") for n in ("u_ready", "pool_mixed", "pool_hi", "pool_ready", "pool_done", "padded"))
        NP = "fox_pre"

        q_hi, q_lo, k_hi, k_lo, v_t, v_hi, v_lo, negc_b, s0, s1, p0, p1, pt_hi, pt_lo, stat, waited = carve(
            ("q_hi", [P, S], F32R), ("q_lo", [P, S], F32R), ("k_hi", [P, S], F32R), ("k_lo", [P, S], F32R), ("v_t", [P, S], F32),
            ("v_hi", [P, KT, P], F32R), ("v_lo", [P, KT, P], F32R), ("negc_b", [P, 2, S], F32),
            ("s0", [P, S], F32), ("s1", [P, S], F32), ("p0", [P, S], F32), ("p1", [P, S], F32),
            ("pt_hi", [P, KT, 256], F32R), ("pt_lo", [P, KT, 256], F32R), ("fox_stat", [P, 16], F32), ("fox_waited", [P, 2 * KT], F32))
        s_sb, p_sb = (s0, s1), (p0, p1)
        qkv_hi, qk_split, vt_ready, vt_done, v_split = (sem(f"fox_{n}") for n in ("qkv_hi", "qk_split", "vt_ready", "vt_transposed", "v_split"))
        scored, maxed, neg_max, exped, p_ready, pt_done, pt_hi_done, pt_split, pv_done, attn_out = (
            sem(f"fox_{n}") for n in ("scored", "maxed", "neg_max", "exped", "p_ready", "pt_transposed", "pt_hi", "pt_split", "pv_done", "attn_out"))
        negc_loaded = sem("fox_negc_loaded")
        cat_hi, cat_ready, out_ready = sem("fox_cat_hi"), sem("fox_cat_ready"), sem("fox_out_ready")
        N = 2 * KT
        credits.extend([(maxed, N), (pt_split, N), (v_split, 1), (attn_out, N // 2), (pv_done, N // 2), (exped, N), (pt_done, N), (qk_split, 2)])

        def length(n):
            return (n % KT + 1) * P

        def sp(e):
            load_chunks(e, NP)
            e.wait_ge(negc_ready, 1)
            e.dma_start(rows_dram[0:8, :], negc_rows[:, :]).then_inc(negc_stored, 16)
            e.wait_ge(negc_stored, 16)
            with e.Fori(0, FOX_PAIRS) as j:
                chunks_once(e, "fox", j)
                e.wait_ge(maxed, N * j + N)
                for hd in range(2):
                    if hd == 0:
                        e.wait_ge(pool_done, 5)
                    e.dma_start(negc_b[:, hd, :], rows_dram[bass.ds(2 * j + hd, 1), :].broadcast_to([P, S])).then_inc(negc_loaded, 16)
            load_chunks(e, "fox_out")

        def pool(e):
            for s, v in tmp_free:
                e.wait_ge(s, v)
            for t in (u0, u1, sum0, sum1):
                e.memset(t[:, 0:PAD], 0.0).then_inc(padded, 1)
            e.memset(ones_rows[:, :], 1.0).then_inc(padded, 1)
            split_chunks(e, NP)
            split_chunks(e, "fox")
            split_chunks(e, "fox_out")

        def pe(e):
            e.wait_ge(split, stream.number(NP, 0))
            columns(e, 0, 0, H_hi, H_lo, ready=h_ready).then_inc(multiplied, 1)
            for g in range(4):
                e.wait_ge(split, stream.number(NP, 1 + g))
                bank = 1 + g % 3
                if g == 3:
                    e.wait_ge(u_ready, 1)
                columns(e, stream.slot(NP, 1 + g), bank, H_hi, H_lo).then_inc(multiplied, 1)
            e.wait_ge(split, stream.number(NP, 5))
            s = stream.slot(NP, 5)
            for g in range(4):
                e.wait_ge(pool_ready, g + 1)
                if g == 0:
                    e.wait_ge(negc_ready, 1)
                else:
                    e.wait_ge(pool_done, g)
                for h in range(2):
                    t = slice(h * HALF, (h + 1) * HALF)
                    ins = product(e, ps[:, h, :], w_hi[s][:, g * P:(g + 1) * P], w_lo[s][:, g * P:(g + 1) * P], mix_hi[:, t], mix_lo[:, t], True, True)
                ins.then_inc(multiplied if g == 3 else pool_mixed, 1)
            e.wait_ge(pool_done, 4)
            with e.Fori(0, FOX_PAIRS) as j:
                for c in range(3):
                    e.wait_ge(split, stream.number("fox", c, j))
                    if c < 2:
                        e.wait_ge(maxed, N * j + N - 1 + c)
                    else:
                        e.wait_ge(pt_split, N * j + N)
                    columns(e, stream.slot("fox", c), c, H_hi, H_lo).then_inc(multiplied, 1)
                e.wait_ge(vt_ready, j + 1)
                e.wait_ge(attn_out, (N // 2) * j + N // 2)
                for k in range(KT):
                    ins = e.transpose(ps[:, 6 + k // 4, (k % 4) * P:(k % 4 + 1) * P], v_t[:, k * P:(k + 1) * P], ident[:, :])
                ins.then_inc(vt_done, 1)
                for n in range(N + 2):
                    if n < N:
                        hd, i, bank = n // KT, n % KT, n % 2
                        r = slice(64 * hd, 64 * hd + 64)
                        if n == 0:
                            e.wait_ge(qk_split, 2 * j + 4)
                        elif n >= 2:
                            e.wait_ge(maxed, N * j + N + n - 1)
                        qs = slice(i * P, (i + 1) * P)
                        for h in range(2):
                            width = min(HALF, length(n) - h * HALF)
                            if width <= 0:
                                continue
                            o, ks = ps[:, 2 * bank + h, 0:width], slice(h * HALF, h * HALF + width)
                            ends = h == (length(n) - 1) // HALF
                            ins = product(e, o, q_hi[r, qs], q_lo[r, qs], k_hi[r, ks], k_lo[r, ks], True, not ends)
                            if ends:
                                ins = e.matmul(ps[:, 2 * bank + h, width - P:width], ident_b[:, :], causal_b[:, :], start=False, stop=True)
                        ins.then_inc(scored, 1)
                    if 1 <= n <= N:
                        m = n - 1
                        e.wait_ge(p_ready, N * j + m + 1)
                        e.wait_ge(pt_split, N * j + N + m)
                        for k in range(m % KT + 1):
                            ins = e.transpose(ps[:, 4 + k // 4, (k % 4) * P:(k % 4 + 1) * P], p_sb[m % 2][:, k * P:(k + 1) * P], ident[:, :])
                        ins.then_inc(pt_done, 1)
                    if n >= 3 and n % 2 == 1:
                        m = (n - 3) // 2
                        e.wait_ge(pt_split, N * j + N + n - 1)
                        if m == 0:
                            e.wait_ge(v_split, j + 2)
                        if m >= 2:
                            e.wait_ge(attn_out, (N // 2) * j + N // 2 + m - 1)
                        last = 2 * (m % (KT // 2)) + 1
                        for k in range(last + 1):
                            cols = slice(P, 256) if k == last else slice(0, 256)
                            ins = product(e, ps[:, 6 + m % 2, cols], v_hi[:, k, :], v_lo[:, k, :], pt_hi[:, k, cols], pt_lo[:, k, cols], k == 0, k == last)
                        ins.then_inc(pv_done, 1)
            with e.Fori(0, 2) as i:
                for c in range(4):
                    e.wait_ge(split, stream.number("fox_out", c, i))
                    e.wait_ge(cat_ready, KT)
                    e.wait_ge(out_ready, 4 * i + c + 1)
                    columns(e, stream.slot("fox_out", c), c, H_hi, H_lo).then_inc(multiplied, 1)
        credits.append((out_ready, 4))

        def act(e):
            a = steps_of(e, "act")
            for s, v in tmp_free:
                e.wait_ge(s, v)
            e.wait_ge(multiplied, stream.number(NP, 0))
            a(e.activation(f_abs[:, :], pair(0)[0:8, :], ACT.Abs, bias=par[0:8, COLUMN["row_bias"]:COLUMN["row_bias"] + 1]))
            a(e.activation(f_abs[:, :], f_abs[:, :], ACT.Exp, scale=-1.0))
            e.activation(f_abs[:, :], f_abs[:, :], ACT.Ln, bias=one_col[0:8, :]).then_inc(f_ln, 1)
            e.wait_ge(padded, 5)
            for g in range(4):
                e.wait_ge(multiplied, stream.number(NP, 1 + g))
                if g >= 2:
                    e.wait_ge(pool_ready, g - 1)
                e.activation(uu[g % 2][:, PAD:], pair(1 + g % 3), ACT.Copy).then_inc(u_ready, 1)
                if g >= 1:
                    split_mixed(e, g - 1)
            split_mixed(e, 3)
            with e.Fori(0, FOX_PAIRS) as j:
                e.wait_ge(pool_done, 5)
                e.wait_ge(multiplied, stream.number("fox", 0, j))
                e.activation(q_hi[:, :], pair(0), ACT.Copy, scale=0.125).then_inc(qkv_hi, 1)
                e.wait_ge(multiplied, stream.number("fox", 1, j))
                e.activation(k_hi[:, :], pair(1), ACT.Copy).then_inc(qkv_hi, 1)
                e.wait_ge(multiplied, stream.number("fox", 2, j))
                e.activation(v_t[:, :], pair(2), ACT.Copy).then_inc(vt_ready, 1)
                e.wait_ge(vt_done, j + 1)
                e.wait_ge(pv_done, (N // 2) * j + N // 2)
                e.activation(v_hi[:, :, :].rearrange("p k n -> p (k n)"), pair(3), ACT.Copy).then_inc(qkv_hi, 1)
                for n in range(N + 4):
                    if n < N:
                        ln = length(n)
                        e.wait_ge(neg_max, N * j + n + 1)
                        e.wait_ge(pt_done, N * j + N + n - 1)
                        e.activation(p_sb[n % 2][:, 0:ln], s_sb[n % 2][:, 0:ln], ACT.Exp, bias=stat[:, 2 + n % 2:3 + n % 2],
                                     accum_out=stat[:, 4 + n % 2:5 + n % 2]).then_inc(exped, 1)
                    if 1 <= n <= N:
                        m = n - 1
                        i = m % KT
                        e.wait_ge(pt_done, N * j + N + m + 1)
                        e.wait_ge(pv_done, (N // 2) * j + N // 2 + m // 2)
                        e.activation(pt_hi[:, 0:i + 1, (i % 2) * P:(i % 2 + 1) * P],
                                     pair(2)[:, 0:(i + 1) * P].rearrange("p (k n) -> p k n", n=P), ACT.Copy).then_inc(pt_hi_done, 1)
                    if n >= 4 and n % 2 == 0:
                        m = (n - 4) // 2
                        hd, c = m // (KT // 2), m % (KT // 2)
                        r = slice(64 * hd, 64 * hd + 64)
                        e.wait_ge(pv_done, (N // 2) * j + N // 2 + m + 1)
                        e.activation(tile(Y, j, r)[:, c * 256:(c + 1) * 256], ps[r, 6 + m % 2, 0:256], ACT.Copy).then_inc(attn_out, 1)
            e.wait_ge(attn_out, (N // 2) * (FOX_PAIRS + 1))
            e.wait_ge(pool_done, 5)
            e.wait_ge(multiplied, stream.number("fox", 2, FOX_PAIRS - 1))
            with e.Fori(0, KT) as k:
                e.activation(tile(H_hi, k), tile(Y, k), ACT.Copy).then_inc(cat_hi, 1)
            with e.Fori(0, 2) as i:
                for c in range(4):
                    e.wait_ge(multiplied, stream.number("fox_out", c, i))
                    e.activation(tile(Y, 4 * i + c), pair(c), ACT.Copy).then_inc(out_ready, 1)

        def split_mixed(e, g):
            e.wait_ge(pool_mixed_full, g + 1)
            if g >= 1:
                e.wait_ge(pool_mixed, g)
            e.activation(mix_hi[:, :], mixed[:, :], ACT.Copy).then_inc(pool_hi_done, 1)
        pool_mixed_full = sem("fox_pool_mixed_full")

        def dve(e):
            o = dve_steps(e)
            bias = par[0:8, COLUMN["row_bias"]:COLUMN["row_bias"] + 1]
            for s, v in tmp_free:
                e.wait_ge(s, v)
            e.wait_ge(sem("act_order"), PRELUDE_ACT + 1)
            o(e.tensor_scalar(f_min[:, :], pair(0)[0:8, :], bias, 0.0, ALU.add, ALU.min))
            e.wait_ge(f_ln, 1)
            o(e.tensor_tensor(f_min[:, :], f_abs[:, :], f_min[:, :], ALU.subtract))
            e.wait_ge(padded, 5)
            e.tensor_tensor_scan(negc_rows[:, :], ones_rows[:, :], f_min[:, :], 0.0, ALU.mult, ALU.add).then_inc(negc_ready, 1)
            for g, w in enumerate(POOL_WINDOWS):
                u, sums = uu[g % 2], (sum0, sum1)
                e.wait_ge(u_ready, g + 1)
                have, at = u, 1
                while at < w:
                    to = sums[0] if have is not sums[0] else sums[1]
                    o(e.tensor_tensor(to[:, PAD:], have[:, PAD:], have[:, PAD - at:PAD + S - at], ALU.add))
                    have, at = to, 2 * at
                if g >= 1:
                    e.wait_ge(pool_hi_done, g)
                o(e.scalar_tensor_tensor(mixed[:, :], have[:, PAD:], 1.0 / w, u[:, PAD:], ALU.mult, ALU.subtract))
                inv = par[:, COLUMN["inv_count"] + PAD * g:COLUMN["inv_count"] + PAD * (g + 1)]
                o(e.tensor_tensor(have[:, PAD:2 * PAD], have[:, PAD:2 * PAD], inv, ALU.mult))
                e.tensor_tensor(mixed[:, 0:PAD], have[:, PAD:2 * PAD], u[:, PAD:2 * PAD], ALU.subtract).then_inc(pool_mixed_full, 1)
                if g >= 1:
                    e.wait_ge(pool_mixed, g)
                    e.tensor_scalar(tile(Y, 3 + g), pair(0), col("pool_scale", g - 1), None, ALU.mult).then_inc(pool_done, 1)
                e.wait_ge(pool_hi_done, g + 1)
                e.tensor_tensor(mix_lo[:, :], mixed[:, :], f32(mix_hi[:, :]), ALU.subtract).then_inc(pool_ready, 1)
            e.wait_ge(multiplied, stream.number(NP, 5))
            o(e.tensor_scalar(tile(Y, 7), pair(0), col("pool_scale", 3), None, ALU.mult))
            e.wait_ge(negc_stored, 16)
            e.engine_nop().then_inc(pool_done, 2)
            with e.Fori(0, FOX_PAIRS) as j:
                o.enter(j, N)
                e.wait_ge(qkv_hi, 3 * j + 1)
                e.scalar_tensor_tensor(q_lo[:, :], pair(0), 0.125, f32(q_hi[:, :]), ALU.mult, ALU.subtract).then_inc(qk_split, 1)
                e.wait_ge(qkv_hi, 3 * j + 2)
                e.tensor_tensor(k_lo[:, :], pair(1), f32(k_hi[:, :]), ALU.subtract).then_inc(qk_split, 1)
                e.wait_ge(qkv_hi, 3 * j + 3)
                e.tensor_tensor(v_lo[:, :, :].rearrange("p k n -> p (k n)"), pair(3), f32(v_hi[:, :, :].rearrange("p k n -> p (k n)")), ALU.subtract).then_inc(v_split, 1)
                e.wait_ge(negc_loaded, 32 * j + 32)
                for n in range(N + 2):
                    if n < N:
                        ln, b = length(n), n % 2
                        e.wait_ge(scored, N * j + n + 1)
                        e.wait_ge(exped, N * j + N + n - 1)
                        e.memset(waited[:, n:n + 1], 0.0)
                        e.tensor_tensor_reduce(out=s_sb[b][:, 0:ln], in0=pair(b)[:, 0:ln], in1=negc_b[:, n // KT, 0:ln], scale=1.0, scalar=FILL,
                                               op0=ALU.add, op1=ALU.max, accum_out=stat[:, b:b + 1]).then_inc(maxed, 1)
                        e.wait_ge(maxed, N * j + N + n + 1)
                        e.tensor_scalar(stat[:, 2 + b:3 + b], stat[:, b:b + 1], -1.0, None, ALU.mult).then_inc(neg_max, 1)
                    if 1 <= n <= N:
                        m = n - 1
                        b, ln = m % 2, length(m)
                        e.wait_ge(exped, N * j + N + m + 1)
                        o(e.reciprocal(stat[:, 6 + b:7 + b], stat[:, 4 + b:5 + b]))
                        e.tensor_scalar(p_sb[b][:, 0:ln], p_sb[b][:, 0:ln], stat[:, 6 + b:7 + b], None, ALU.mult).then_inc(p_ready, 1)
                    if n >= 2:
                        m = n - 2
                        i = m % KT
                        e.wait_ge(pt_hi_done, N * j + m + 1)
                        cols = slice((i % 2) * P, (i % 2 + 1) * P)
                        e.tensor_tensor(pt_lo[:, 0:i + 1, cols], pair(2)[:, 0:(i + 1) * P].rearrange("p (k n) -> p k n", n=P),
                                        f32(pt_hi[:, 0:i + 1, cols]), ALU.subtract).then_inc(pt_split, 1)
                o.leave(FOX_PAIRS)
            with e.Fori(0, KT) as k:
                e.wait_ge(cat_hi, k + 1)
                e.tensor_tensor(tile(H_lo, k), tile(Y, k), f32(tile(H_hi, k)), ALU.subtract).then_inc(cat_ready, 1)

        return dict(sp=sp, pool=pool, pe=pe, act=act, dve=dve, y_ready=[(out_ready, 12)], tmp_free=[(out_ready, 12), (cat_ready, KT)])

    def ffn(l, h_ready, tmp_free):
        f_hi0, f_hi1, f_lo0, f_lo1, th0, th1, a0, a1, f0, f1 = carve(
            *[(f"ffn{l}_{n}", [P, 2, S], F32R) for n in ("f_hi0", "f_hi1", "f_lo0", "f_lo1")],
            *[(f"ffn{l}_{n}", [P, S], F32) for n in ("th0", "th1", "a0", "a1", "f0", "f1")])
        f_hi, f_lo, th, a, f = (f_hi0, f_hi1), (f_lo0, f_lo1), (th0, th1), (a0, a1), (f0, f1)
        tanh_done, gated, f_full, f_hi_done, f_ready, down_part, y_added = (
            sem(f"ffn_{n}") for n in ("tanh", "gated", "f_full", "f_hi", "f_ready", "down_part", "y_added"))
        LOOPS = (FF_BLOCKS - 1) // 2
        first, loop, tail = f"ffn{l}_first", f"ffn{l}", f"ffn{l}_last"
        if l == 0:
            credits.extend([(y_added, KT), (gated, 2)])
        B = l * FF_BLOCKS

        def pe_gate_up(e, b, name, at, i, ready=None):
            for c in range(4):
                e.wait_ge(split, stream.number(name, at + c, i))
                if ready is None:
                    e.wait_ge(f_full, 2 * (b - 1) + c // 2 + 1)
                    e.wait_ge(y_added, 8 * b - 4 + c + 1)
                columns(e, stream.slot(name, at + c), c, H_hi, H_lo, ready=ready if c == 0 else None).then_inc(multiplied, 1)

        def pe_down(e, b, par_, name, at, i, alone=False):
            for c in range(2):
                s = stream.slot(name, at + c)
                e.wait_ge(split, stream.number(name, at + c, i))
                if c == 0:
                    e.wait_ge(f_ready, 2 * b + 2)
                for q in range(4):
                    n = 4 * c + q
                    if n >= 4 or alone:
                        e.wait_ge(y_added, 8 * b + (n - 4) + 1 + 8)
                    else:
                        e.wait_ge(f_full, 2 * (b + 1) + q // 2 + 1)
                    ins = columns(e, s, q, f_hi[par_], f_lo[par_], kt=2, at=q * P, step=HALF)
                    ins.then_inc(multiplied if q == 3 else down_part, 1)

        def act_block(e, b, par_, name, at, i):
            for t in range(2):
                e.wait_ge(multiplied, stream.number(name, at + 2 * t, i))
                e.wait_ge(gated, 2 * b + t + 1)
                e.activation(th[t][:, :], pair(2 * t), ACT.Tanh, scale=0.5).then_inc(tanh_done, 1)
                e.wait_ge(f_full, 2 * b + t + 1)
                e.activation(f_hi[par_][:, t, :], f[t][:, :], ACT.Copy).then_inc(f_hi_done, 1)

        def dve_block(e, b, par_, name, at, i):
            for t in range(2):
                e.wait_ge(tanh_done, 2 * b + t + 1)
                e.scalar_tensor_tensor(a[t][:, :], th[t][:, :], 1.0, pair(2 * t), ALU.add, ALU.mult).then_inc(gated, 1)
                e.wait_ge(gated, 2 * b + t + 3)
                e.wait_ge(multiplied, stream.number(name, at + 2 * t + 1, i))
                e.scalar_tensor_tensor(f[t][:, :], a[t][:, :], 0.5, pair(2 * t + 1), ALU.mult, ALU.mult).then_inc(f_full, 1)
                e.wait_ge(f_hi_done, 2 * b + t + 1)
                e.tensor_tensor(f_lo[par_][:, t, :], f[t][:, :], f32(f_hi[par_][:, t, :]), ALU.subtract).then_inc(f_ready, 1)

        def dve_down(e, b, name, at, i):
            for n in range(KT):
                if n % 4 == 3:
                    e.wait_ge(multiplied, stream.number(name, at + n // 4, i))
                else:
                    e.wait_ge(down_part, 6 * b + 3 * (n // 4) + n % 4 + 1)
                e.tensor_tensor(Y[:, n, :], Y[:, n, :], pair(n % 4), ALU.add).then_inc(y_added, 1)
            e.wait_ge(y_added, 8 * b + 16)

        def sp(e):
            for name in (first, loop, tail):
                load_chunks(e, name)

        def pool(e):
            for name in (first, loop, tail):
                split_chunks(e, name)

        def pe(e):
            pe_gate_up(e, B, first, 0, 0, ready=h_ready)
            with e.Fori(0, LOOPS) as i:
                for u in range(2):
                    pe_gate_up(e, B + 2 * i + 1 + u, loop, 6 * u, i)
                    pe_down(e, B + 2 * i + u, u, loop, 6 * u + 4, i)
            pe_down(e, B + FF_BLOCKS - 1, 0, tail, 0, 0, alone=True)

        def act(e):
            for s, v in tmp_free:
                e.wait_ge(s, v)
            act_block(e, B, 0, first, 0, 0)
            with e.Fori(0, LOOPS) as i:
                for u in range(2):
                    e.wait_ge(y_added, 8 * (B + 2 * i + u) + 8)
                    act_block(e, B + 2 * i + 1 + u, 1 - u, loop, 6 * u, i)

        def dve(e):
            for s, v in tmp_free:
                e.wait_ge(s, v)
            dve_steps(e)(e.memset(Y[:, :, :], 0.0))
            dve_block(e, B, 0, first, 0, 0)
            with e.Fori(0, LOOPS) as i:
                for u in range(2):
                    dve_block(e, B + 2 * i + 1 + u, 1 - u, loop, 6 * u, i)
                    dve_down(e, B + 2 * i + u, loop, 6 * u + 4, i)
            dve_down(e, B + FF_BLOCKS - 1, tail, 0, 0)

        done = [(y_added, KT * (B + FF_BLOCKS + 1))]
        return dict(sp=sp, pool=pool, pe=pe, act=act, dve=dve, y_ready=done, tmp_free=done)

    def prelude():
        theta, turns, small, e8, s8, p8, t16, u16, v16 = carve(
            ("pre_theta", [P, POWERS, 16], F32), ("pre_turns", [P, POWERS, 16], F32), ("pre_small", [P, POWERS, 16], F32),
            ("pre_e8", [P, 8], F32), ("pre_s8", [P, 8], F32), ("pre_p8", [P, 8], F32),
            ("pre_t16", [P, 16], F32), ("pre_u16", [P, 16], F32), ("pre_v16", [P, 16], F32))

        def vec(name, n):
            return par[:, COLUMN[name]:COLUMN[name] + n]

        TURN = (6.28125, 0.0019350051879882812, 3.0199159819e-07)
        ROUND = 12582912.0
        marks = {}

        def dve(e):
            o = dve_steps(e)
            for k, (name, n) in enumerate((("od_b_a", 8), ("od_b_x", 8), ("b_glu", 4))):
                o(e.tensor_scalar(half_bias[:, 8 * k:8 * k + n], vec(name, n), 0.5, None, ALU.mult))
            e.wait_ge(sem("act_order"), 2)
            o(e.tensor_scalar(s8[:, :], e8[:, :], 2.0, None, ALU.add))
            o(e.reciprocal(s8[:, :], s8[:, :]))
            o(e.tensor_tensor(s8[:, :], s8[:, :], e8[:, :], ALU.mult))
            o(e.tensor_tensor(e8[:, :], s8[:, :], s8[:, :], ALU.mult))
            o(e.tensor_scalar(p8[:, :], e8[:, :], 1.0 / 19, 1.0 / 17, ALU.mult, ALU.add))
            for n in (15, 13, 11, 9, 7, 5, 3, 1):
                o(e.tensor_tensor(p8[:, :], p8[:, :], e8[:, :], ALU.mult))
                o(e.tensor_scalar(p8[:, :], p8[:, :], 1.0 / n, None, ALU.add))
            o(e.scalar_tensor_tensor(p8[:, :], p8[:, :], 2.0, s8[:, :], ALU.mult, ALU.mult))
            o(e.tensor_scalar(s8[:, :], vec("od_lam", 8), -1.0, 0.0, ALU.mult, ALU.max))
            o(e.tensor_tensor(p8[:, :], p8[:, :], s8[:, :], ALU.add))
            o(e.tensor_scalar(decay4[:, :], p8[:, :], -4.0, None, ALU.mult))
            e.wait_ge(sem("act_order"), 3)
            o(e.tensor_tensor(theta[:, 0, :], vec("lam_im", 16), t16[:, :], ALU.mult))
            o(e.tensor_tensor(u16[:, :], vec("lam_re", 16), t16[:, :], ALU.mult))
            marks["exponent"] = o.n
            for k in range(1, POWERS):
                o(e.tensor_scalar(theta[:, k, :], theta[:, 0, :], float(2 ** k), None, ALU.mult))
            o(e.tensor_scalar(turns[:, :, :], theta[:, :, :], 0.15915494309189535, None, ALU.mult))
            o(e.tensor_scalar(turns[:, :, :], turns[:, :, :], ROUND, ROUND, ALU.add, ALU.subtract))
            for part in TURN:
                o(e.scalar_tensor_tensor(theta[:, :, :], turns[:, :, :], -part, theta[:, :, :], ALU.mult, ALU.add))
            o(e.tensor_scalar(theta[:, :, :], theta[:, :, :], 3.1415925, -3.1415925, ALU.min, ALU.max))
            o(e.scalar_tensor_tensor(small[:, :, :], theta[:, :, :], -1.0, theta[:, :, :], ALU.mult, ALU.max))
            o(e.tensor_scalar(small[:, :, :], small[:, :, :], -1.0, 1.5707963267948966, ALU.mult, ALU.add))
            marks["angles"] = o.n
            e.wait_ge(sem("act_order"), 6)
            lr, li = vec("lam_re", 16), vec("lam_im", 16)
            o(e.tensor_tensor(t16[:, :], mag[:, :], rot_re[:, 0, :], ALU.mult))
            o(e.tensor_scalar(t16[:, :], t16[:, :], -1.0, None, ALU.add))
            o(e.tensor_tensor(u16[:, :], mag[:, :], rot_im[:, 0, :], ALU.mult))
            o(e.tensor_tensor(q_re[:, :], t16[:, :], lr, ALU.mult))
            o(e.tensor_tensor(v16[:, :], u16[:, :], li, ALU.mult))
            o(e.tensor_tensor(q_re[:, :], q_re[:, :], v16[:, :], ALU.add))
            o(e.tensor_tensor(q_im[:, :], u16[:, :], lr, ALU.mult))
            o(e.tensor_tensor(v16[:, :], t16[:, :], li, ALU.mult))
            o(e.tensor_tensor(q_im[:, :], q_im[:, :], v16[:, :], ALU.subtract))
            o(e.tensor_tensor(t16[:, :], lr, lr, ALU.mult))
            o(e.tensor_tensor(u16[:, :], li, li, ALU.mult))
            o(e.tensor_tensor(t16[:, :], t16[:, :], u16[:, :], ALU.add))
            o(e.reciprocal(t16[:, :], t16[:, :]))
            o(e.tensor_tensor(q_re[:, :], q_re[:, :], t16[:, :], ALU.mult))
            o(e.tensor_tensor(q_im[:, :], q_im[:, :], t16[:, :], ALU.mult))
            marks["end"] = o.n

        def act(e):
            a = steps_of(e, "act")
            a.step(e.activation(e8[:, :], vec("od_lam", 8), ACT.Abs))
            a.after(1)
            a.step(e.activation(e8[:, :], e8[:, :], ACT.Exp, scale=-1.0))
            a.step(e.activation(t16[:, :], vec("log_dt", 16), ACT.Exp))
            e.wait_ge(sem("dve_order"), EXPONENT)
            a.step(e.activation(mag[:, :], u16[:, :], ACT.Exp))
            e.wait_ge(sem("dve_order"), ANGLES)
            a.step(e.activation(rot_im[:, :, :], theta[:, :, :], ACT.Sin))
            a.step(e.activation(rot_re[:, :, :], small[:, :, :], ACT.Sin))

        EXPONENT, ANGLES, END = 30, 47, 62
        def checked(e):
            dve(e)
            assert (marks["exponent"], marks["angles"], marks["end"]) == (EXPONENT, ANGLES, END), marks

        return dict(dve=checked, act=act, tmp_free=[(sem("dve_order"), END)])

    def lru(h_ready, tmp_free):
        xpad, xc, xc_hi, xc_lo, G, out_hi, out_lo, T0, T1, T2, T3 = carve(
            ("lru_xpad", [P, 2, 3 + S], F32), ("lru_xc", [P, 2, S], F32), ("lru_xc_hi", [P, 2, S], F32R), ("lru_xc_lo", [P, 2, S], F32R),
            ("lru_G", [P, 2, S], F32), ("lru_out_hi", [P, 2, S], F32R), ("lru_out_lo", [P, 2, S], F32R),
            *[(f"lru_T{n}", [P, S], F32) for n in range(4)])
        names = ("x_read", "gate_in", "gate_sq", "gate_arg", "gate_tanh", "conv", "xc_hi", "xc_ready", "gates_read", "log_a", "a_tanh",
                 "root_arg", "root", "out_full", "out_hi", "out_ready", "y_added", "down_part", "wax_part")
        s = {n: sem(f"lru_{n}") for n in names}
        first, loop, tail = "lru_first", "lru", "lru_last"
        T = (T0, T1, T2, T3)
        credits.extend([(s["out_ready"], 2), (s["y_added"], KT)])

        def pe_in(e, j, name, i, ready=None):
            for c in range(4):
                e.wait_ge(split, stream.number(name, c, i))
                if ready is None:
                    e.wait_ge(s["gates_read"], 4 * (j - 1) + (1, 3, 2, 4)[c])
                columns(e, stream.slot(name, c), c, H_hi, H_lo, ready=ready if c == 0 else None).then_inc(multiplied, 1)

        def pe_out(e, j, name, at, i, alone=False):
            for c in range(2):
                sl = stream.slot(name, at + c)
                e.wait_ge(split, stream.number(name, at + c, i))
                e.wait_ge(s["out_ready"], 2 * j + 4)
                for q in range(4):
                    n = 4 * c + q
                    if n >= 4:
                        e.wait_ge(s["y_added"], 8 * j + (n - 4) + 1 + KT)
                    elif alone:
                        e.wait_ge(s["gates_read"], 4 * (j + 1))
                    elif n < 2:
                        e.wait_ge(s["x_read"], 2 * (j + 1) + n + 1)
                    else:
                        e.wait_ge(s["gate_sq"], 2 * (j + 1) + n - 1)
                    columns(e, sl, q, out_hi, out_lo, kt=2, at=q * P, step=HALF).then_inc(multiplied if q == 3 else s["down_part"], 1)

        def pe_gates(e, j, name, at, i, first_head=False):
            sl = stream.slot(name, at)
            e.wait_ge(split, stream.number(name, at, i))
            for c, bank in ((0, 0), (2, 2), (1, 1), (3, 3)):
                if c == 0:
                    e.wait_ge(s["xc_ready"], 2 * j + 2)
                if first_head:
                    if c < 2:
                        e.wait_ge(s["x_read"], 2)
                    else:
                        e.wait_ge(s["gate_sq"], 2)
                else:
                    e.wait_ge(s["y_added"], 8 * (j - 1) + 4 + bank + 1 + KT)
                columns(e, sl, bank, xc_hi, xc_lo, kt=2, at=HALF * (c // 2) + (c % 2) * P, step=256).then_inc(multiplied if c == 3 else s["wax_part"], 1)

        def act_in(e, j, name, i):
            for t in range(2):
                e.wait_ge(multiplied, stream.number(name, t, i))
                e.activation(xpad[:, t, 3:], pair(t), ACT.Copy).then_inc(s["x_read"], 1)
            for t in range(2):
                e.wait_ge(multiplied, stream.number(name, 2 + t, i))
                e.activation(G[:, t, :], pair(2 + t), ACT.Copy).then_inc(s["gate_in"], 1)
                e.activation(T[t][:, :], pair(2 + t), ACT.Square).then_inc(s["gate_sq"], 1)
            for t in range(2):
                e.wait_ge(s["conv"], 2 * j + t + 1)
                e.activation(xc_hi[:, t, :], xc[:, t, :], ACT.Copy).then_inc(s["xc_hi"], 1)
            for t in range(2):
                e.wait_ge(s["gate_arg"], 2 * j + t + 1)
                e.activation(T[t][:, :], T[t][:, :], ACT.Tanh, scale=GELU_C).then_inc(s["gate_tanh"], 1)

        def act_chain(e, j, name, at, i):
            for t in range(2):
                c = bass.ds(2 * j + t, 1)
                if t == 0:
                    e.wait_ge(s["wax_part"], 3 * j + 1)
                    e.wait_ge(s["gate_tanh"], 2 * j + 2)
                    e.wait_ge(s["out_ready"], 2 * j + 2)
                    e.wait_ge(s["gelu"], 2 * j + 2)
                else:
                    e.wait_ge(s["wax_part"], 3 * j + 3)
                    e.wait_ge(s["out_ready"], 2 * j + 3)
                e.activation(T[0][:, :], pair(t), ACT.Tanh, scale=0.5, bias=half_bias[:, c]).then_inc(s["gates_read"], 1)
                if t == 0:
                    e.wait_ge(s["wax_part"], 3 * j + 2)
                else:
                    e.wait_ge(multiplied, stream.number(name, at, i))
                e.activation(T[1][:, :], pair(2 + t), ACT.Tanh, scale=0.5, bias=half_bias[:, bass.ds(8 + 2 * j + t, 1)]).then_inc(s["gates_read"], 1)
                e.wait_ge(s["log_a"], 2 * j + t + 1)
                e.activation(T[2][:, :], T[0][:, :], ACT.Exp).then_inc(s["a_tanh"], 1)
                e.activation(T[3][:, :], T[0][:, :], ACT.Tanh).then_inc(s["a_tanh"], 1)
                e.wait_ge(s["root_arg"], 2 * j + t + 1)
                e.activation(T[0][:, :], T[0][:, :], ACT.Sqrt).then_inc(s["root"], 1)
                e.wait_ge(s["out_full"], 2 * j + t + 1)
                e.activation(out_hi[:, t, :], T[0][:, :], ACT.Copy).then_inc(s["out_hi"], 1)
        s["gelu"] = sem("lru_gelu")

        def dve_in(e, o, j):
            for t in range(2):
                e.wait_ge(s["x_read"], 2 * j + t + 1)
                o(e.tensor_scalar(xc[:, t, :], xpad[:, t, 3:], col("od_conv3", 2 * j + t), col("od_conv_b", 2 * j + t), ALU.mult, ALU.add))
                for back in (1, 2, 3):
                    ins = e.scalar_tensor_tensor(xc[:, t, :], xpad[:, t, 3 - back:3 - back + S], col(f"od_conv{3 - back}", 2 * j + t), xc[:, t, :], ALU.mult, ALU.add)
                    if back < 3:
                        o(ins)
                ins.then_inc(s["conv"], 1)
                e.wait_ge(s["xc_hi"], 2 * j + t + 1)
                e.tensor_tensor(xc_lo[:, t, :], xc[:, t, :], f32(xc_hi[:, t, :]), ALU.subtract).then_inc(s["xc_ready"], 1)
            for t in range(2):
                e.wait_ge(s["gate_sq"], 2 * j + t + 1)
                o(e.tensor_scalar(T[t][:, :], T[t][:, :], GELU_A, 1.0, ALU.mult, ALU.add))
                e.tensor_tensor(T[t][:, :], T[t][:, :], G[:, t, :], ALU.mult).then_inc(s["gate_arg"], 1)
            for t in range(2):
                e.wait_ge(s["gate_tanh"], 2 * j + t + 1)
                e.scalar_tensor_tensor(G[:, t, :], T[t][:, :], 1.0, G[:, t, :], ALU.add, ALU.mult).then_inc(s["gelu"], 1)
            e.wait_ge(s["gelu"], 2 * j + 2)

        def dve_chain(e, o, j):
            for t in range(2):
                c = decay4[:, bass.ds(2 * j + t, 1)]
                e.wait_ge(s["gates_read"], 4 * j + 2 * t + 1)
                e.tensor_scalar(T[0][:, :], T[0][:, :], c, c, ALU.mult, ALU.add).then_inc(s["log_a"], 1)
                e.wait_ge(s["gates_read"], 4 * j + 2 * t + 2)
                o(e.scalar_tensor_tensor(T[1][:, :], T[1][:, :], 1.0, xc[:, t, :], ALU.add, ALU.mult))
                e.wait_ge(s["a_tanh"], 4 * j + 2 * t + 2)
                o(e.tensor_scalar(T[0][:, :], T[3][:, :], -1.0, 1.0, ALU.mult, ALU.add))
                o(e.reciprocal(T[0][:, :], T[0][:, :]))
                e.scalar_tensor_tensor(T[0][:, :], T[3][:, :], -2.0, T[0][:, :], ALU.mult, ALU.mult).then_inc(s["root_arg"], 1)
                e.wait_ge(s["root"], 2 * j + t + 1)
                o(e.scalar_tensor_tensor(T[1][:, :], T[0][:, :], 0.5, T[1][:, :], ALU.mult, ALU.mult))
                o(e.tensor_tensor_scan(T[3][:, :], T[2][:, :], T[1][:, :], 0.0, ALU.mult, ALU.add))
                e.scalar_tensor_tensor(T[0][:, :], T[3][:, :], 0.5, G[:, t, :], ALU.mult, ALU.mult).then_inc(s["out_full"], 1)
                e.wait_ge(s["out_hi"], 2 * j + t + 1)
                e.tensor_tensor(out_lo[:, t, :], T[0][:, :], f32(out_hi[:, t, :]), ALU.subtract).then_inc(s["out_ready"], 1)
                e.wait_ge(s["out_ready"], 2 * j + t + 3)

        def dve_out(e, j, name, at, i):
            for n in range(KT):
                if n % 4 == 3:
                    e.wait_ge(multiplied, stream.number(name, at + n // 4, i))
                else:
                    e.wait_ge(s["down_part"], 6 * j + 3 * (n // 4) + n % 4 + 1)
                e.tensor_tensor(Y[:, n, :], Y[:, n, :], pair(n % 4), ALU.add).then_inc(s["y_added"], 1)
            e.wait_ge(s["y_added"], 8 * j + 2 * KT)

        IN_STEPS, CHAIN_STEPS = 8, 10

        def sp(e):
            for name in (first, loop, tail):
                load_chunks(e, name)

        def pool(e):
            for name in (first, loop, tail):
                split_chunks(e, name)

        def pe(e):
            pe_in(e, 0, first, 0, ready=h_ready)
            pe_gates(e, 0, first, 4, 0, first_head=True)
            with e.Fori(0, LRU_HEADS - 1) as i:
                pe_in(e, i + 1, loop, i)
                pe_out(e, i, loop, 4, i)
                pe_gates(e, i + 1, loop, 6, i)
            pe_out(e, LRU_HEADS - 1, tail, 0, 0, alone=True)

        def act(e):
            for w, v in tmp_free:
                e.wait_ge(w, v)
            act_in(e, 0, first, 0)
            act_chain(e, 0, first, 4, 0)
            with e.Fori(0, LRU_HEADS - 1) as i:
                e.wait_ge(s["out_ready"], 2 * i + 4)
                act_in(e, i + 1, loop, i)
                act_chain(e, i + 1, loop, 6, i)

        def dve(e):
            o = dve_steps(e)
            for w, v in tmp_free:
                e.wait_ge(w, v)
            o(e.memset(Y[:, :, :], 0.0))
            o(e.memset(xpad[:, :, 0:3], 0.0))
            dve_in(e, o, 0)
            dve_chain(e, o, 0)
            with e.Fori(0, LRU_HEADS - 1) as i:
                o.enter(i, IN_STEPS + CHAIN_STEPS)
                dve_in(e, o, i + 1)
                dve_out(e, i, loop, 4, i)
                dve_chain(e, o, i + 1)
            o.leave(LRU_HEADS - 1)
            dve_out(e, LRU_HEADS - 1, tail, 0, 0)

        done = [(s["y_added"], KT * (LRU_HEADS + 1))]
        return dict(sp=sp, pool=pool, pe=pe, act=act, dve=dve, y_ready=done, tmp_free=done)

    def s5(h_ready, tmp_free):
        u, b_map, c_map, cq, E0, E1, turned, p, t, s, x0, x1, low = carve(
            ("s5_u", [P, S5_TILES, S], F32), ("s5_b_map", [P, 1024], F32), ("s5_c_map", [P, 2, 4, P], F32), ("s5_cq", [P, 2, 4, P], F32),
            ("s5_E0", [P, 2, S], F32), ("s5_E1", [P, 2, S], F32), ("s5_turned", [P, 2, HALF], F32), ("s5_p", [P, 2, S], F32),
            ("s5_t", [P, 4, S], F32), ("s5_s", [P, 2, S], F32), ("s5_x0", [P, P], F32), ("s5_x1", [P, P], F32),
            ("s5_low", [P, STATE_TILES, 2, LOW], F32))
        ys_hi = nc.alloc_sbuf_tensor_at("ys_hi", [P, S5_TILES, S], F32R, offset=y_at)
        ys_lo = nc.alloc_sbuf_tensor_at("ys_lo", [P, S5_TILES, S], F32R, offset=y_at + S5_TILES * S * 4)
        E, LEVELS = (E0, E1), POWERS - LOW_POWERS
        (u_read, b_loaded, c_loaded, bu_done, p_read, p_used, E_ready, E_used, cq_ready, s_ready, cs_done, y_full, y_squared, y_arg,
         y_tanh, y_gelu, y_hi, ys_ready, low_ready, E_scaled) = (sem(f"s5_{n}") for n in (
             "u_read", "b_loaded", "c_loaded", "bu_done", "p_read", "p_used", "E_ready", "E_used", "cq_ready", "s_ready", "cs_done", "y_full",
             "y_squared", "y_arg", "y_tanh", "y_gelu", "y_hi", "ys_ready", "low_ready", "E_scaled"))
        credits.extend([(bu_done, 8), (cq_ready, 4), (p_read, 2), (p_used, 1), (E_used, 2), (cs_done, 1), (y_full, 1)])
        U = "s5_u"

        def sp(e):
            load_chunks(e, U)
            for w, v in tmp_free:
                e.wait_ge(w, v)
            with e.Fori(0, S5_TILES) as c:
                e.wait_ge(bu_done, 8 * c + 8)
                e.dma_start(b_map[:, :], A["s5_b"][bass.ds(P * c, P), :]).then_inc(b_loaded, 16)
                e.wait_ge(cq_ready, 4 * c + 4)
                e.dma_start(c_map[:, :, :, :].rearrange("p a s n -> p (a s n)"), A["s5_c"][bass.ds(P * c, P), :]).then_inc(c_loaded, 16)

        def pool(e):
            o = steps_of(e, "pool")
            split_chunks(e, U)
            for w, v in tmp_free:
                e.wait_ge(w, v)
            e.wait_ge(low_ready, 1)
            with e.Fori(0, STATE_TILES // 2) as i:
                o.enter(i, 2 * 3 * LEVELS)
                for b in range(2):
                    n = 2 * i + b
                    re, im = E[b][:, 0, :], E[b][:, 1, :]
                    e.wait_ge(E_used, n + 1)
                    e.tensor_copy(E[b][:, :, 0:LOW], low[:, bass.ds(n, 1), :, :].rearrange("p o a w -> p (o a) w")).then_inc(E_ready, 1)
                    for l in range(LEVELS):
                        w = LOW << l
                        ci = rot_im[:, LOW_POWERS + l, bass.ds(n, 1)].broadcast_to([P, w])
                        e.wait_ge(E_ready, (LEVELS + 1) * n + l + 1)
                        a = o.step(e.tensor_tensor(turned[:, 0, 0:w], im[:, 0:w], ci, ALU.mult))
                        d = o.step(e.tensor_tensor(turned[:, 1, 0:w], re[:, 0:w], ci, ALU.mult))
                        e.wait_ge(E_scaled, 2 * LEVELS * n + 2 * l + 2)
                        o.after(a)
                        o.step(e.tensor_tensor(re[:, w:2 * w], re[:, w:2 * w], turned[:, 0, 0:w], ALU.subtract))
                        o.after(d)
                        e.tensor_tensor(im[:, w:2 * w], im[:, w:2 * w], turned[:, 1, 0:w], ALU.add).then_inc(E_ready, 1)
                    e.wait_ge(E_ready, (LEVELS + 1) * (n + 1))
            o.leave(STATE_TILES // 2)

        def pe_inputs(e, c, st):
            n = 4 * c + st
            if st == 0:
                e.wait_ge(b_loaded, 16 * c + 16)
            e.wait_ge(p_read, 2 * n + 2)
            for part in range(2):
                for h in range(2):
                    ins = e.matmul(ps[:, 2 * part + h, :], b_map[:, part * HALF + st * P:part * HALF + (st + 1) * P],
                                   tile(u, c)[:, h * HALF:(h + 1) * HALF], start=True, stop=True)
                ins.then_inc(bu_done, 1)

        def pe_outputs(e, c, st):
            e.wait_ge(s_ready, 4 * c + st + 1)
            e.wait_ge(cq_ready, 4 * c + st + 5)
            if st == 0:
                e.wait_ge(y_full, c + 1)
            for part in range(2):
                for h in range(2):
                    ins = e.matmul(ps[:, 4 + h, :], cq[:, part, st, :], s[:, part, h * HALF:(h + 1) * HALF],
                                   start=st == 0 and part == 0, stop=st == 3 and part == 1)
            ins.then_inc(cs_done, 1)

        def pe(e):
            for c in range(S5_TILES):
                e.wait_ge(split, stream.number(U, c))
                columns(e, stream.slot(U, c), c, H_hi, H_lo, ready=h_ready if c == 0 else None).then_inc(multiplied, 1)
            e.wait_ge(u_read, S5_TILES)

            def tile_of_channels(c, last):
                for st in range(4):
                    if st < 3:
                        pe_inputs(e, c, st + 1)
                    elif not last:
                        pe_inputs(e, c + 1, 0)
                    pe_outputs(e, c, st)

            pe_inputs(e, 0, 0)
            with e.Fori(0, S5_TILES - 1) as c:
                tile_of_channels(c, False)
            tile_of_channels(S5_TILES - 1, True)

        def act(e):
            for w, v in tmp_free:
                e.wait_ge(w, v)
            for c in range(S5_TILES):
                e.wait_ge(multiplied, stream.number(U, c))
                e.activation(u[:, c, :], pair(c), ACT.Copy).then_inc(u_read, 1)

            def scale(c, st):
                n, buf = 4 * c + st, E[st % 2]
                for l in range(LEVELS):
                    w, cr = LOW << l, rot_re[:, LOW_POWERS + l, bass.ds(n, 1)]
                    e.wait_ge(E_ready, (LEVELS + 1) * n + l + 1)
                    for part in range(2):
                        e.activation(buf[:, part, w:2 * w], buf[:, part, 0:w], ACT.Copy, scale=cr).then_inc(E_scaled, 1)

            def inputs(c, st):
                n = 4 * c + st
                e.wait_ge(p_used, n + 1)
                for part in range(2):
                    e.wait_ge(bu_done, 2 * n + part + 9)
                    e.activation(p[:, part, :], pair(part), ACT.Copy).then_inc(p_read, 1)

            def tile_of_channels(c, last):
                for st in range(4):
                    if st < 3:
                        inputs(c, st + 1)
                    elif not last:
                        inputs(c + 1, 0)
                    if st < 2:
                        scale(c, st + 2)
                    elif not last:
                        scale(c + 1, st - 2)
                e.wait_ge(y_full, c + 2)
                e.activation(t[:, 1, :], t[:, 0, :], ACT.Square).then_inc(y_squared, 1)
                e.wait_ge(y_arg, c + 1)
                e.activation(t[:, 1, :], t[:, 1, :], ACT.Tanh, scale=GELU_C).then_inc(y_tanh, 1)
                e.wait_ge(y_gelu, c + 1)
                e.activation(tile(ys_hi, c), t[:, 2, :], ACT.Copy, scale=0.5).then_inc(y_hi, 1)

            scale(0, 0)
            inputs(0, 0)
            scale(0, 1)
            with e.Fori(0, S5_TILES - 1) as c:
                tile_of_channels(c, False)
            tile_of_channels(S5_TILES - 1, True)

        def dve(e):
            o = dve_steps(e)
            for w, v in tmp_free:
                e.wait_ge(w, v)

            def states(c, st):
                n = 4 * c + st
                Er, Ei = E[st % 2][:, 0, :], E[st % 2][:, 1, :]
                qr, qi = q_re[:, bass.ds(n, 1)], q_im[:, bass.ds(n, 1)]
                if st == 0:
                    e.wait_ge(c_loaded, 16 * c + 16)
                e.wait_ge(cs_done, n + 1)
                cr, ci = c_map[:, 0, st, :], c_map[:, 1, st, :]
                a = o.step(e.tensor_scalar(x0[:, :], ci, qi, None, ALU.mult))
                b = o.step(e.tensor_scalar(x1[:, :], cr, qi, None, ALU.mult))
                o.after(a)
                a = o.step(e.scalar_tensor_tensor(cq[:, 0, st, :], cr, qr, x0[:, :], ALU.mult, ALU.subtract))
                o.after(b)
                e.scalar_tensor_tensor(cq[:, 1, st, :], ci, qr, x1[:, :], ALU.mult, ALU.add).then_inc(cq_ready, 1)
                e.wait_ge(p_read, 2 * n + 4)
                e.wait_ge(E_ready, (LEVELS + 1) * (n + 1))
                o.step(e.tensor_tensor(t[:, 0, :], Er, p[:, 0, :], ALU.mult))
                a = o.step(e.tensor_tensor(t[:, 1, :], Ei, p[:, 1, :], ALU.mult))
                o.step(e.tensor_tensor(t[:, 2, :], Er, p[:, 1, :], ALU.mult))
                e.tensor_tensor(t[:, 3, :], Ei, p[:, 0, :], ALU.mult).then_inc(p_used, 1)
                o.after(a)
                a = o.step(e.tensor_tensor(t[:, 0, :], t[:, 0, :], t[:, 1, :], ALU.add))
                e.wait_ge(p_used, n + 2)
                b = o.step(e.tensor_tensor(t[:, 2, :], t[:, 2, :], t[:, 3, :], ALU.subtract))
                decay = mag[:, bass.ds(n, 1)].broadcast_to([P, S])
                o.after(a)
                a = o.step(e.tensor_tensor_scan(t[:, 1, :], decay, t[:, 0, :], 0.0, ALU.mult, ALU.add))
                o.after(b)
                b = o.step(e.tensor_tensor_scan(t[:, 3, :], decay, t[:, 2, :], 0.0, ALU.mult, ALU.add))
                o.after(b)
                a = o.step(e.tensor_tensor(t[:, 2, :], Ei, t[:, 3, :], ALU.mult))
                b = o.step(e.tensor_tensor(t[:, 0, :], Er, t[:, 1, :], ALU.mult))
                o.after(a)
                a = o.step(e.tensor_tensor(t[:, 3, :], Er, t[:, 3, :], ALU.mult))
                o.after(b)
                e.tensor_tensor(t[:, 1, :], Ei, t[:, 1, :], ALU.mult).then_inc(E_used, 1)
                b = o.step(e.tensor_tensor(s[:, 0, :], t[:, 0, :], t[:, 2, :], ALU.subtract))
                e.wait_ge(E_used, n + 3)
                e.scalar_tensor_tensor(s[:, 1, :], t[:, 3, :], -1.0, t[:, 1, :], ALU.mult, ALU.subtract).then_inc(s_ready, 1)
                e.wait_ge(s_ready, n + 1)

            def gelu(c):
                e.wait_ge(cs_done, 4 * c + 5)
                e.scalar_tensor_tensor(t[:, 0, :], tile(u, c), col("d_skip", c), pair(2), ALU.mult, ALU.add).then_inc(y_full, 1)
                e.wait_ge(y_squared, c + 1)
                o(e.tensor_scalar(t[:, 1, :], t[:, 1, :], GELU_A, 1.0, ALU.mult, ALU.add))
                e.tensor_tensor(t[:, 1, :], t[:, 1, :], t[:, 0, :], ALU.mult).then_inc(y_arg, 1)
                e.wait_ge(y_tanh, c + 1)
                e.scalar_tensor_tensor(t[:, 2, :], t[:, 1, :], 1.0, t[:, 0, :], ALU.add, ALU.mult).then_inc(y_gelu, 1)
                e.wait_ge(y_hi, c + 1)
                e.scalar_tensor_tensor(tile(ys_lo, c), t[:, 2, :], 0.5, f32(tile(ys_hi, c)), ALU.mult, ALU.subtract).then_inc(ys_ready, 1)
                e.wait_ge(ys_ready, c + 1)

            o.step(e.memset(low[:, :, 0, 0:1], 1.0))
            o(e.memset(low[:, :, 1, 0:1], 0.0))
            for k in range(LOW_POWERS):
                w = 1 << k
                re, im = low[:, :, 0, 0:w], low[:, :, 1, 0:w]
                re_up, im_up = low[:, :, 0, w:2 * w], low[:, :, 1, w:2 * w]
                a, b = (t[:, n, 0:STATE_TILES * w].rearrange("p (n w) -> p n w", w=w) for n in range(2))
                cr, ci = (r[:, k, :].rearrange("p (n o) -> p n o", o=1).broadcast_to([P, STATE_TILES, w]) for r in (rot_re, rot_im))
                o.step(e.tensor_tensor(a, im, ci, ALU.mult))
                o.step(e.tensor_tensor(b, re, ci, ALU.mult))
                o.step(e.tensor_tensor(re_up, re, cr, ALU.mult))
                o(e.tensor_tensor(im_up, im, cr, ALU.mult))
                o.step(e.tensor_tensor(re_up, re_up, a, ALU.subtract))
                if k < LOW_POWERS - 1:
                    o(e.tensor_tensor(im_up, im_up, b, ALU.add))
                else:
                    e.tensor_tensor(im_up, im_up, b, ALU.add).then_inc(low_ready, 1)
                    e.wait_ge(low_ready, 1)

            states(0, 0)
            per = 4 * 14 + 1
            with e.Fori(0, S5_TILES - 1) as c:
                o.enter(c, per)
                for st in range(1, 4):
                    states(c, st)
                states(c + 1, 0)
                gelu(c)
            o.leave(S5_TILES - 1)
            for st in range(1, 4):
                states(S5_TILES - 1, st)
            gelu(S5_TILES - 1)

        done = [(ys_ready, S5_TILES)]
        return dict(sp=sp, pool=pool, pe=pe, act=act, dve=dve, ys=(ys_hi, ys_lo), ready=done, tmp_free=done)

    def glu(ys, ready):
        ys_hi, ys_lo = ys
        yo_hi, yo_lo, th, tz0, tz1, y0, y1 = carve(
            ("yo_hi", [P, 4, S], F32R), ("yo_lo", [P, 4, S], F32R), ("glu_th", [P, 4, S], F32), ("glu_tz0", [P, S], F32),
            ("glu_tz1", [P, S], F32), ("glu_y0", [P, S], F32), ("glu_y1", [P, S], F32))
        tz, y = (tz0, tz1), (y0, y1)
        part, th_done, gated, tz_done, full, hi_done, yo_ready = (
            sem(f"glu_{n}") for n in ("part", "th", "gated", "tz", "full", "hi", "yo_ready"))
        G = "glu"

        def sp(e):
            load_chunks(e, G)

        def pool(e):
            split_chunks(e, G)

        def pe(e):
            for w, v in ready:
                e.wait_ge(w, v)
            for n in range(4):
                e.wait_ge(split, stream.number(G, n // 2))
                columns(e, stream.slot(G, n // 2), n, ys_hi, ys_lo, kt=4, at=(n % 2) * P, step=256).then_inc(multiplied if n % 2 else part, 1)
            for n in range(4):
                e.wait_ge(split, stream.number(G, 2 + n))
                e.wait_ge(th_done, n + 1)
                columns(e, stream.slot(G, 2 + n), n, H_hi, H_lo).then_inc(multiplied, 1)

        def act(e):
            for w, v in ready:
                e.wait_ge(w, v)
            for n in range(4):
                if n % 2:
                    e.wait_ge(multiplied, stream.number(G, n // 2))
                else:
                    e.wait_ge(part, n // 2 + 1)
                e.activation(th[:, n, :], pair(n), ACT.Tanh, scale=0.5, bias=half_bias[:, 16 + n:17 + n]).then_inc(th_done, 1)
            for n in range(4):
                e.wait_ge(multiplied, stream.number(G, 2 + n))
                if n >= 2:
                    e.wait_ge(yo_ready, n - 1)
                e.activation(tz[n % 2][:, :], pair(n), ACT.Tanh, scale=0.5).then_inc(tz_done, 1)
                e.wait_ge(full, n + 1)
                e.activation(yo_hi[:, n, :], tz[n % 2][:, :], ACT.Copy, scale=0.25).then_inc(hi_done, 1)

        def dve(e):
            o = dve_steps(e)
            for n in range(4):
                if n >= 2:
                    e.wait_ge(gated, n - 1)
                o(e.tensor_tensor(y[n % 2][:, :], f32(ys_hi[:, n, :]), f32(ys_lo[:, n, :]), ALU.add))
                e.wait_ge(th_done, n + 1)
                e.scalar_tensor_tensor(th[:, n, :], th[:, n, :], 1.0, y[n % 2][:, :], ALU.add, ALU.mult).then_inc(gated, 1)
            for n in range(4):
                e.wait_ge(tz_done, n + 1)
                o(e.scalar_tensor_tensor(tz[n % 2][:, :], tz[n % 2][:, :], 1.0, pair(n), ALU.add, ALU.mult))
                e.wait_ge(gated, n + 1)
                e.tensor_tensor(tz[n % 2][:, :], tz[n % 2][:, :], th[:, n, :], ALU.mult).then_inc(full, 1)
                e.wait_ge(hi_done, n + 1)
                e.scalar_tensor_tensor(yo_lo[:, n, :], tz[n % 2][:, :], 0.25, f32(yo_hi[:, n, :]), ALU.mult, ALU.subtract).then_inc(yo_ready, 1)

        return dict(sp=sp, pool=pool, pe=pe, act=act, dve=dve, yo=(yo_hi, yo_lo), ready=[(yo_ready, 4)])

    def s5_out(yo, ready):
        yo_hi, yo_lo = yo
        G0, G1, f_abs, f_min, i_row, sums, neg_max, neg_m, ones_rows = carve(
            ("s5_G0", [P, S], F32), ("s5_G1", [P, S], F32),
            *[(f"ml_{n}", [4, S], F32) for n in ("f_abs", "f_min", "i_row", "sums", "neg_max", "neg_m", "ones_rows")], keep=2 * 4 * S * 4)
        G = (G0, G1)
        part, g_read, parted, stored = (sem(f"s5_out_{n}") for n in ("part", "g_read", "parted", "stored"))
        f_ln, rows_ready, rows_stored, turned, cols_ready = (
            sem(f"ml_{n}") for n in ("f_ln", "rows_ready", "rows_stored", "turned", "cols_ready"))
        credits.extend([(parted, 2), (g_read, 2), (stored, 32)])
        M, O = "ml_pre", "s5_out"

        def sp(e):
            load_chunks(e, M)
            load_chunks(e, O)
            e.wait_ge(rows_ready, 1)
            e.dma_start(rows_dram[8:12, :], neg_max[:, :]).then_inc(rows_stored, 16)
            e.dma_start(rows_dram[12:16, :], neg_m[:, :]).then_inc(rows_stored, 16)

        def pool(e):
            split_chunks(e, M)
            split_chunks(e, O)

        def pe(e):
            for w, v in ready:
                e.wait_ge(w, v)
            for c in range(2):
                e.wait_ge(split, stream.number(M, c))
                columns(e, stream.slot(M, c), 2 + c, H_hi, H_lo).then_inc(multiplied, 1)
            with e.Fori(0, 4) as i:
                e.wait_ge(split, stream.number(O, 0, i))
                for t in range(2):
                    e.wait_ge(parted, 2 * i + t + 1)
                    columns(e, stream.slot(O, 0), t, yo_hi, yo_lo, kt=4, at=t * P, step=256).then_inc(multiplied if t else part, 1)
                for t in range(2):
                    e.wait_ge(split, stream.number(O, 1 + t, i))
                    e.wait_ge(rows_ready, 1)
                    e.wait_ge(g_read, 2 * i + t + 1)
                    columns(e, stream.slot(O, 1 + t), 2 + t, H_hi, H_lo).then_inc(multiplied, 1)
            e.wait_ge(parted, 10)
            for k in range(KT):
                ins = e.transpose(ps[:, 0, k * 4:(k + 1) * 4], i_row[:, k * P:(k + 1) * P], ident[0:4, 0:4])
            ins.then_inc(turned, 1)

        def act(e):
            a = steps_of(e, "act")
            bias = par[0:4, COLUMN["row_bias"] + 2:COLUMN["row_bias"] + 3]
            for w, v in ready:
                e.wait_ge(w, v)
            e.wait_ge(multiplied, stream.number(M, 1))
            a(e.activation(f_abs[:, :], pair(3)[0:4, :], ACT.Abs, bias=bias))
            a(e.activation(f_abs[:, :], f_abs[:, :], ACT.Exp, scale=-1.0))
            e.activation(f_abs[:, :], f_abs[:, :], ACT.Ln, bias=one_col[0:4, :]).then_inc(f_ln, 1)
            with e.Fori(0, 4) as i:
                for t in range(2):
                    e.wait_ge(multiplied, stream.number(O, 1 + t, i))
                    if t == 0:
                        e.wait_ge(stored, 32 * i + 32)
                    e.activation(G[t][:, :], pair(2 + t), ACT.Tanh, scale=0.5).then_inc(g_read, 1)
                for t in range(2):
                    e.wait_ge(parted, 2 * i + t + 3)
                    e.dma_start(part_dram[bass.ds(2 * i + t, 1), :, :].rearrange("o p n -> p (o n)"), G[t][:, :]).then_inc(stored, 16)
            e.wait_ge(turned, 1)
            e.activation(gate_cols[:, :, :].rearrange("p k h -> p (k h)"), ps[:, 0, 0:4 * KT], ACT.Copy).then_inc(cols_ready, 1)

        def dve(e):
            o = dve_steps(e)
            col_i, col_f = (par[0:4, COLUMN["row_bias"] + n:COLUMN["row_bias"] + n + 1] for n in (1, 2))
            for w, v in ready:
                e.wait_ge(w, v)
            e.wait_ge(multiplied, stream.number(M, 0))
            o(e.memset(ones_rows[:, :], 1.0))
            o(e.tensor_scalar(i_row[:, :], pair(2)[0:4, :], col_i, None, ALU.add))
            e.wait_ge(sem("act_order"), PRELUDE_ACT + 3)
            o(e.tensor_scalar(f_min[:, :], pair(3)[0:4, :], col_f, 0.0, ALU.add, ALU.min))
            e.wait_ge(f_ln, 1)
            o(e.tensor_tensor(f_min[:, :], f_min[:, :], f_abs[:, :], ALU.subtract))
            o(e.tensor_tensor_scan(sums[:, :], ones_rows[:, :], f_min[:, :], 0.0, ALU.mult, ALU.add))
            o(e.tensor_tensor(i_row[:, :], i_row[:, :], sums[:, :], ALU.subtract))
            o(e.tensor_tensor_scan(f_abs[:, :], ones_rows[:, :], i_row[:, :], FILL, ALU.mult, ALU.max))
            o(e.tensor_scalar(neg_max[:, :], f_abs[:, :], -1.0, None, ALU.mult))
            e.scalar_tensor_tensor(neg_m[:, :], sums[:, :], -1.0, f_abs[:, :], ALU.mult, ALU.subtract).then_inc(rows_ready, 1)
            with e.Fori(0, 4) as i:
                for t in range(2):
                    e.wait_ge(g_read, 2 * i + t + 3)
                    e.scalar_tensor_tensor(G[t][:, :], G[t][:, :], 1.0, pair(t), ALU.add, ALU.mult).then_inc(parted, 1)

        return dict(sp=sp, pool=pool, pe=pe, act=act, dve=dve, part_stored=(stored, 160), rows_stored=(rows_stored, 32),
                    cols_ready=(cols_ready, 1), tmp_free=[(cols_ready, 1), (rows_stored, 32), (stored, 160)])

    def mlstm(h_ready, tmp_free, rows_stored):
        two_tiles, X = 2 * S * 4, 3
        (xpad,) = carve(("ml_xpad", [P, 2, X + S], F32))
        u_at = two_tiles + 32
        u_hi, u_lo, c_hi, c_lo, v_hi, v_lo, acc, so, negm_b, st_hi, st_lo, capped = carve(
            ("ml_u_hi", [P, 2, S], F32R), ("ml_u_lo", [P, 2, S], F32R), ("ml_c_hi", [P, 2, S], F32R),
            ("ml_c_lo", [P, 2, S], F32R), ("ml_v_hi", [P, KT, 256], F32R), ("ml_v_lo", [P, KT, 256], F32R), ("ml_acc", [P, 2, S], F32),
            ("ml_so", [P, 2, S], F32), ("ml_negm_b", [P, S], F32), ("ml_st_hi", [P, 2, HALF], F32R), ("ml_st_lo", [P, 2, HALF], F32R),
            ("ml_capped", [P, P], F32), keep=u_at)
        E, st, em = carve(("ml_E", [P, HALF], F32), ("ml_st", [P, HALF], F32), ("ml_em", [P, S], F32))
        (tz,) = carve(("ml_tz", [P, 2, S], F32))
        q, k_ = carve(("ml_q", [P, 2, S], F32), ("ml_k", [P, 2, S], F32), keep=u_at)
        out_hi, out_lo = carve(("ml_out_hi", [P, 2, S], F32R), ("ml_out_lo", [P, 2, S], F32R), keep=u_at)
        sq, rstd, c_full = carve(("ml_sq", [P, 2, S], F32), ("ml_rstd", [P, S], F32), ("ml_c_full", [P, S], F32), keep=u_at + 4 * two_tiles)
        (tc,) = carve(("ml_tc", [P, 2, S], F32), keep=u_at + 8 * two_tiles + S * 4)
        names = ("x_read", "u_hi", "u_ready", "conv", "c_tanh", "c_full", "c_hi", "c_ready", "o_read", "v_part", "v_hi", "v_ready",
                 "qk_part", "qk_read", "neg_loaded", "em_loaded", "em_ready", "capped", "E_ready", "scored", "st_full", "st_hi", "st_ready", "num_done",
                 "h_read", "gated", "squared", "summed", "rooted", "tz", "f_full", "out_hi", "out_ready", "out_part", "y_added")
        s = {n: sem(f"mlstm_{n}") for n in names}
        credits.extend([(s["y_added"], KT), (s["st_full"], 1)])
        N = "ml"
        pieces = [(hf, k, max(0, k * P - hf * HALF)) for hf in range(2) for k in range(4 * hf + 4)]
        M = len(pieces)
        diagonal = [m for m, (hf, k, off) in enumerate(pieces) if k * P >= hf * HALF]
        num_bank, den_bank = (2, 5), (4, 7)

        def sp(e):
            load_chunks(e, N)

        def pool(e):
            split_chunks(e, N)

        def pe(e):
            for w, v in tmp_free:
                e.wait_ge(w, v)

            def scores(j, m):
                hf, k, off = pieces[m]
                if m == 0:
                    e.wait_ge(s["qk_read"], 4 * j + 4)
                elif m >= 2:
                    e.wait_ge(s["st_full"], M * j + m)
                for d in range(2):
                    ins = e.matmul(ps[:, m % 2, 0:HALF - off], k_[:, d, k * P:(k + 1) * P], q[:, d, hf * HALF + off:(hf + 1) * HALF],
                                   start=d == 0, stop=d == 1)
                ins.then_inc(s["scored"], 1)

            def values(j, m):
                hf, k, off = pieces[m]
                first, last = k == 0, k == 4 * hf + 3
                e.wait_ge(s["st_ready"], M * j + m + 1)
                hi, lo = st_hi[:, m % 2, 0:HALF - off], st_lo[:, m % 2, 0:HALF - off]
                for d in range(2):
                    product(e, ps[:, num_bank[hf] + d, off:], v_hi[:, k, d * P:(d + 1) * P], v_lo[:, k, d * P:(d + 1) * P], hi, lo, first, last)
                e.matmul(ps[:, den_bank[hf], off:], ones_r[:, :], hi, start=first, stop=False)
                e.matmul(ps[:, den_bank[hf], off:], ones_r[:, :], lo, start=False, stop=last).then_inc(s["num_done"], 1)

            with e.Fori(0, MLSTM_HEADS) as j:
                for c in range(4):
                    e.wait_ge(split, stream.number(N, c, j))
                    e.wait_ge(s["y_added"], 8 * j + 5 + c)
                    columns(e, stream.slot(N, c), c, H_hi, H_lo).then_inc(multiplied, 1)
                sl = stream.slot(N, 4)
                e.wait_ge(split, stream.number(N, 4, j))
                e.wait_ge(s["u_ready"], 2 * j + 2)
                for m in range(KT):
                    for t in range(2):
                        ins = product(e, ps[:, m // 2, (m % 2) * 256:(m % 2 + 1) * 256], u_hi[:, t, m * P:(m + 1) * P], u_lo[:, t, m * P:(m + 1) * P],
                                      w_hi[sl][:, t * 256:(t + 1) * 256], w_lo[sl][:, t * 256:(t + 1) * 256], t == 0, t == 1)
                    if m == 3:
                        ins.then_inc(s["v_part"], 1)
                ins.then_inc(multiplied, 1)
                sl = stream.slot(N, 5)
                e.wait_ge(split, stream.number(N, 5, j))
                e.wait_ge(s["c_ready"], 2 * j + 2)
                for n in range(4):
                    if n < 2:
                        e.wait_ge(s["o_read"], 2 * j + n + 1)
                    else:
                        e.wait_ge(s["v_ready"], 2 * j + n - 1)
                    columns(e, sl, (2, 3, 0, 1)[n], c_hi, c_lo, kt=2, at=HALF * (n // 2) + (n % 2) * P, step=256).then_inc(multiplied if n == 3 else s["qk_part"], 1)
                scores(j, 0)
                scores(j, 1)
                for m in range(M):
                    values(j, m)
                    if m + 2 < M:
                        scores(j, m + 2)
                for t in range(2):
                    e.wait_ge(split, stream.number(N, 6 + t, j))
                    if t == 0:
                        e.wait_ge(s["st_full"], M * j + M + 1)
                    else:
                        e.wait_ge(s["h_read"], 4 * j + 2)
                    columns(e, stream.slot(N, 6 + t), t, H_hi, H_lo).then_inc(multiplied, 1)
                    if t == 0:
                        e.wait_ge(s["squared"], 2 * j + 2)
                        for d in range(2):
                            for h in range(2):
                                ins = e.matmul(ps[:, 4 + h, :], ones[:, :], sq[:, d, h * HALF:(h + 1) * HALF], start=d == 0, stop=d == 1)
                        ins.then_inc(s["summed"], 1)
                for c in range(2):
                    sl = stream.slot(N, 8 + c)
                    e.wait_ge(split, stream.number(N, 8 + c, j))
                    e.wait_ge(s["out_ready"], 2 * j + 2)
                    for n in range(4):
                        if c == 1:
                            e.wait_ge(s["y_added"], 8 * j + n + 1 + KT)
                        columns(e, sl, n, out_hi, out_lo, kt=2, at=n * P, step=HALF).then_inc(multiplied if n == 3 else s["out_part"], 1)

        def act(e):
            for w, v in tmp_free + [rows_stored]:
                e.wait_ge(w, v)
            with e.Fori(0, MLSTM_HEADS) as j:
                e.wait_ge(s["y_added"], 8 * j + 8)
                e.dma_start(negm_b[:, :], rows_dram[bass.ds(8 + j, 1), :].broadcast_to([P, S])).then_inc(s["neg_loaded"], 16)
                for t in range(2):
                    e.wait_ge(multiplied, stream.number(N, t, j))
                    e.activation(xpad[:, t, X:], pair(t), ACT.Copy).then_inc(s["x_read"], 1)
                    e.activation(u_hi[:, t, :], pair(t), ACT.Copy).then_inc(s["u_hi"], 1)
                for t in range(2):
                    e.wait_ge(s["conv"], 2 * j + t + 1)
                    e.activation(tc[:, t, :], acc[:, t, :], ACT.Tanh, scale=0.5).then_inc(s["c_tanh"], 1)
                for t in range(2):
                    e.wait_ge(s["c_full"], 2 * j + t + 1)
                    e.activation(c_hi[:, t, :], acc[:, t, :], ACT.Copy, scale=0.5).then_inc(s["c_hi"], 1)
                e.wait_ge(s["u_ready"], 2 * j + 2)
                e.dma_start(em[:, :], rows_dram[bass.ds(12 + j, 1), :].broadcast_to([P, S])).then_inc(s["em_loaded"], 16)
                for t in range(2):
                    e.wait_ge(multiplied, stream.number(N, 2 + t, j))
                    e.activation(so[:, t, :], pair(2 + t), ACT.Tanh, scale=0.5).then_inc(s["o_read"], 1)
                e.wait_ge(s["em_loaded"], 16 * j + 16)
                e.activation(em[:, :], em[:, :], ACT.Exp).then_inc(s["em_ready"], 1)
                for t in range(2):
                    e.wait_ge(*((s["v_part"], j + 1) if t == 0 else (multiplied, stream.number(N, 4, j))))
                    e.activation(v_hi[:, 4 * t:4 * t + 4, :].rearrange("p k n -> p (k n)"), pair(t), ACT.Copy).then_inc(s["v_hi"], 1)
                for n in range(4):
                    e.wait_ge(*((multiplied, stream.number(N, 5, j)) if n == 3 else (s["qk_part"], 3 * j + n + 1)))
                    if n < 2:
                        e.activation(q[:, n, :], pair(2 + n), ACT.Copy, scale=256 ** -0.5).then_inc(s["qk_read"], 1)
                    else:
                        e.activation(k_[:, n - 2, :], pair(n - 2), ACT.Copy).then_inc(s["qk_read"], 1)
                e.wait_ge(s["neg_loaded"], 16 * j + 16)

                def weights(m):
                    hf, k, off = pieces[m]
                    t0, g = hf * HALF + off, gate_cols[:, k, bass.ds(j, 1)]
                    at = P if m in diagonal else 0
                    if at:
                        e.wait_ge(s["capped"], 8 * j + k + 1)
                        ins = e.activation(E[:, 0:P], capped[:, :], ACT.Exp)
                    if at < HALF - off:
                        ins = e.activation(E[:, at:HALF - off], negm_b[:, t0 + at:(hf + 1) * HALF], ACT.Exp, bias=g)
                    ins.then_inc(s["E_ready"], 1)

                e.wait_ge(s["st_full"], M * j + 1)
                weights(0)
                for m in range(M):
                    width = HALF - pieces[m][2]
                    e.wait_ge(s["st_full"], M * j + m + 2)
                    if m >= 2:
                        e.wait_ge(s["num_done"], M * j + m - 1)
                    e.activation(st_hi[:, m % 2, 0:width], st[:, 0:width], ACT.Copy).then_inc(s["st_hi"], 1)
                    if m + 1 < M:
                        weights(m + 1)
                e.wait_ge(s["gated"], 4 * j + 4)
                for t in range(2):
                    e.activation(sq[:, t, :], acc[:, t, :], ACT.Square).then_inc(s["squared"], 1)
                e.wait_ge(multiplied, stream.number(N, 6, j))
                e.activation(tz[:, 0, :], pair(0), ACT.Tanh, scale=0.5).then_inc(s["tz"], 1)
                e.wait_ge(s["summed"], j + 1)
                e.activation(rstd[:, :], pair(2), ACT.Sqrt, scale=1.0 / 256, bias=eps_col[:, :]).then_inc(s["rooted"], 1)
                e.wait_ge(multiplied, stream.number(N, 7, j))
                e.activation(tz[:, 1, :], pair(1), ACT.Tanh, scale=0.5).then_inc(s["tz"], 1)
                for t in range(2):
                    e.wait_ge(s["f_full"], 2 * j + t + 1)
                    e.activation(out_hi[:, t, :], acc[:, t, :], ACT.Copy, scale=0.5).then_inc(s["out_hi"], 1)

        def dve(e):
            o = dve_steps(e)
            for w, v in tmp_free:
                e.wait_ge(w, v)
            o(e.memset(Y[:, :, :], 0.0))
            with e.Fori(0, MLSTM_HEADS) as j:
                o.enter(j, 24)
                o(e.memset(xpad[:, :, 0:X], 0.0))
                for t in range(2):
                    n = 2 * j + t
                    e.wait_ge(s["x_read"], n + 1)
                    o(e.tensor_scalar(acc[:, t, :], xpad[:, t, X:], col("ml_conv3", n), col("ml_conv_b", n), ALU.mult, ALU.add))
                    for back in (1, 2, 3):
                        ins = e.scalar_tensor_tensor(acc[:, t, :], xpad[:, t, X - back:X - back + S], col(f"ml_conv{3 - back}", n), acc[:, t, :], ALU.mult, ALU.add)
                        if back < 3:
                            o(ins)
                    ins.then_inc(s["conv"], 1)
                    e.wait_ge(s["u_hi"], n + 1)
                    e.tensor_tensor(u_lo[:, t, :], xpad[:, t, X:], f32(u_hi[:, t, :]), ALU.subtract).then_inc(s["u_ready"], 1)
                for t in range(2):
                    n = 2 * j + t
                    e.wait_ge(s["c_tanh"], n + 1)
                    e.scalar_tensor_tensor(acc[:, t, :], tc[:, t, :], 1.0, acc[:, t, :], ALU.add, ALU.mult).then_inc(s["c_full"], 1)
                    e.wait_ge(s["c_hi"], n + 1)
                    e.scalar_tensor_tensor(c_lo[:, t, :], acc[:, t, :], 0.5, f32(c_hi[:, t, :]), ALU.mult, ALU.subtract).then_inc(s["c_ready"], 1)
                for t in range(2):
                    e.wait_ge(s["o_read"], 2 * j + t + 1)
                    o(e.tensor_scalar(so[:, t, :], so[:, t, :], 1.0, 0.5, ALU.add, ALU.mult))
                for t in range(2):
                    e.wait_ge(s["v_hi"], 2 * j + t + 1)
                    half = slice(4 * t, 4 * t + 4)
                    e.tensor_tensor(v_lo[:, half, :].rearrange("p k n -> p (k n)"), pair(t), f32(v_hi[:, half, :].rearrange("p k n -> p (k n)")),
                                    ALU.subtract).then_inc(s["v_ready"], 1)

                def cap_weights(m):
                    hf, k, off = pieces[m]
                    if k:
                        e.wait_ge(s["E_ready"], M * j + diagonal[k - 1] + 1)
                    t0 = hf * HALF + off
                    e.scalar_tensor_tensor(capped[:, :], negm_b[:, t0:t0 + P], gate_cols[:, k, bass.ds(j, 1)], cap[:, :],
                                           ALU.add, ALU.min).then_inc(s["capped"], 1)

                def divide(hf):
                    half = slice(hf * HALF, (hf + 1) * HALF)
                    e.wait_ge(s["num_done"], M * j + (M if hf else 4))
                    if hf == 0:
                        e.wait_ge(s["em_ready"], j + 1)
                    o(e.tensor_tensor(em[:, half], ps[:, den_bank[hf], :], em[:, half], ALU.max))
                    o(e.scalar_tensor_tensor(em[:, half], ps[:, den_bank[hf], :], -1.0, em[:, half], ALU.mult, ALU.max))
                    o(e.reciprocal(em[:, half], em[:, half]))
                    for d in range(2):
                        e.tensor_tensor(acc[:, d, half], ps[:, num_bank[hf] + d, :], em[:, half], ALU.mult).then_inc(s["h_read"], 1)
                    for d in range(2):
                        e.wait_ge(s["h_read"], 4 * j + 2 * hf + d + 1)
                        e.tensor_tensor(acc[:, d, half], acc[:, d, half], so[:, d, half], ALU.mult).then_inc(s["gated"], 1)

                e.wait_ge(s["neg_loaded"], 16 * j + 16)
                cap_weights(0)
                for m in range(M):
                    width = HALF - pieces[m][2]
                    e.wait_ge(s["E_ready"], M * j + m + 1)
                    e.wait_ge(s["scored"], M * j + m + 1)
                    e.tensor_tensor(st[:, 0:width], ps[:, m % 2, 0:width], E[:, 0:width], ALU.mult).then_inc(s["st_full"], 1)
                    if m + 1 in diagonal:
                        cap_weights(m + 1)
                    e.wait_ge(s["st_hi"], M * j + m + 1)
                    e.tensor_tensor(st_lo[:, m % 2, 0:width], st[:, 0:width], f32(st_hi[:, m % 2, 0:width]), ALU.subtract).then_inc(s["st_ready"], 1)
                    e.wait_ge(s["st_ready"], M * j + m + 1)
                    if m == 6:
                        divide(0)
                divide(1)
                e.wait_ge(s["rooted"], j + 1)
                o(e.reciprocal(rstd[:, :], rstd[:, :]))
                for t in range(2):
                    n = 2 * j + t
                    o(e.tensor_tensor(c_full[:, :], f32(c_hi[:, t, :]), f32(c_lo[:, t, :]), ALU.add))
                    o(e.scalar_tensor_tensor(acc[:, t, :], acc[:, t, :], col("head_g", n), rstd[:, :], ALU.mult, ALU.mult))
                    o(e.scalar_tensor_tensor(acc[:, t, :], c_full[:, :], col("skip", n), acc[:, t, :], ALU.mult, ALU.add))
                    e.wait_ge(s["tz"], n + 1)
                    o(e.scalar_tensor_tensor(tz[:, t, :], tz[:, t, :], 1.0, pair(t), ALU.add, ALU.mult))
                    e.tensor_tensor(acc[:, t, :], acc[:, t, :], tz[:, t, :], ALU.mult).then_inc(s["f_full"], 1)
                    e.wait_ge(s["out_hi"], n + 1)
                    e.scalar_tensor_tensor(out_lo[:, t, :], acc[:, t, :], 0.5, f32(out_hi[:, t, :]), ALU.mult, ALU.subtract).then_inc(s["out_ready"], 1)
                for n in range(KT):
                    if n % 4 == 3:
                        e.wait_ge(multiplied, stream.number(N, 8 + n // 4, j))
                    else:
                        e.wait_ge(s["out_part"], 6 * j + 3 * (n // 4) + n % 4 + 1)
                    e.tensor_tensor(Y[:, n, :], Y[:, n, :], pair(n % 4), ALU.add).then_inc(s["y_added"], 1)
                e.wait_ge(s["y_added"], 8 * j + 2 * KT)
            o.leave(MLSTM_HEADS)

        done = [(s["y_added"], KT * (MLSTM_HEADS + 1))]
        return dict(sp=sp, pool=pool, pe=pe, act=act, dve=dve, y_ready=done, tmp_free=done)

    def merge(ready, part_stored):
        m_hi, m_lo, tg0, tg1, part0, part1 = carve(("m_hi", [P, KT, S], F32R), ("m_lo", [P, KT, S], F32R), *[(f"merge_{n}", [P, S], F32) for n in ("tg0", "tg1", "part0", "part1")])
        tg, part = (tg0, tg1), (part0, part1)
        part_loaded, g_read, full, hi_done, m_ready, out_ready = (
            sem(f"merge_{n}") for n in ("part_loaded", "g_read", "full", "hi", "m_ready", "out_ready"))
        credits.extend([(g_read, 4), (m_ready, 2), (full, 2), (out_ready, 4)])
        G, O = "merge", "final_out"

        def sp(e):
            load_chunks(e, G)
            load_chunks(e, O)

        def pool(e):
            split_chunks(e, G)
            split_chunks(e, O)

        def pe(e):
            for w, v in ready:
                e.wait_ge(w, v)
            with e.Fori(0, 2) as i:
                for c in range(4):
                    e.wait_ge(split, stream.number(G, c, i))
                    e.wait_ge(g_read, 4 * i + c + 1)
                    columns(e, stream.slot(G, c), c, H_hi, H_lo).then_inc(multiplied, 1)
            e.wait_ge(g_read, 12)
            with e.Fori(0, 2) as i:
                for c in range(4):
                    e.wait_ge(split, stream.number(O, c, i))
                    e.wait_ge(m_ready, KT + 2)
                    e.wait_ge(out_ready, 4 * i + c + 1)
                    columns(e, stream.slot(O, c), c, m_hi, m_lo).then_inc(multiplied, 1)

        def act(e):
            for w, v in ready + [part_stored]:
                e.wait_ge(w, v)
            with e.Fori(0, 2) as i:
                for c in range(4):
                    n = 4 * i + c
                    e.wait_ge(full, n + 1)
                    e.dma_start(part[c % 2][:, :], part_dram[bass.ds(n, 1), :, :].rearrange("o p n -> p (o n)")).then_inc(part_loaded, 16)
                    e.wait_ge(multiplied, stream.number(G, c, i))
                    e.wait_ge(m_ready, n + 1)
                    e.activation(tg[c % 2][:, :], pair(c), ACT.Tanh, scale=0.5).then_inc(g_read, 1)
                    e.wait_ge(full, n + 3)
                    e.activation(tile(m_hi, n), tg[c % 2][:, :], ACT.Copy, scale=0.5).then_inc(hi_done, 1)
            with e.Fori(0, 2) as i:
                for c in range(4):
                    e.wait_ge(multiplied, stream.number(O, c, i))
                    e.wait_ge(m_ready, KT + 2)
                    e.activation(tile(Y, 4 * i + c), pair(c), ACT.Copy).then_inc(out_ready, 1)

        def dve(e):
            o = dve_steps(e)
            for w, v in ready:
                e.wait_ge(w, v)
            with e.Fori(0, 2) as i:
                o.enter(i, 4)
                for c in range(4):
                    n = 4 * i + c
                    b = c % 2
                    e.wait_ge(g_read, n + 5)
                    o(e.scalar_tensor_tensor(tg[b][:, :], tg[b][:, :], 1.0, tile(Y, n), ALU.add, ALU.mult))
                    e.wait_ge(part_loaded, 16 * n + 16)
                    e.tensor_tensor(tg[b][:, :], tg[b][:, :], part[b][:, :], ALU.add).then_inc(full, 1)
                    e.wait_ge(hi_done, n + 1)
                    e.scalar_tensor_tensor(tile(m_lo, n), tg[b][:, :], 0.5, f32(tile(m_hi, n)), ALU.mult, ALU.subtract).then_inc(m_ready, 1)
                e.wait_ge(m_ready, 4 * i + 6)
            o.leave(2)

        done = [(out_ready, KT + 4)]
        return dict(sp=sp, pool=pool, pe=pe, act=act, dve=dve, y_ready=done, tmp_free=done)


    def constants(e):
        o = steps_of(e, "pool")
        o.step(e.memset(ident[:, :], 0.0))
        o.step(e.memset(causal_b[:, :], 0.0))
        o.step(e.memset(cap[:, :], 0.0))
        o.step(e.memset(eps_col[:, :], EPS))
        o.step(e.memset(one_col[:, :], 1.0))
        o.step(e.memset(ones[:, :], 1.0))
        o.after(o.n)
        o(e.affine_select(out=ident[:, :], in_=ident[:, :], compare_op=ALU.not_equal, fill=1.0, base=0, pattern=[[-1, P]], channel_multiplier=1))
        o(e.affine_select(out=causal_b[:, :], in_=causal_b[:, :], compare_op=ALU.is_ge, fill=FILL, base=0, pattern=[[-1, P]], channel_multiplier=1))
        o(e.affine_select(out=cap[:, :], in_=cap[:, :], compare_op=ALU.is_ge, fill=FILL, base=0, pattern=[[1, P]], channel_multiplier=-1))
        o(e.tensor_copy(ones_r[:, :], ones[:, :]))
        e.tensor_copy(ident_b[:, :], ident[:, :]).then_inc(consts, 1)

    steps = []
    steps = []
    pl = prelude()
    b0 = boundary("b0", None, "mix_pre0", A["x_t"], [], pl["tmp_free"])
    fx = fox(b0["h_ready"], b0["tmp_free"])
    b1 = boundary("b1", "mix_post0", "ffn_pre0", A["x_t"], fx["y_ready"], fx["tmp_free"])
    f0 = ffn(0, b1["h_ready"], b1["tmp_free"])
    b2 = boundary("b2", "ffn_post0", "mix_pre1", x_dram, f0["y_ready"], f0["tmp_free"])
    lr = lru(b2["h_ready"], b2["tmp_free"])
    b3 = boundary("b3", "mix_post1", "ffn_pre1", x_dram, lr["y_ready"], lr["tmp_free"])
    f1 = ffn(1, b3["h_ready"], b3["tmp_free"])
    b4 = boundary("b4", "ffn_post1", "norm_pre", x_dram, f1["y_ready"], f1["tmp_free"])
    s5_ = s5(b4["h_ready"], b4["tmp_free"])
    gl = glu(s5_["ys"], s5_["ready"])
    so = s5_out(gl["yo"], gl["ready"])
    ml = mlstm(b4["h_ready"], so["tmp_free"], so["rows_stored"])
    mg = merge(ml["y_ready"], so["part_stored"])
    b5 = boundary("b5", "norm_post", None, x_dram, mg["y_ready"], mg["tmp_free"])
    steps += [pl, b0, fx, b1, f0, b2, lr, b3, f1, b4, s5_, gl, so, ml, mg, b5]

    def run(engine, which):
        for step in steps:
            if which in step:
                step[which](engine)

    with nc.Block() as block:
        @block.sync
        def _(e):
            for s, n in credits:
                e.sem_inc(s, n)
            e.dma_start(par[:, :], A["params"]).then_inc(params_loaded, 16)
            run(e, "sp")

        @block.gpsimd
        def _(e):
            constants(e)
            run(e, "pool")

        @block.tensor
        def _(e):
            e.wait_ge(consts, 1)
            run(e, "pe")

        @block.scalar
        def _(e):
            e.wait_ge(consts, 1)
            e.wait_ge(params_loaded, 16)
            run(e, "act")

        @block.vector
        def _(e):
            e.wait_ge(consts, 1)
            e.wait_ge(params_loaded, 16)
            run(e, "dve")


def kernel(**inputs):
    import concourse.bacc as bacc
    from concourse.bass_utils import run_bass_kernel_spmd

    v = {k: np.asarray(a) for k, a in inputs.items()}

    def columns_of(a):
        return np.ascontiguousarray(a.reshape(-1, P).T)

    packed = {"od_conv_b": v["od_conv_b"], "od_b_a": v["od_b_a"], "od_b_x": v["od_b_x"], "od_lam": v["od_lam"],
              "norm_pre": v["norm_pre_g_2"], "ml_conv_b": v["conv_b_2"], "head_g": v["head_g_2"], "skip": v["skip_a_2"],
              "norm_post": v["norm_post_g_2"], "pool_scale": v["ev_pool_scale"], "d_skip": v["D_skip_2"], "b_glu": v["b_glu_2"],
              "lam_re": v["lam_re_2"], "lam_im": v["lam_im_2"], "log_dt": np.repeat(v["log_dt_2"].reshape(-1, 1), 64, axis=1)}
    for l in range(2):
        packed |= {f"mix_pre{l}": v["mix_pre_g"][l], f"mix_post{l}": v["mix_post_g"][l],
                   f"ffn_pre{l}": v["ffn_pre_g"][l], f"ffn_post{l}": v["ffn_post_g"][l]}
    for t in range(4):
        packed |= {f"od_conv{t}": v["od_conv_w"][0, t], f"ml_conv{t}": v["conv_w_2"][0, t]}
    params = np.zeros((P, n_columns), np.float32)
    for name, n in VECTORS:
        if name in packed:
            params[:, COLUMN[name]:COLUMN[name] + n] = columns_of(packed[name])
    params[0:8, COLUMN["row_bias"]] = v["ev_b_f"][0]
    params[0:4, COLUMN["row_bias"] + 1] = v["b_i_2"][0]
    params[0:4, COLUMN["row_bias"] + 2] = v["b_f_2"][0]
    for g, w in enumerate(POOL_WINDOWS):
        at = COLUMN["inv_count"] + PAD * g
        params[:, at:at + PAD] = [1.0 / min(t + 1, w) for t in range(PAD)]
    s5_b = np.zeros((S5_TILES, P, 2, 4, P), np.float32)
    s5_c = np.zeros((S5_TILES, P, 2, 4, P), np.float32)
    for g in range(32):
        t, local, st, at = g // 8, g % 8, (g % 8) // 2, 64 * (g % 2)
        for part, (b, c) in enumerate(((v["B_re_2"], v["C_re_2"]), (v["B_im_2"], v["C_im_2"]))):
            s5_b[t, 16 * local:16 * local + 16, part, st, at:at + 64] = b[0, g].T
            s5_c[t, at:at + 64, part, st, 16 * local:16 * local + 16] = c[0, g].T
    arrays = {
        "x_t": np.ascontiguousarray(v["x"][0].T).reshape(KT, P, S), "params": params,
        "s5_b": s5_b.reshape(S5_TILES * P, 1024), "s5_c": s5_c.reshape(S5_TILES * P, 1024),
        "ev_w_in": v["ev_w_in"][0], "ev_pool_w": v["ev_pool_w"].reshape(512, P), "ev_w_out": v["ev_w_out"][0],
        "ffn_w_gate": v["ffn_w_gate"], "ffn_w_up": v["ffn_w_up"], "ffn_w_down": v["ffn_w_down"],
        "od_w_in": v["od_w_in"][0], "od_w_a": v["od_w_a"].reshape(D, 256), "od_w_x": v["od_w_x"].reshape(D, 256), "od_w_out": v["od_w_out"][0],
        "w_in_2": v["w_in_2"][0], "w_q_2": v["w_q_2"].reshape(D, 256), "w_k_2": v["w_k_2"].reshape(D, 256), "w_v_2": v["w_v_2"].reshape(D, 256),
        "w_a_out_2": v["w_a_out_2"][0], "w_glu_2": v["w_glu_2"][0], "w_b_out_2": v["w_b_out_2"][0], "w_o_2": v["w_o_2"][0],
    }
    nc = bacc.Bacc("TRN2", target_bir_lowering=False, num_devices=1, dynamic_dma_scratch_size=1024)
    maps, handles = {}, {}
    for name, a in arrays.items():
        maps[f"in_{name}"] = np.ascontiguousarray(a)
        handles[name] = nc.dram_tensor(f"in_{name}", a.shape, F32, kind="ExternalInput").ap()
    out = nc.dram_tensor("out", (KT, P, S), F32, kind="ExternalOutput").ap()
    block_program(nc, handles, out)
    r = run_bass_kernel_spmd(nc, [maps], core_ids=[0])
    return np.ascontiguousarray(np.asarray(r.results[0]["out"]).reshape(D, S).T).reshape(1, S, D)
```

```python
import concourse.bass as bass
from concourse import mybir
import numpy as np

F32 = mybir.dt.float32
F32R = mybir.dt.float32r
BF16 = mybir.dt.bfloat16
ACT = mybir.ActivationFunctionType
ALU = mybir.AluOpType

P = 128
S = 1024
D = 1024
HALF = 512
KT = D // P
D_FF = 2816
FF_BLOCKS = D_FF // (2 * P)
FOX_WIDTH = 512
FOX_PAIRS = 4
LRU_HEADS = 4
MLSTM_HEADS = 4
POOL_WINDOWS = (2, 4, 8, 16)
PAD = 16
S5_TILES = 4
STATE_TILES = 16
POWERS = 10
LC = 8
NC = S // LC
PRELUDE_ACT = 2
CONSTANT_STEPS = 14
EPS = 1e-6
FILL = -3.0e38
GELU_C = 0.7978845608028654
GELU_A = 0.044715
SLOTS = 3

VECTORS = [("mix_pre0", 8), ("mix_pre1", 8), ("mix_post0", 8), ("mix_post1", 8),
           ("ffn_pre0", 8), ("ffn_pre1", 8), ("ffn_post0", 8), ("ffn_post1", 8),
           ("od_conv0", 8), ("od_conv1", 8), ("od_conv2", 8), ("od_conv3", 8), ("od_conv_b", 8),
           ("od_b_a", 8), ("od_b_x", 8), ("od_lam", 8), ("norm_pre", 8),
           ("ml_conv0", 8), ("ml_conv1", 8), ("ml_conv2", 8), ("ml_conv3", 8), ("ml_conv_b", 8),
           ("head_g", 8), ("skip", 8), ("norm_post", 8),
           ("pool_scale", 4), ("d_skip", 4), ("b_glu", 4),
           ("lam_re", 16), ("lam_im", 16), ("log_dt", 16), ("row_bias", 3), ("inv_count", 64)]
COLUMN, n_columns = {}, 0
for _name, _n in VECTORS:
    COLUMN[_name] = n_columns
    n_columns += _n


def column_chunk(w, c0, step=0):
    return [(w, 8, 128, 0, 0, c0, step, 0)]


def block_chunk(w, kt, n, r0, rstep, c0, cstep=0, at=0):
    return [(w, kt, n, r0, rstep, c0, cstep, at)]


def phases_of_the_stream(A):
    ev, od, w2 = A["ev_w_in"], A["od_w_in"], A["w_in_2"]

    def gate_up(l, b0, step):
        return [column_chunk(A["ffn_w_gate"][l], b0, step), column_chunk(A["ffn_w_up"][l], b0, step),
                column_chunk(A["ffn_w_gate"][l], b0 + P, step), column_chunk(A["ffn_w_up"][l], b0 + P, step)]

    def down(l, r0, step):
        return [block_chunk(A["ffn_w_down"][l], 2, HALF, r0, step, c) for c in (0, HALF)]

    def ffn(l):
        return [(f"ffn{l}_first", 1, gate_up(l, 0, 0)),
                (f"ffn{l}", (FF_BLOCKS - 1) // 2, gate_up(l, 256, 512) + down(l, 0, 512) + gate_up(l, 512, 512) + down(l, 256, 512)),
                (f"ffn{l}_last", 1, down(l, D_FF - 256, 0))]

    def lru_in(c0, step):
        return [column_chunk(od, D + c0, step), column_chunk(od, D + c0 + P, step),
                column_chunk(od, c0, step), column_chunk(od, c0 + P, step)]

    def lru_gates(r0, step):
        return [block_chunk(A["od_w_a"], 2, 256, r0, step, 0) + block_chunk(A["od_w_x"], 2, 256, r0, step, 0, 0, 512)]

    def lru_out(r0, step):
        return [block_chunk(A["od_w_out"], 2, HALF, r0, step, c) for c in (0, HALF)]

    def mlstm(step):
        return ([column_chunk(w2, 0, step), column_chunk(w2, P, step),
                 column_chunk(w2, 2048, step), column_chunk(w2, 2048 + P, step),
                 block_chunk(A["w_v_2"], 2, 256, 0, step, 0),
                 block_chunk(A["w_q_2"], 2, 256, 0, step, 0) + block_chunk(A["w_k_2"], 2, 256, 0, step, 0, 0, 512),
                 column_chunk(w2, 1024, step), column_chunk(w2, 1024 + P, step)]
                + [block_chunk(A["w_a_out_2"], 2, HALF, 0, step, c) for c in (0, HALF)])

    listed = ([("fox_pre", 1, [column_chunk(ev, 1536)] + [column_chunk(ev, 1544 + g * P) for g in range(4)]
                + [block_chunk(A["ev_pool_w"], 4, P, 0, 0, 0)]),
               ("fox", FOX_PAIRS, [column_chunk(ev, c, P) for c in (0, 512, 1024)]),
               ("fox_out", 2, [column_chunk(A["ev_w_out"], c * P, 512) for c in range(4)])]
              + ffn(0)
              + [("lru_first", 1, lru_in(0, 0) + lru_gates(0, 0)),
                 ("lru", LRU_HEADS - 1, lru_in(256, 256) + lru_out(0, 256) + lru_gates(256, 256)),
                 ("lru_last", 1, lru_out(768, 0))]
              + ffn(1)
              + [("s5_u", 1, [column_chunk(w2, 3080 + c * P) for c in range(S5_TILES)]),
                 ("glu", 1, [column_chunk(w2, 3592 + c * P) for c in range(4)]
                  + [block_chunk(A["w_glu_2"], 4, 256, 0, 0, c) for c in (0, 256)]),
                 ("ml_pre", 1, [column_chunk(w2, 3072), column_chunk(w2, 3076)]),
                 ("s5_out", 4, [block_chunk(A["w_b_out_2"], 4, 256, 0, 0, 0, 256),
                                column_chunk(w2, 4104 + D, 256), column_chunk(w2, 4104 + D + P, 256)]),
                 ("ml", MLSTM_HEADS, mlstm(256)),
                 ("merge", 2, [column_chunk(w2, 4104 + c * P, 512) for c in range(4)]),
                 ("final_out", 2, [column_chunk(A["w_o_2"], c * P, 512) for c in range(4)])])
    slots, out = {3: (0, 1, 2), 2: (0, 1), 4: (0, 1, 2, 1), 5: (0, 1, 2, 0, 1), 6: (0, 1, 2) * 2,
                  7: (0, 1, 2, 0, 1, 2, 1), 10: (0, 1, 2) * 3 + (1,), 12: (0, 1, 2) * 4}, []
    for name, count, body in listed:
        out.append((name, count, body, slots[len(body)]))
    return out


class Stream:

    def __init__(self, listed):
        self.of, self.body, self.count, uses, last, n = {}, {}, {}, [0] * SLOTS, [None] * SLOTS, 0
        for name, count, body, slots in listed:
            m = len(body)
            distance = [10 ** 6] * m
            first, start = n, list(uses)
            for i in range(count):
                for j, s in enumerate(slots):
                    if last[s] is not None:
                        distance[j] = min(distance[j], n - last[s])
                    last[s] = n
                    uses[s] += 1
                    n += 1
            per = [slots.count(s) for s in range(SLOTS)]
            rank = [slots[:j].count(s) for j, s in enumerate(slots)]
            self.of[name] = (first, m, slots, distance, start, per, rank)
            self.body[name], self.count[name] = body, count

    def slot(self, name, j):
        return self.of[name][2][j]

    def number(self, name, j, i=0):
        first, m = self.of[name][:2]
        return first + j + 1 + i * m

    def before(self, name, j, i=0):
        d = self.of[name][3][j]
        return None if d == 10 ** 6 else self.number(name, j, i) - d

    def loads(self, name, j, i=0):
        first, m, slots, _, start, per, rank = self.of[name]
        s = slots[j]
        return start[s] + rank[j] + 1 + i * per[s]


class Order:

    def __init__(self, engine, sem):
        self.engine, self.sem, self.n, self.i, self.per = engine, sem, 0, 0, 0

    def step(self, ins):
        ins.then_inc(self.sem, 1)
        self.n += 1
        return self.n

    def after(self, n):
        self.engine.wait_ge(self.sem, n + self.i * self.per if self.per else n)

    def __call__(self, ins):
        self.after(self.step(ins))

    def enter(self, i, per):
        self.i, self.per, self.entered = i, per, self.n

    def leave(self, count):
        assert self.n - self.entered == self.per, (self.n - self.entered, self.per)
        self.n, self.per = self.entered + count * self.per, 0


def block_program(nc, A, out_x):
    listed = phases_of_the_stream(A)
    stream = Stream(listed)

    place = [-(-nc.sbuf_base // 32) * 32]

    def fixed(name, shape, dt=F32):
        size = int(np.prod(shape[1:])) * (2 if dt == BF16 else 4)
        t = nc.alloc_sbuf_tensor_at(name, shape, dt, offset=place[0])
        place[0] += -(-size // 32) * 32
        return t

    H_hi, H_lo = fixed("H_hi", [P, KT, S], F32R), fixed("H_lo", [P, KT, S], F32R)
    y_at = place[0]
    Y = fixed("Y", [P, KT, S])
    raw = [fixed(f"raw{s}", [P, 1024]) for s in range(SLOTS)]
    w_hi = [fixed(f"w_hi{s}", [P, 1024], F32R) for s in range(SLOTS)]
    w_lo = [fixed(f"w_lo{s}", [P, 1024], F32R) for s in range(SLOTS)]
    par = fixed("par", [P, n_columns])
    ident = fixed("ident", [P, P])
    ident_b = fixed("ident_b", [P, P], BF16)
    causal_b = fixed("causal_b", [P, P], BF16)
    cap = fixed("cap", [P, P])
    up_to = fixed("up_to", [P, 4])
    ones = fixed("ones", [P, P])
    pick = fixed("pick", [P, KT * KT])
    ones_r = fixed("ones_r", [P, P], F32R)
    eps_col = fixed("eps_col", [P, 1])
    warm = fixed("warm", [P, 1])
    one_col = fixed("one_col", [P, 1])
    half_bias = fixed("half_bias", [P, 20])
    decay4 = fixed("decay4", [P, 8])
    rot_re, rot_im = fixed("rot_re", [P, POWERS, 16]), fixed("rot_im", [P, POWERS, 16])
    gate_cols = fixed("gate_cols", [P, KT, 4])
    mag, q_re, q_im = (fixed(n, [P, 16]) for n in ("mag", "q_re", "q_im"))
    tmp_at = place[0]

    def carve(*wanted, keep=0):
        at, out = tmp_at + keep, []
        for name, shape, dt in wanted:
            size = int(np.prod(shape[1:])) * (2 if dt == BF16 else 4)
            out.append(nc.alloc_sbuf_tensor_at(name, shape, dt, offset=at))
            at += -(-size // 32) * 32
        assert at <= nc.sbuf_usable_end, (wanted[0][0], at - nc.sbuf_usable_end)
        return out

    ps = nc.alloc_psum_tensor("ps", [P, 8, HALF], F32)

    def pair(b):
        return ps[:, 2 * b:2 * b + 2, :].rearrange("p b n -> p (b n)")

    def tile(t, k, parts=slice(0, P)):
        if isinstance(k, int):
            return t[parts, k, :]
        return t[parts, bass.ds(k, 1), :].rearrange("p o n -> p (o n)")

    def col(name, k=0):
        return par[:, bass.ds(COLUMN[name] + k, 1)]

    def f32(ap):
        return ap.bitcast(F32)

    x_dram = nc.dram_tensor("x_dram", [KT, P, S], F32, kind="Internal").ap()
    rows_dram = nc.dram_tensor("rows_dram", [16, S], F32, kind="Internal").ap()
    part_dram = nc.dram_tensor("part_dram", [KT, P, S], F32, kind="Internal").ap()

    x_dram_t = x_dram.rearrange("k p n -> p k n")
    credits = []
    sems = {}

    def sem(name):
        if name not in sems:
            sems[name] = nc.alloc_semaphore(name)
        return sems[name]

    own_steps = {}

    def steps_of(e, name):
        if name not in own_steps:
            own_steps[name] = Order(e, sem(f"{name}_order"))
        return own_steps[name]

    def dve_steps(e):
        return steps_of(e, "dve")

    params_loaded, consts = sem("params_loaded"), sem("constants_made")

    loaded = [sem(f"chunk_loaded{s}") for s in range(SLOTS)]
    split_hi, split = sem("chunk_hi"), sem("chunk_split")
    multiplied = sem("chunk_multiplied")

    def chunks_once(sp, name, i, first=0, last=None):
        for j in range(first, len(stream.body[name]) if last is None else last):
            parts = stream.body[name][j]
            s, before = stream.slot(name, j), stream.before(name, j, i)
            if before is not None:
                sp.wait_ge(split, before)
            for w, kt, n, r0, rstep, c0, cstep, at in parts:
                rows = bass.ds(r0 + rstep * i, kt * P) if rstep else slice(r0, r0 + kt * P)
                cols = bass.ds(c0 + cstep * i, n) if cstep else slice(c0, c0 + n)
                sp.dma_start(raw[s][:, at:at + kt * n].rearrange("p (k n) -> p k n", k=kt),
                             w[rows, cols].rearrange("(k p) n -> p k n", p=P)).then_inc(loaded[s], 32 // len(parts))

    def load_chunks(sp, name, first=0, last=None):
        if stream.count[name] == 1:
            chunks_once(sp, name, 0, first, last)
        else:
            with sp.Fori(0, stream.count[name]) as i:
                chunks_once(sp, name, i)

    def split_chunks(pool, name, first=0, last=None):
        count = stream.count[name]

        def once(i):
            for j in range(first, len(stream.body[name]) if last is None else last):
                parts = stream.body[name][j]
                s, before = stream.slot(name, j), stream.before(name, j, i)
                n = sum(p[1] * p[2] for p in parts)
                pool.wait_ge(loaded[s], 32 * stream.loads(name, j, i))
                if before is not None:
                    pool.wait_ge(multiplied, before)
                pool.tensor_tensor(w_hi[s][:, :n], raw[s][:, :n], one_col[:, :].broadcast_to([P, n]), ALU.mult).then_inc(split_hi, 1)
                pool.wait_ge(split_hi, stream.number(name, j, i))
                pool.tensor_tensor(w_lo[s][:, :n], raw[s][:, :n], f32(w_hi[s][:, :n]), ALU.subtract).then_inc(split, 1)

        if count == 1:
            once(0)
        else:
            with pool.Fori(0, count) as i:
                once(i)

    def product(pe, o, l_hi, l_lo, r_hi, r_lo, first, last):
        pe.matmul(o, l_hi, r_hi, start=first, stop=False)
        pe.matmul(o, l_hi, r_lo, start=False, stop=False)
        return pe.matmul(o, l_lo, r_hi, start=False, stop=last)

    def columns(pe, s, bank, r_hi, r_lo, kt=KT, at=0, step=P, ready=None, part=None):
        for k in range(*(part or (0, kt))):
            if ready is not None:
                n = len(ready)
                pe.wait_ge(ready[k % n][0], ready[k % n][1] + k // n + 1)
            w = slice(at + k * step, at + k * step + P)
            for h in range(2):
                t = slice(h * HALF, (h + 1) * HALF)
                last = product(pe, ps[:, 2 * bank + h, :], w_hi[s][:, w], w_lo[s][:, w],
                               r_hi[:, k, t], r_lo[:, k, t], k == 0, k == kt - 1)
        return last

    boundary_counts = {}
    h_hi_at = -(-nc.sbuf_base // 32) * 32

    def boundary(tag, post, pre, src, y_ready, x_free, sq_free, next_chunks=None, x_at=None):
        n_post, n_pre = (KT if post else 0), (KT if pre else 0)
        X = nc.alloc_sbuf_tensor_at(f"{tag}_X", [P, KT, S], F32, offset=h_hi_at if x_at is None else x_at)
        t2, t3, sq0, sq1, t0, t1, spreads, roots, inverses = carve(
            *[(f"{tag}_{n}", [P, S], F32) for n in ("t2", "t3", "sq0", "sq1", "t0", "t1")],
            (f"{tag}_spreads", [KT, KT, P], F32), (f"{tag}_roots", [KT, P], F32), (f"{tag}_inverses", [KT, P], F32), keep=14 * S * 4)
        y_sum = t1
        sq, tmp = (sq0, sq1), (t0, t1, t2, t3)
        stats = int(bool(post)) + int(bool(pre))
        totals = dict(x_loaded=16, x_even=n_post // 2, x_odd=n_post // 2, x_stored=16 * n_post, y_squared=n_post, y_summed=max(0, n_post - 1), squared=n_pre, summed=KT - 1 if pre else 0,
                      all_summed=2 * stats, rooted=stats, inverted=stats, spreads_made=1, y_scaled=n_post,
                      h_full=n_pre, h_hi=n_pre, h_even=n_pre // 2, h_odd=n_pre // 2)
        b = {n: boundary_counts.get(n, 0) for n in totals}
        for n in totals:
            boundary_counts[n] = b[n] + totals[n]
        q = {n: sem(f"boundary_{n}") for n in totals}
        x_new = ("x_even", "x_odd")
        sums = [ps[0:KT, 4 + 2 * n, 0:P] for n in range(2)]
        first = 0 if post else 1

        def sp(e):
            for w, v in x_free:
                e.wait_ge(w, v)
            e.dma_start(X[:, :, :], src.rearrange("k p n -> p k n")).then_inc(q["x_loaded"], 16)

        def act(e):
            for w, v in sq_free:
                e.wait_ge(w, v)

            def root(stat):
                e.wait_ge(q["all_summed"], b["all_summed"] + 2 * (stat - first) + 1)
                e.activation(roots[:, :], sums[stat], ACT.Sqrt, scale=1.0 / D, bias=eps_col[0:KT, :]).then_inc(q["rooted"], 1)

            e.activation(warm[:, :], eps_col[:, :], ACT.Sqrt)
            if post:
                with e.Fori(0, KT // 2) as i:
                    for t in range(2):
                        k = 2 * i + t
                        e.wait_ge(y_ready[0], y_ready[1] + k + 1)
                        e.wait_ge(q["y_summed"], b["y_summed"] + k + 1)
                        e.activation(sq[t][:, :], tile(Y, k), ACT.Square).then_inc(q["y_squared"], 1)
                root(0)
            if pre:
                if not post:
                    e.wait_ge(q["x_loaded"], b["x_loaded"] + 16)
                with e.Fori(0, KT // 2) as i:
                    for t in range(2):
                        k = 2 * i + t
                        if post:
                            e.wait_ge(q[x_new[t]], b[x_new[t]] + i + 1 + 2 * t)
                        e.wait_ge(q["summed"], b["summed"] + k + 1)
                        e.activation(sq[t][:, :], tile(X, k), ACT.Square).then_inc(q["squared"], 1)
                        if post:
                            e.dma_start(tile(x_dram_t, k), tile(X, k)).then_inc(q["x_stored"], 16)
                root(1)
                if post:
                    e.wait_ge(q["x_stored"], b["x_stored"] + 16 * KT)
                with e.Fori(0, KT // 4) as i:
                    for t in range(4):
                        e.wait_ge(q["h_full"], b["h_full"] + 4 * i + t + 1)
                        e.activation(tile(H_hi, 4 * i + t), tmp[t][:, :], ACT.Copy).then_inc(q["h_hi"], 1)
            else:
                with e.Fori(0, KT // 2) as i:
                    for t in range(2):
                        e.wait_ge(q[x_new[t]], b[x_new[t]] + i + 1 + 2 * t)
                        e.dma_start(tile(out_x.rearrange("k p n -> p k n"), 2 * i + t), tile(X, 2 * i + t)).then_inc(q["x_stored"], 16)
                e.wait_ge(q["x_stored"], b["x_stored"] + 16 * KT)

        def pe(e):
            def add(stat, squares, start, stop):
                for m in range(KT):
                    ins = e.matmul(sums[stat], pick[:, m * KT:(m + 1) * KT], squares[:, m * P:(m + 1) * P], start=start and m == 0, stop=stop and m == KT - 1)
                return ins

            def spread(stat):
                e.wait_ge(q["spreads_made"], b["spreads_made"] + 1)
                e.wait_ge(q["inverted"], b["inverted"] + stat - first + 1)
                for m in range(KT):
                    ins = e.matmul(ps[:, 2 * stat + m // 4, (m % 4) * P:(m % 4 + 1) * P], spreads[:, m, :], inverses[:, :], start=True, stop=True)
                ins.then_inc(q["all_summed"], 1)

            if post:
                e.wait_ge(q["y_summed"], b["y_summed"] + KT - 1 + 2)
                e.wait_ge(y_ready[0], y_ready[1] + KT)
                add(0, y_sum, True, False)
                e.wait_ge(q["y_squared"], b["y_squared"] + KT)
                add(0, sq[1], False, True).then_inc(q["all_summed"], 1)
                spread(0)
            if pre:
                for k in range(KT):
                    e.wait_ge(q["squared"], b["squared"] + k + 1)
                    add(1, sq[k % 2], k == 0, k == KT - 1).then_inc(q["all_summed" if k == KT - 1 else "summed"], 1)
                spread(1)

        def pool(e):
            o = steps_of(e, "pool")
            for w, v in sq_free:
                e.wait_ge(w, v)
            e.tensor_tensor(spreads[:, :, :], ident[0:KT, 0:KT].rearrange("p (m o) -> p m o", o=1).broadcast_to([KT, KT, P]),
                            ones[0:KT, :].rearrange("p (o n) -> p o n", o=1).broadcast_to([KT, KT, P]), ALU.mult).then_inc(q["spreads_made"], 1)
            if post:
                o(e.memset(y_sum[:, :], 0.0))

                def sum_up(k, squares):
                    e.wait_ge(q["y_squared"], b["y_squared"] + k + 1)
                    e.tensor_tensor(y_sum[:, :], y_sum[:, :], squares[:, :], ALU.add).then_inc(q["y_summed"], 1)
                    e.wait_ge(q["y_summed"], b["y_summed"] + k + 3)

                with e.Fori(0, KT // 2 - 1) as i:
                    for t in range(2):
                        sum_up(2 * i + t, sq[t])
                sum_up(KT - 2, sq[0])
                with e.Fori(0, KT // 4) as i:
                    for t in (1, 3):
                        k = 4 * i + t
                        e.wait_ge(q["y_scaled"], b["y_scaled"] + k + 1)
                        e.tensor_tensor(tile(X, k), tile(X, k), tmp[t][:, :], ALU.add).then_inc(q["x_odd"], 1)
            if next_chunks:
                split_chunks(e, next_chunks, 0, SLOTS)
            if pre:
                with e.Fori(0, KT // 4) as i:
                    for t in (1, 3):
                        k = 4 * i + t
                        e.wait_ge(q["h_hi"], b["h_hi"] + k + 1)
                        e.tensor_tensor(tile(H_lo, k), tmp[t][:, :], f32(tile(H_hi, k)), ALU.subtract).then_inc(q["h_odd"], 1)

        def dve(e):
            def inverse(stat):
                e.wait_ge(q["rooted"], b["rooted"] + stat - first + 1)
                e.reciprocal(inverses[:, :], roots[:, :]).then_inc(q["inverted"], 1)
                e.wait_ge(q["all_summed"], b["all_summed"] + 2 * (stat - first) + 2)

            for w, v in sq_free:
                e.wait_ge(w, v)
            if post:
                inverse(0)
                e.wait_ge(q["x_loaded"], b["x_loaded"] + 16)
                with e.Fori(0, KT // 4) as i:
                    for t in range(4):
                        k = 4 * i + t
                        if t % 2:
                            e.wait_ge(q["x_odd"], b["x_odd"] + 2 * i + t // 2 + 1)
                        e.scalar_tensor_tensor(tmp[t][:, :], tile(Y, k), col(post, k), pair(0), ALU.mult, ALU.mult).then_inc(q["y_scaled"], 1)
                        if t % 2:
                            e.wait_ge(q["y_scaled"], b["y_scaled"] + k)
                            e.tensor_tensor(tile(X, k - 1), tile(X, k - 1), tmp[t - 1][:, :], ALU.add).then_inc(q["x_even"], 1)
                    e.wait_ge(q["x_even"], b["x_even"] + 2 * i + 2)
                e.wait_ge(q["x_odd"], b["x_odd"] + n_post // 2 + 2)
            if pre:
                if post:
                    e.wait_ge(q["y_scaled"], b["y_scaled"] + KT)
                inverse(1)
                with e.Fori(0, KT // 4) as i:
                    def low(t):
                        k = 4 * i + t
                        e.wait_ge(q["h_hi"], b["h_hi"] + k + 1)
                        e.tensor_tensor(tile(H_lo, k), tmp[t][:, :], f32(tile(H_hi, k)), ALU.subtract).then_inc(q["h_even"], 1)

                    for t in range(4):
                        k = 4 * i + t
                        if t % 2:
                            e.wait_ge(q["h_odd"], b["h_odd"] + 2 * i + t // 2 + 1)
                        e.scalar_tensor_tensor(tmp[t][:, :], tile(X, k), col(pre, k), pair(1), ALU.mult, ALU.mult).then_inc(q["h_full"], 1)
                        if t % 2:
                            low(t - 1)
                    e.wait_ge(q["h_even"], b["h_even"] + 2 * i + 2)

        if "boundary" not in own_steps:
            own_steps["boundary"] = True
            credits.extend([(q["summed"], 2), (q["y_summed"], 2), (q["x_odd"], 2), (q["h_odd"], 2)])
        h_ready = [(q["h_even"], b["h_even"]), (q["h_odd"], b["h_odd"] + 2)]
        done = ([(w, v + n_pre // 2) for w, v in h_ready] if pre else []) + ([(q["x_stored"], b["x_stored"] + 16 * KT)] if post else [])
        return dict(sp=sp, act=act, pe=pe, pool=pool, dve=dve, h_ready=h_ready, tmp_free=done)

    def fox(h_ready, tmp_free):
        u0, u1, sum0, sum1, mixed, mix_hi, mix_lo, f_abs, f_min, negc_rows, ones_rows = carve(
            ("pool_u0", [P, PAD + S], F32), ("pool_u1", [P, PAD + S], F32), ("pool_sum0", [P, PAD + S], F32), ("pool_sum1", [P, PAD + S], F32),
            ("pool_mixed", [P, S], F32), ("pool_hi", [P, S], F32R), ("pool_lo", [P, S], F32R),
            ("f_abs", [8, S], F32), ("f_min", [8, S], F32), ("negc_rows", [8, S], F32), ("ones_rows", [8, S], F32))
        uu = (u0, u1)
        negc_ready, negc_stored = (sem(f"fox_{n}") for n in ("negc_ready", "negc_stored"))
        u_ready, pool_mixed, pool_hi_done, pool_ready, pool_done = (sem(f"fox_{n}") for n in ("u_ready", "pool_mixed", "pool_hi", "pool_ready", "pool_done"))
        NP = "fox_pre"

        q_hi, q_lo, k_hi, k_lo, v_t, v_hi, v_lo, negc_b, s0, s1, p0, p1, pt_hi, pt_lo, stat, waited = carve(
            ("q_hi", [P, S], F32R), ("q_lo", [P, S], F32R), ("k_hi", [P, S], F32R), ("k_lo", [P, S], F32R), ("v_t", [P, S], F32),
            ("v_hi", [P, KT, P], F32R), ("v_lo", [P, KT, P], F32R), ("negc_b", [P, 2, S], F32),
            ("s0", [P, S], F32), ("s1", [P, S], F32), ("p0", [P, S], F32), ("p1", [P, S], F32),
            ("pt_hi", [P, KT, 256], F32R), ("pt_lo", [P, KT, 256], F32R), ("fox_stat", [P, 16], F32), ("fox_waited", [P, 2 * KT], F32))
        s_sb, p_sb = (s0, s1), (p0, p1)
        qkv_hi, qk_split, vt_ready, vt_done, v_split = (sem(f"fox_{n}") for n in ("qkv_hi", "qk_split", "vt_ready", "vt_transposed", "v_split"))
        scored, maxed, exped, p_ready, pt_done, pt_hi_done, pt_split, pv_done, attn_out = (
            sem(f"fox_{n}") for n in ("scored", "maxed", "exped", "p_ready", "pt_transposed", "pt_hi", "pt_split", "pv_done", "attn_out"))
        negc_loaded = sem("fox_negc_loaded")
        cat_hi, cat_ready, out_ready = sem("fox_cat_hi"), sem("fox_cat_ready"), sem("fox_out_ready")
        N = 2 * KT
        credits.extend([(maxed, N), (pt_split, N), (v_split, 1), (attn_out, N // 2), (pv_done, N // 2), (exped, N), (pt_done, N), (qk_split, 2)])

        def length(n):
            return (n % KT + 1) * P

        def sp(e):
            load_chunks(e, NP)
            e.wait_ge(negc_ready, 1)
            e.dma_start(rows_dram[0:8, :], negc_rows[:, :]).then_inc(negc_stored, 16)
            e.wait_ge(negc_stored, 16)
            with e.Fori(0, FOX_PAIRS) as j:
                chunks_once(e, "fox", j)
                e.wait_ge(maxed, N * j + N)
                for hd in range(2):
                    if hd == 0:
                        e.wait_ge(pool_done, 5)
                    e.dma_start(negc_b[:, hd, :], rows_dram[bass.ds(2 * j + hd, 1), :].broadcast_to([P, S])).then_inc(negc_loaded, 16)
            load_chunks(e, "fox_out")

        def pool(e):
            for s, v in tmp_free:
                e.wait_ge(s, v)
            o = steps_of(e, "pool")
            for t in (u0, u1, sum0, sum1):
                o.step(e.memset(t[:, 0:PAD], 0.0))
            o.step(e.memset(ones_rows[:, :], 1.0))
            split_chunks(e, NP, SLOTS)
            split_chunks(e, "fox")
            split_chunks(e, "fox_out")

        def pe(e):
            e.wait_ge(split, stream.number(NP, 0))
            columns(e, 0, 0, H_hi, H_lo, ready=h_ready).then_inc(multiplied, 1)
            for g in range(4):
                e.wait_ge(split, stream.number(NP, 1 + g))
                bank = 1 + g % 3
                if g == 3:
                    e.wait_ge(u_ready, 1)
                columns(e, stream.slot(NP, 1 + g), bank, H_hi, H_lo).then_inc(multiplied, 1)
            e.wait_ge(split, stream.number(NP, 5))
            s = stream.slot(NP, 5)
            for g in range(4):
                e.wait_ge(pool_ready, g + 1)
                if g == 0:
                    e.wait_ge(negc_ready, 1)
                else:
                    e.wait_ge(pool_done, g)
                for h in range(2):
                    t = slice(h * HALF, (h + 1) * HALF)
                    ins = product(e, ps[:, h, :], w_hi[s][:, g * P:(g + 1) * P], w_lo[s][:, g * P:(g + 1) * P], mix_hi[:, t], mix_lo[:, t], True, True)
                ins.then_inc(multiplied if g == 3 else pool_mixed, 1)
            e.wait_ge(pool_done, 4)
            with e.Fori(0, FOX_PAIRS) as j:
                for c in range(3):
                    e.wait_ge(split, stream.number("fox", c, j))
                    if c < 2:
                        e.wait_ge(maxed, N * j + N - 1 + c)
                    else:
                        e.wait_ge(pt_split, N * j + N)
                    columns(e, stream.slot("fox", c), c, H_hi, H_lo).then_inc(multiplied, 1)
                e.wait_ge(vt_ready, j + 1)
                e.wait_ge(attn_out, (N // 2) * j + N // 2)
                for k in range(KT):
                    ins = e.transpose(ps[:, 6 + k // 4, (k % 4) * P:(k % 4 + 1) * P], v_t[:, k * P:(k + 1) * P], ident[:, :])
                ins.then_inc(vt_done, 1)
                for n in range(N + 2):
                    if n < N:
                        hd, i, bank = n // KT, n % KT, n % 2
                        r = slice(64 * hd, 64 * hd + 64)
                        if n == 0:
                            e.wait_ge(qk_split, 2 * j + 4)
                        elif n >= 2:
                            e.wait_ge(maxed, N * j + N + n - 1)
                        qs = slice(i * P, (i + 1) * P)
                        for h in range(2):
                            width = min(HALF, length(n) - h * HALF)
                            if width <= 0:
                                continue
                            o, ks = ps[:, 2 * bank + h, 0:width], slice(h * HALF, h * HALF + width)
                            ends = h == (length(n) - 1) // HALF
                            ins = product(e, o, q_hi[r, qs], q_lo[r, qs], k_hi[r, ks], k_lo[r, ks], True, not ends)
                            if ends:
                                ins = e.matmul(ps[:, 2 * bank + h, width - P:width], ident_b[:, :], causal_b[:, :], start=False, stop=True)
                        ins.then_inc(scored, 1)
                    if 1 <= n <= N:
                        m = n - 1
                        e.wait_ge(p_ready, N * j + m + 1)
                        e.wait_ge(pt_split, N * j + N + m)
                        for k in range(m % KT + 1):
                            ins = e.transpose(ps[:, 4 + k // 4, (k % 4) * P:(k % 4 + 1) * P], p_sb[m % 2][:, k * P:(k + 1) * P], ident[:, :])
                        ins.then_inc(pt_done, 1)
                    if n >= 3 and n % 2 == 1:
                        m = (n - 3) // 2
                        e.wait_ge(pt_split, N * j + N + n - 1)
                        if m == 0:
                            e.wait_ge(v_split, j + 2)
                        if m >= 2:
                            e.wait_ge(attn_out, (N // 2) * j + N // 2 + m - 1)
                        last = 2 * (m % (KT // 2)) + 1
                        for k in range(last + 1):
                            cols = slice(P, 256) if k == last else slice(0, 256)
                            ins = product(e, ps[:, 6 + m % 2, cols], v_hi[:, k, :], v_lo[:, k, :], pt_hi[:, k, cols], pt_lo[:, k, cols], k == 0, k == last)
                        ins.then_inc(pv_done, 1)
            with e.Fori(0, 2) as i:
                for c in range(4):
                    e.wait_ge(split, stream.number("fox_out", c, i))
                    e.wait_ge(out_ready, 4 * i + c + 1)
                    columns(e, stream.slot("fox_out", c), c, H_hi, H_lo, ready=[(cat_ready, 0)] if c == 0 else None).then_inc(multiplied, 1)
        credits.append((out_ready, 4))

        def act(e):
            a = steps_of(e, "act")
            for s, v in tmp_free:
                e.wait_ge(s, v)
            e.wait_ge(multiplied, stream.number(NP, 0))
            a(e.activation(f_abs[:, :], pair(0)[0:8, :], ACT.Abs, bias=par[0:8, COLUMN["row_bias"]:COLUMN["row_bias"] + 1]))
            a(e.activation(f_abs[:, :], f_abs[:, :], ACT.Exp, scale=-1.0))
            a.step(e.activation(f_abs[:, :], f_abs[:, :], ACT.Ln, bias=one_col[0:8, :]))
            e.wait_ge(sem("pool_order"), CONSTANT_STEPS + 5)
            for g in range(4):
                e.wait_ge(multiplied, stream.number(NP, 1 + g))
                if g >= 2:
                    e.wait_ge(pool_ready, g - 1)
                e.activation(uu[g % 2][:, PAD:], pair(1 + g % 3), ACT.Copy).then_inc(u_ready, 1)
                if g >= 1:
                    split_mixed(e, g - 1)
            split_mixed(e, 3)
            with e.Fori(0, FOX_PAIRS) as j:
                e.wait_ge(pool_done, 5)
                e.wait_ge(multiplied, stream.number("fox", 0, j))
                e.activation(q_hi[:, :], pair(0), ACT.Copy, scale=0.125).then_inc(qkv_hi, 1)
                e.wait_ge(multiplied, stream.number("fox", 1, j))
                e.activation(k_hi[:, :], pair(1), ACT.Copy).then_inc(qkv_hi, 1)
                e.wait_ge(multiplied, stream.number("fox", 2, j))
                e.activation(v_t[:, :], pair(2), ACT.Copy).then_inc(vt_ready, 1)
                e.wait_ge(vt_done, j + 1)
                e.wait_ge(pv_done, (N // 2) * j + N // 2)
                e.activation(v_hi[:, :, :].rearrange("p k n -> p (k n)"), pair(3), ACT.Copy).then_inc(qkv_hi, 1)
                for n in range(N + 4):
                    if n < N:
                        ln = length(n)
                        e.wait_ge(maxed, N * j + N + n + 1)
                        e.wait_ge(pt_done, N * j + N + n - 1)
                        e.activation(p_sb[n % 2][:, 0:ln], s_sb[n % 2][:, 0:ln], ACT.Exp, scale=-1.0, bias=stat[:, n % 2:1 + n % 2],
                                     accum_out=stat[:, 4 + n % 2:5 + n % 2]).then_inc(exped, 1)
                    if 1 <= n <= N:
                        m = n - 1
                        i = m % KT
                        e.wait_ge(pt_done, N * j + N + m + 1)
                        e.wait_ge(pv_done, (N // 2) * j + N // 2 + m // 2)
                        e.activation(pt_hi[:, 0:i + 1, (i % 2) * P:(i % 2 + 1) * P],
                                     pair(2)[:, 0:(i + 1) * P].rearrange("p (k n) -> p k n", n=P), ACT.Copy).then_inc(pt_hi_done, 1)
                    if n >= 4 and n % 2 == 0:
                        m = (n - 4) // 2
                        hd, c = m // (KT // 2), m % (KT // 2)
                        r = slice(64 * hd, 64 * hd + 64)
                        e.wait_ge(pv_done, (N // 2) * j + N // 2 + m + 1)
                        e.activation(tile(Y, j, r)[:, c * 256:(c + 1) * 256], ps[r, 6 + m % 2, 0:256], ACT.Copy).then_inc(attn_out, 1)
            e.wait_ge(attn_out, (N // 2) * (FOX_PAIRS + 1))
            e.wait_ge(pool_done, 5)
            e.wait_ge(multiplied, stream.number("fox", 2, FOX_PAIRS - 1))
            with e.Fori(0, KT) as k:
                e.activation(tile(H_hi, k), tile(Y, k), ACT.Copy).then_inc(cat_hi, 1)

        def split_mixed(e, g):
            e.wait_ge(pool_mixed_full, g + 1)
            if g >= 1:
                e.wait_ge(pool_mixed, g)
            e.activation(mix_hi[:, :], mixed[:, :], ACT.Copy).then_inc(pool_hi_done, 1)
        pool_mixed_full = sem("fox_pool_mixed_full")

        def dve(e):
            o = dve_steps(e)
            bias = par[0:8, COLUMN["row_bias"]:COLUMN["row_bias"] + 1]
            for s, v in tmp_free:
                e.wait_ge(s, v)
            e.wait_ge(sem("act_order"), PRELUDE_ACT + 1)
            o(e.tensor_scalar(f_min[:, :], pair(0)[0:8, :], bias, 0.0, ALU.add, ALU.min))
            e.wait_ge(sem("act_order"), PRELUDE_ACT + 3)
            o(e.tensor_tensor(f_min[:, :], f_abs[:, :], f_min[:, :], ALU.subtract))
            e.wait_ge(sem("pool_order"), CONSTANT_STEPS + 5)
            e.tensor_tensor_scan(negc_rows[:, :], ones_rows[:, :], f_min[:, :], 0.0, ALU.mult, ALU.add).then_inc(negc_ready, 1)
            for g, w in enumerate(POOL_WINDOWS):
                u, sums = uu[g % 2], (sum0, sum1)
                e.wait_ge(u_ready, g + 1)
                have, at = u, 1
                while at < w:
                    to = sums[0] if have is not sums[0] else sums[1]
                    o(e.tensor_tensor(to[:, PAD:], have[:, PAD:], have[:, PAD - at:PAD + S - at], ALU.add))
                    have, at = to, 2 * at
                if g >= 1:
                    e.wait_ge(pool_hi_done, g)
                o(e.scalar_tensor_tensor(mixed[:, :], have[:, PAD:], 1.0 / w, u[:, PAD:], ALU.mult, ALU.subtract))
                inv = par[:, COLUMN["inv_count"] + PAD * g:COLUMN["inv_count"] + PAD * (g + 1)]
                o(e.tensor_tensor(have[:, PAD:2 * PAD], have[:, PAD:2 * PAD], inv, ALU.mult))
                e.tensor_tensor(mixed[:, 0:PAD], have[:, PAD:2 * PAD], u[:, PAD:2 * PAD], ALU.subtract).then_inc(pool_mixed_full, 1)
                if g >= 1:
                    e.wait_ge(pool_mixed, g)
                    e.tensor_scalar(tile(Y, 3 + g), pair(0), col("pool_scale", g - 1), None, ALU.mult).then_inc(pool_done, 1)
                e.wait_ge(pool_hi_done, g + 1)
                e.tensor_tensor(mix_lo[:, :], mixed[:, :], f32(mix_hi[:, :]), ALU.subtract).then_inc(pool_ready, 1)
            e.wait_ge(multiplied, stream.number(NP, 5))
            o(e.tensor_scalar(tile(Y, 7), pair(0), col("pool_scale", 3), None, ALU.mult))
            e.wait_ge(negc_stored, 16)
            e.engine_nop().then_inc(pool_done, 2)
            with e.Fori(0, FOX_PAIRS) as j:
                o.enter(j, N)
                e.wait_ge(qkv_hi, 3 * j + 1)
                e.scalar_tensor_tensor(q_lo[:, :], pair(0), 0.125, f32(q_hi[:, :]), ALU.mult, ALU.subtract).then_inc(qk_split, 1)
                e.wait_ge(qkv_hi, 3 * j + 2)
                e.tensor_tensor(k_lo[:, :], pair(1), f32(k_hi[:, :]), ALU.subtract).then_inc(qk_split, 1)
                e.wait_ge(qkv_hi, 3 * j + 3)
                e.tensor_tensor(v_lo[:, :, :].rearrange("p k n -> p (k n)"), pair(3), f32(v_hi[:, :, :].rearrange("p k n -> p (k n)")), ALU.subtract).then_inc(v_split, 1)
                e.wait_ge(negc_loaded, 32 * j + 32)
                for n in range(N + 1):
                    if n < N:
                        ln, b = length(n), n % 2
                        e.wait_ge(scored, N * j + n + 1)
                        e.wait_ge(exped, N * j + N + n - 1)
                        e.memset(waited[:, n:n + 1], 0.0)
                        e.tensor_tensor_reduce(out=s_sb[b][:, 0:ln], in0=pair(b)[:, 0:ln], in1=negc_b[:, n // KT, 0:ln], scale=-1.0, scalar=-FILL,
                                               op0=ALU.add, op1=ALU.min, accum_out=stat[:, b:b + 1]).then_inc(maxed, 1)
                        e.wait_ge(exped, N * j + N + n + 1)
                        o(e.reciprocal(stat[:, 6 + b:7 + b], stat[:, 4 + b:5 + b]))
                        e.tensor_scalar(p_sb[b][:, 0:ln], p_sb[b][:, 0:ln], stat[:, 6 + b:7 + b], None, ALU.mult).then_inc(p_ready, 1)
                    if n >= 1:
                        m = n - 1
                        i = m % KT
                        e.wait_ge(pt_hi_done, N * j + m + 1)
                        cols = slice((i % 2) * P, (i % 2 + 1) * P)
                        e.tensor_tensor(pt_lo[:, 0:i + 1, cols], pair(2)[:, 0:(i + 1) * P].rearrange("p (k n) -> p k n", n=P),
                                        f32(pt_hi[:, 0:i + 1, cols]), ALU.subtract).then_inc(pt_split, 1)
                o.leave(FOX_PAIRS)
            with e.Fori(0, KT) as k:
                e.wait_ge(cat_hi, k + 1)
                e.tensor_tensor(tile(H_lo, k), tile(Y, k), f32(tile(H_hi, k)), ALU.subtract).then_inc(cat_ready, 1)
            e.wait_ge(cat_ready, KT)
            with e.Fori(0, 2) as i:
                for c in range(4):
                    e.wait_ge(multiplied, stream.number("fox_out", c, i))
                    e.tensor_copy(tile(Y, 4 * i + c), pair(c)).then_inc(out_ready, 1)

        attended = [(attn_out, (N // 2) * (FOX_PAIRS + 1)), (pool_done, 5)]
        return dict(sp=sp, pool=pool, pe=pe, act=act, dve=dve, y_ready=(out_ready, 4), x_free=attended, sq_free=attended)

    def ffn(l, h_ready, tmp_free):
        f_hi0, f_hi1, f_lo0, f_lo1, th0, th1, a0, a1, f0, f1 = carve(
            *[(f"ffn{l}_{n}", [P, 2, S], F32R) for n in ("f_hi0", "f_hi1", "f_lo0", "f_lo1")],
            *[(f"ffn{l}_{n}", [P, S], F32) for n in ("th0", "th1", "a0", "a1", "f0", "f1")])
        f_hi, f_lo, th, a, f = (f_hi0, f_hi1), (f_lo0, f_lo1), (th0, th1), (a0, a1), (f0, f1)
        tanh_done, gated, f_full, f_hi_done, f_ready, down_part, y_added = (
            sem(f"ffn_{n}") for n in ("tanh", "gated", "f_full", "f_hi", "f_ready", "down_part", "y_added"))
        LOOPS = (FF_BLOCKS - 1) // 2
        first, loop, tail = f"ffn{l}_first", f"ffn{l}", f"ffn{l}_last"
        if l == 0:
            credits.extend([(y_added, KT), (gated, 2)])
        B = l * FF_BLOCKS

        def pe_gate_up(e, b, name, at, i, ready=None):
            for c in range(4):
                e.wait_ge(split, stream.number(name, at + c, i))
                if ready is None:
                    e.wait_ge(f_full, 2 * (b - 1) + c // 2 + 1)
                    e.wait_ge(y_added, 8 * b - 4 + c + 1)
                columns(e, stream.slot(name, at + c), c, H_hi, H_lo, ready=ready if c == 0 else None).then_inc(multiplied, 1)

        def pe_down(e, b, par_, name, at, i, alone=False):
            for c in range(2):
                s = stream.slot(name, at + c)
                e.wait_ge(split, stream.number(name, at + c, i))
                if c == 0:
                    e.wait_ge(f_ready, 2 * b + 2)
                for q in range(4):
                    n = 4 * c + q
                    if n >= 4 or alone:
                        e.wait_ge(y_added, 8 * b + (n - 4) + 1 + 8)
                    else:
                        e.wait_ge(f_full, 2 * (b + 1) + q // 2 + 1)
                    ins = columns(e, s, q, f_hi[par_], f_lo[par_], kt=2, at=q * P, step=HALF)
                    ins.then_inc(multiplied if q == 3 else down_part, 1)

        def act_block(e, b, par_, name, at, i):
            for t in range(2):
                e.wait_ge(multiplied, stream.number(name, at + 2 * t, i))
                e.wait_ge(gated, 2 * b + t + 1)
                e.activation(th[t][:, :], pair(2 * t), ACT.Tanh, scale=0.5).then_inc(tanh_done, 1)
                e.wait_ge(f_full, 2 * b + t + 1)
                e.activation(f_hi[par_][:, t, :], f[t][:, :], ACT.Copy).then_inc(f_hi_done, 1)

        def dve_block(e, b, par_, name, at, i):
            for t in range(2):
                e.wait_ge(tanh_done, 2 * b + t + 1)
                e.scalar_tensor_tensor(a[t][:, :], th[t][:, :], 1.0, pair(2 * t), ALU.add, ALU.mult).then_inc(gated, 1)
                e.wait_ge(gated, 2 * b + t + 3)
                e.wait_ge(multiplied, stream.number(name, at + 2 * t + 1, i))
                e.scalar_tensor_tensor(f[t][:, :], a[t][:, :], 0.5, pair(2 * t + 1), ALU.mult, ALU.mult).then_inc(f_full, 1)
                e.wait_ge(f_hi_done, 2 * b + t + 1)
                e.tensor_tensor(f_lo[par_][:, t, :], f[t][:, :], f32(f_hi[par_][:, t, :]), ALU.subtract).then_inc(f_ready, 1)

        def dve_down(e, b, name, at, i):
            for n in range(KT):
                if n % 4 == 3:
                    e.wait_ge(multiplied, stream.number(name, at + n // 4, i))
                else:
                    e.wait_ge(down_part, 6 * b + 3 * (n // 4) + n % 4 + 1)
                e.tensor_tensor(Y[:, n, :], Y[:, n, :], pair(n % 4), ALU.add).then_inc(y_added, 1)
            e.wait_ge(y_added, 8 * b + 16)

        def sp(e):
            for name in (first, loop, tail):
                load_chunks(e, name)

        def pool(e):
            split_chunks(e, first, SLOTS)
            for name in (loop, tail):
                split_chunks(e, name)

        def pe(e):
            pe_gate_up(e, B, first, 0, 0, ready=h_ready)
            with e.Fori(0, LOOPS) as i:
                for u in range(2):
                    pe_gate_up(e, B + 2 * i + 1 + u, loop, 6 * u, i)
                    pe_down(e, B + 2 * i + u, u, loop, 6 * u + 4, i)
            pe_down(e, B + FF_BLOCKS - 1, 0, tail, 0, 0, alone=True)

        def act(e):
            for s, v in tmp_free:
                e.wait_ge(s, v)
            act_block(e, B, 0, first, 0, 0)
            with e.Fori(0, LOOPS) as i:
                for u in range(2):
                    e.wait_ge(y_added, 8 * (B + 2 * i + u) + 8)
                    act_block(e, B + 2 * i + 1 + u, 1 - u, loop, 6 * u, i)

        def dve(e):
            for s, v in tmp_free:
                e.wait_ge(s, v)
            dve_steps(e)(e.memset(Y[:, :, :], 0.0))
            dve_block(e, B, 0, first, 0, 0)
            with e.Fori(0, LOOPS) as i:
                for u in range(2):
                    dve_block(e, B + 2 * i + 1 + u, 1 - u, loop, 6 * u, i)
                    dve_down(e, B + 2 * i + u, loop, 6 * u + 4, i)
            dve_down(e, B + FF_BLOCKS - 1, tail, 0, 0)

        return dict(sp=sp, pool=pool, pe=pe, act=act, dve=dve, y_ready=(y_added, KT * (B + FF_BLOCKS)),
                    x_free=[(multiplied, stream.number(loop, 9, LOOPS - 1))], sq_free=[])

    def prelude():
        theta, turns, small, e24, n24, r24, bits, s8, p8, u16, v16 = carve(
            ("pre_theta", [P, POWERS, 16], F32), ("pre_turns", [P, POWERS, 16], F32), ("pre_small", [P, POWERS, 16], F32),
            ("pre_e24", [P, 24], F32), ("pre_n24", [P, 24], F32), ("pre_r24", [P, 24], F32), ("pre_bits", [P, 24], mybir.dt.int32),
            ("pre_s8", [P, 8], F32), ("pre_p8", [P, 8], F32), ("pre_u16", [P, 16], F32), ("pre_v16", [P, 16], F32))
        e8, t16 = e24[:, 0:8], e24[:, 8:24]

        def vec(name, n):
            return par[:, COLUMN[name]:COLUMN[name] + n]

        TURN = (6.28125, 0.0019350051879882812, 3.0199159819e-07)
        ROUND = 12582912.0

        def exponential(e, o, out, x, n):
            turns_, rest, two_k = n24[:, 0:n], r24[:, 0:n], bits[:, 0:n]
            o(e.tensor_scalar(x, x, 88.0, -87.0, ALU.min, ALU.max))
            o(e.tensor_scalar(turns_, x, 1.4426950408889634, ROUND, ALU.mult, ALU.add))
            o(e.tensor_scalar(turns_, turns_, ROUND, None, ALU.subtract))
            o(e.scalar_tensor_tensor(x, turns_, -0.693359375, x, ALU.mult, ALU.add))
            o(e.scalar_tensor_tensor(x, turns_, 2.12194440e-4, x, ALU.mult, ALU.add))
            o(e.tensor_scalar(rest, x, 1.0 / 5040, None, ALU.mult))
            for c in (1.0 / 720, 1.0 / 120, 1.0 / 24, 1.0 / 6, 0.5, 1.0):
                o(e.scalar_tensor_tensor(rest, rest, c, x, ALU.add, ALU.mult))
            o(e.tensor_scalar(two_k, turns_, 127.0, 8388608.0, ALU.add, ALU.mult))
            o(e.scalar_tensor_tensor(out, rest, 1.0, two_k.bitcast(F32), ALU.add, ALU.mult))

        def dve(e):
            o = dve_steps(e)
            o(e.scalar_tensor_tensor(e8, vec("od_lam", 8), -1.0, vec("od_lam", 8), ALU.mult, ALU.min))
            o(e.tensor_copy(t16, vec("log_dt", 16)))
            exponential(e, o, e24[:, :], e24[:, :], 24)
            for k, (name, n) in enumerate((("od_b_a", 8), ("od_b_x", 8), ("b_glu", 4))):
                o(e.tensor_scalar(half_bias[:, 8 * k:8 * k + n], vec(name, n), 0.5, None, ALU.mult))
            o(e.tensor_scalar(s8[:, :], e8, 2.0, None, ALU.add))
            o(e.reciprocal(s8[:, :], s8[:, :]))
            o(e.tensor_tensor(s8[:, :], s8[:, :], e8, ALU.mult))
            o(e.tensor_tensor(e8, s8[:, :], s8[:, :], ALU.mult))
            o(e.tensor_scalar(p8[:, :], e8, 1.0 / 19, 1.0 / 17, ALU.mult, ALU.add))
            for n in (15, 13, 11, 9, 7, 5, 3, 1):
                o(e.tensor_tensor(p8[:, :], p8[:, :], e8, ALU.mult))
                o(e.tensor_scalar(p8[:, :], p8[:, :], 1.0 / n, None, ALU.add))
            o(e.scalar_tensor_tensor(p8[:, :], p8[:, :], 2.0, s8[:, :], ALU.mult, ALU.mult))
            o(e.tensor_scalar(s8[:, :], vec("od_lam", 8), -1.0, 0.0, ALU.mult, ALU.max))
            o(e.tensor_tensor(p8[:, :], p8[:, :], s8[:, :], ALU.add))
            o(e.tensor_scalar(decay4[:, :], p8[:, :], -4.0, None, ALU.mult))
            o(e.tensor_tensor(theta[:, 0, :], vec("lam_im", 16), t16, ALU.mult))
            o(e.tensor_tensor(u16[:, :], vec("lam_re", 16), t16, ALU.mult))
            exponential(e, o, mag[:, :], u16[:, :], 16)
            for k in range(1, POWERS):
                o(e.tensor_scalar(theta[:, k, :], theta[:, 0, :], float(2 ** k), None, ALU.mult))
            o(e.tensor_scalar(turns[:, :, :], theta[:, :, :], 0.15915494309189535, None, ALU.mult))
            o(e.tensor_scalar(turns[:, :, :], turns[:, :, :], ROUND, ROUND, ALU.add, ALU.subtract))
            for part in TURN:
                o(e.scalar_tensor_tensor(theta[:, :, :], turns[:, :, :], -part, theta[:, :, :], ALU.mult, ALU.add))
            o(e.tensor_scalar(theta[:, :, :], theta[:, :, :], 3.1415925, -3.1415925, ALU.min, ALU.max))
            o(e.scalar_tensor_tensor(small[:, :, :], theta[:, :, :], -1.0, theta[:, :, :], ALU.mult, ALU.max))
            o(e.tensor_scalar(small[:, :, :], small[:, :, :], -1.0, 1.5707963267948966, ALU.mult, ALU.add))
            assert o.n == ANGLES
            e.wait_ge(sem("act_order"), PRELUDE_ACT)
            lr, li = vec("lam_re", 16), vec("lam_im", 16)
            o(e.tensor_tensor(t16, mag[:, :], rot_re[:, 0, :], ALU.mult))
            o(e.tensor_scalar(t16, t16, -1.0, None, ALU.add))
            o(e.tensor_tensor(u16[:, :], mag[:, :], rot_im[:, 0, :], ALU.mult))
            o(e.tensor_tensor(q_re[:, :], t16, lr, ALU.mult))
            o(e.tensor_tensor(v16[:, :], u16[:, :], li, ALU.mult))
            o(e.tensor_tensor(q_re[:, :], q_re[:, :], v16[:, :], ALU.add))
            o(e.tensor_tensor(q_im[:, :], u16[:, :], lr, ALU.mult))
            o(e.tensor_tensor(v16[:, :], t16, li, ALU.mult))
            o(e.tensor_tensor(q_im[:, :], q_im[:, :], v16[:, :], ALU.subtract))
            o(e.tensor_tensor(t16, lr, lr, ALU.mult))
            o(e.tensor_tensor(u16[:, :], li, li, ALU.mult))
            o(e.tensor_tensor(t16, t16, u16[:, :], ALU.add))
            o(e.reciprocal(t16, t16))
            o(e.tensor_tensor(q_re[:, :], q_re[:, :], t16, ALU.mult))
            o(e.tensor_tensor(q_im[:, :], q_im[:, :], t16, ALU.mult))
            assert o.n == END

        def act(e):
            a = steps_of(e, "act")
            e.wait_ge(sem("dve_order"), ANGLES)
            a.step(e.activation(rot_im[:, :, :], theta[:, :, :], ACT.Sin))
            a.step(e.activation(rot_re[:, :, :], small[:, :, :], ACT.Sin))

        ANGLES, END = 77, 92
        return dict(dve=dve, act=act, tmp_free=[(sem("dve_order"), END)])

    def lru(h_ready, tmp_free):
        xpad, xc, xc_hi, xc_lo, G, out_hi, out_lo, T0, T1, T2, T3 = carve(
            ("lru_xpad", [P, 2, 3 + S], F32), ("lru_xc", [P, 2, S], F32), ("lru_xc_hi", [P, 2, S], F32R), ("lru_xc_lo", [P, 2, S], F32R),
            ("lru_G", [P, 2, S], F32), ("lru_out_hi", [P, 2, S], F32R), ("lru_out_lo", [P, 2, S], F32R),
            *[(f"lru_T{n}", [P, S], F32) for n in range(4)])
        names = ("x_read", "gate_sq", "gate_arg", "gate_tanh", "conv", "xc_hi", "xc_ready", "gates_read", "log_a", "decay",
                 "root", "out_full", "out_hi", "out_ready", "y_added", "down_part", "wax_part")
        s = {n: sem(f"lru_{n}") for n in names}
        first, loop, tail = "lru_first", "lru", "lru_last"
        T = (T0, T1, T2, T3)
        credits.extend([(s["out_ready"], 2), (s["y_added"], KT)])

        def pe_in(e, j, name, i, ready=None):
            for c in range(4):
                e.wait_ge(split, stream.number(name, c, i))
                if ready is None:
                    e.wait_ge(s["gates_read"], 4 * (j - 1) + (1, 3, 2, 4)[c])
                columns(e, stream.slot(name, c), c, H_hi, H_lo, ready=ready if c == 0 else None).then_inc(multiplied, 1)

        def pe_out(e, j, name, at, i, alone=False):
            for c in range(2):
                sl = stream.slot(name, at + c)
                e.wait_ge(split, stream.number(name, at + c, i))
                e.wait_ge(s["out_ready"], 2 * j + 4)
                for q in range(4):
                    n = 4 * c + q
                    if n >= 4:
                        e.wait_ge(s["y_added"], 8 * j + (n - 4) + 1 + KT)
                    elif alone:
                        e.wait_ge(s["gates_read"], 4 * (j + 1))
                    elif n < 2:
                        e.wait_ge(s["x_read"], 2 * (j + 1) + n + 1)
                    else:
                        e.wait_ge(s["gate_sq"], 2 * (j + 1) + n - 1)
                    columns(e, sl, q, out_hi, out_lo, kt=2, at=q * P, step=HALF).then_inc(multiplied if q == 3 else s["down_part"], 1)

        def pe_gates(e, j, name, at, i, first_head=False):
            sl = stream.slot(name, at)
            e.wait_ge(split, stream.number(name, at, i))
            for c, bank in ((0, 0), (2, 2), (1, 1), (3, 3)):
                if c == 0:
                    e.wait_ge(s["xc_ready"], 2 * j + 2)
                if first_head:
                    if c < 2:
                        e.wait_ge(s["x_read"], 2)
                    else:
                        e.wait_ge(s["gate_sq"], 2)
                else:
                    e.wait_ge(s["y_added"], 8 * (j - 1) + 4 + bank + 1 + KT)
                columns(e, sl, bank, xc_hi, xc_lo, kt=2, at=HALF * (c // 2) + (c % 2) * P, step=256).then_inc(multiplied if c == 3 else s["wax_part"], 1)

        def act_in(e, j, name, i):
            for t in range(2):
                e.wait_ge(multiplied, stream.number(name, t, i))
                e.activation(xpad[:, t, 3:], pair(t), ACT.Copy).then_inc(s["x_read"], 1)
            for t in range(2):
                e.wait_ge(s["conv"], 2 * j + t + 1)
                e.activation(xc_hi[:, t, :], xc[:, t, :], ACT.Copy).then_inc(s["xc_hi"], 1)
            for t in range(2):
                e.wait_ge(multiplied, stream.number(name, 2 + t, i))
                e.activation(G[:, t, :], pair(2 + t), ACT.Copy)
                e.activation(T[t][:, :], pair(2 + t), ACT.Square).then_inc(s["gate_sq"], 1)
            for t in range(2):
                e.wait_ge(s["gate_arg"], 2 * j + t + 1)
                e.activation(T[t][:, :], T[t][:, :], ACT.Tanh, scale=GELU_C).then_inc(s["gate_tanh"], 1)

        def act_chain(e, j, name, at, i):
            for t in range(2):
                c = bass.ds(2 * j + t, 1)
                if t == 0:
                    e.wait_ge(s["wax_part"], 3 * j + 1)
                    e.wait_ge(s["gate_tanh"], 2 * j + 2)
                    e.wait_ge(s["out_ready"], 2 * j + 2)
                    e.wait_ge(s["gelu"], 2 * j + 2)
                else:
                    e.wait_ge(s["wax_part"], 3 * j + 3)
                    e.wait_ge(s["out_ready"], 2 * j + 3)
                e.activation(T[0][:, :], pair(t), ACT.Tanh, scale=0.5, bias=half_bias[:, c]).then_inc(s["gates_read"], 1)
                if t == 0:
                    e.wait_ge(s["wax_part"], 3 * j + 2)
                else:
                    e.wait_ge(multiplied, stream.number(name, at, i))
                e.activation(T[1][:, :], pair(2 + t), ACT.Tanh, scale=0.5, bias=half_bias[:, bass.ds(8 + 2 * j + t, 1)]).then_inc(s["gates_read"], 1)
                e.wait_ge(s["log_a"], 2 * j + t + 1)
                e.activation(T[2][:, :], T[0][:, :], ACT.Exp).then_inc(s["decay"], 1)
                e.activation(T[3][:, :], T[0][:, :], ACT.Tanh, scale=0.5).then_inc(s["decay"], 1)
                e.wait_ge(s["decay"], 4 * j + 2 * t + 2)
                e.activation(T[0][:, :], T[3][:, :], ACT.Sqrt, scale=-1.0).then_inc(s["root"], 1)
                e.wait_ge(s["out_full"], 2 * j + t + 1)
                e.activation(out_hi[:, t, :], T[0][:, :], ACT.Copy).then_inc(s["out_hi"], 1)
        s["gelu"] = sem("lru_gelu")

        def dve_in(e, o, j):
            for t in range(2):
                e.wait_ge(s["x_read"], 2 * j + t + 1)
                o(e.tensor_scalar(xc[:, t, :], xpad[:, t, 3:], col("od_conv3", 2 * j + t), col("od_conv_b", 2 * j + t), ALU.mult, ALU.add))
                for back in (1, 2, 3):
                    ins = e.scalar_tensor_tensor(xc[:, t, :], xpad[:, t, 3 - back:3 - back + S], col(f"od_conv{3 - back}", 2 * j + t), xc[:, t, :], ALU.mult, ALU.add)
                    if back < 3:
                        o(ins)
                ins.then_inc(s["conv"], 1)
                e.wait_ge(s["xc_hi"], 2 * j + t + 1)
                e.tensor_tensor(xc_lo[:, t, :], xc[:, t, :], f32(xc_hi[:, t, :]), ALU.subtract).then_inc(s["xc_ready"], 1)
            for t in range(2):
                e.wait_ge(s["gate_sq"], 2 * j + t + 1)
                o(e.tensor_scalar(T[t][:, :], T[t][:, :], GELU_A, 1.0, ALU.mult, ALU.add))
                e.tensor_tensor(T[t][:, :], T[t][:, :], G[:, t, :], ALU.mult).then_inc(s["gate_arg"], 1)
            for t in range(2):
                e.wait_ge(s["gate_tanh"], 2 * j + t + 1)
                e.scalar_tensor_tensor(G[:, t, :], T[t][:, :], 1.0, G[:, t, :], ALU.add, ALU.mult).then_inc(s["gelu"], 1)
            e.wait_ge(s["gelu"], 2 * j + 2)

        def dve_chain(e, o, j):
            for t in range(2):
                c = decay4[:, bass.ds(2 * j + t, 1)]
                e.wait_ge(s["gates_read"], 4 * j + 2 * t + 1)
                e.tensor_scalar(T[0][:, :], T[0][:, :], c, c, ALU.mult, ALU.add).then_inc(s["log_a"], 1)
                e.wait_ge(s["gates_read"], 4 * j + 2 * t + 2)
                o(e.scalar_tensor_tensor(T[1][:, :], T[1][:, :], 1.0, xc[:, t, :], ALU.add, ALU.mult))
                e.wait_ge(s["decay"], 4 * j + 2 * t + 1)
                o(e.scalar_tensor_tensor(T[1][:, :], T[2][:, :], 1.0, T[1][:, :], ALU.add, ALU.mult))
                e.wait_ge(s["root"], 2 * j + t + 1)
                o(e.scalar_tensor_tensor(T[1][:, :], T[0][:, :], 0.5, T[1][:, :], ALU.mult, ALU.mult))
                o(e.tensor_tensor_scan(T[3][:, :], T[2][:, :], T[1][:, :], 0.0, ALU.mult, ALU.add))
                e.scalar_tensor_tensor(T[0][:, :], T[3][:, :], 0.5, G[:, t, :], ALU.mult, ALU.mult).then_inc(s["out_full"], 1)
                e.wait_ge(s["out_hi"], 2 * j + t + 1)
                e.tensor_tensor(out_lo[:, t, :], T[0][:, :], f32(out_hi[:, t, :]), ALU.subtract).then_inc(s["out_ready"], 1)
                e.wait_ge(s["out_ready"], 2 * j + t + 3)

        def dve_out(e, j, name, at, i):
            for n in range(KT):
                if n % 4 == 3:
                    e.wait_ge(multiplied, stream.number(name, at + n // 4, i))
                else:
                    e.wait_ge(s["down_part"], 6 * j + 3 * (n // 4) + n % 4 + 1)
                e.tensor_tensor(Y[:, n, :], Y[:, n, :], pair(n % 4), ALU.add).then_inc(s["y_added"], 1)
            e.wait_ge(s["y_added"], 8 * j + 2 * KT)

        IN_STEPS, CHAIN_STEPS = 8, 8

        def sp(e):
            for name in (first, loop, tail):
                load_chunks(e, name)

        def pool(e):
            split_chunks(e, first, SLOTS)
            for name in (loop, tail):
                split_chunks(e, name)

        def pe(e):
            pe_in(e, 0, first, 0, ready=h_ready)
            pe_gates(e, 0, first, 4, 0, first_head=True)
            with e.Fori(0, LRU_HEADS - 1) as i:
                pe_in(e, i + 1, loop, i)
                pe_out(e, i, loop, 4, i)
                pe_gates(e, i + 1, loop, 6, i)
            pe_out(e, LRU_HEADS - 1, tail, 0, 0, alone=True)

        def act(e):
            for w, v in tmp_free:
                e.wait_ge(w, v)
            act_in(e, 0, first, 0)
            act_chain(e, 0, first, 4, 0)
            with e.Fori(0, LRU_HEADS - 1) as i:
                e.wait_ge(s["out_ready"], 2 * i + 4)
                act_in(e, i + 1, loop, i)
                act_chain(e, i + 1, loop, 6, i)

        def dve(e):
            o = dve_steps(e)
            for w, v in tmp_free:
                e.wait_ge(w, v)
            o(e.memset(Y[:, :, :], 0.0))
            o(e.memset(xpad[:, :, 0:3], 0.0))
            dve_in(e, o, 0)
            dve_chain(e, o, 0)
            with e.Fori(0, LRU_HEADS - 1) as i:
                o.enter(i, IN_STEPS + CHAIN_STEPS)
                dve_in(e, o, i + 1)
                dve_out(e, i, loop, 4, i)
                dve_chain(e, o, i + 1)
            o.leave(LRU_HEADS - 1)
            dve_out(e, LRU_HEADS - 1, tail, 0, 0)

        return dict(sp=sp, pool=pool, pe=pe, act=act, dve=dve, y_ready=(s["y_added"], KT * LRU_HEADS),
                    x_free=[(multiplied, stream.number(loop, 3, LRU_HEADS - 2))], sq_free=[(s["out_ready"], 2 * LRU_HEADS + 2)])

    def s5(h_ready, tmp_free):
        u, taps0, taps1, bn, cn, pw, E, aB0, aB1, Ca0, Ca1, turned0, turned1, near0, near1, pt, w, s0, s1, t, mag8 = carve(
            ("s5_u", [P, S5_TILES, S], F32), ("s5_taps0", [P, S], F32), ("s5_taps1", [P, S], F32),
            ("s5_bn", [P, STATE_TILES, 2, 32], F32), ("s5_cn", [P, STATE_TILES, 2, 32], F32), ("s5_pw", [P, 2, STATE_TILES, LC + 1], F32),
            ("s5_E", [P, STATE_TILES, 2, NC], F32), ("s5_aB0", [P, 2, LC, 32], F32), ("s5_aB1", [P, 2, LC, 32], F32),
            ("s5_Ca0", [P, 2, LC, 32], F32), ("s5_Ca1", [P, 2, LC, 32], F32), ("s5_turned0", [P, HALF], F32), ("s5_turned1", [P, HALF], F32),
            ("s5_near0", [P, 4, 64], F32), ("s5_near1", [P, 4, 64], F32), ("s5_pt", [P, 4, LC, 32], F32), ("s5_w", [P, 4, NC], F32),
            ("s5_s0", [P, 2, NC + 8], F32), ("s5_s1", [P, 2, NC + 8], F32), ("s5_t", [P, 2, S], F32), ("s5_mag8", [P, STATE_TILES], F32))
        taps2, taps3 = (nc.alloc_sbuf_tensor_at(f"s5_taps{n}", [P, S], F32, offset=y_at + (m * S5_TILES + S5_TILES - 1) * S * 4) for m, n in enumerate((2, 3)))
        taps, aB, Ca, turned, near, s = (taps0, taps1, taps2, taps3), (aB0, aB1), (Ca0, Ca1), (turned0, turned1), (near0, near1), (s0, s1)
        ys_hi = nc.alloc_sbuf_tensor_at("ys_hi", [P, S5_TILES, S], F32R, offset=y_at)
        ys_lo = nc.alloc_sbuf_tensor_at("ys_lo", [P, S5_TILES, S], F32R, offset=y_at + S5_TILES * S * 4)
        (u_read, maps_loaded, maps_ready, aB_ready, transposed, near_done, near_ready, turned_ready, v_done, v_used, s_ready, y_done, y_full,
         y_squared, y_arg, y_tanh, y_gelu, y_hi, ys_ready) = (sem(f"s5_{n}") for n in (
             "u_read", "maps_loaded", "maps_ready", "aB_ready", "transposed", "near_done", "near_ready", "turned_ready", "v_done", "v_used",
             "s_ready", "y_done", "y_full", "y_squared", "y_arg", "y_tanh", "y_gelu", "y_hi", "ys_ready"))
        taps_loaded = [sem(f"s5_taps{n}_loaded") for n in range(4)]
        credits.extend([(near_done, 2), (near_ready, 2), (turned_ready, 2), (v_done, 2), (v_used, 2), (y_done, 4), (y_full, 1)])
        U = "s5_u"
        turn_bank, near_bank, v_bank = (0, 4), (1, 3), (2, 5)

        def chunked(ap):
            return ap.rearrange("p (k j) -> p j k", j=LC)

        def each_tile(c, last, step, ahead):
            for st in range(4):
                if st + ahead < 4:
                    step(c, st + ahead)
                elif not last:
                    step(c + 1, st + ahead - 4)

        def sp(e):
            load_chunks(e, U)
            for w_, v in tmp_free:
                e.wait_ge(w_, v)
            e.dma_start(bn[:, :, :, :], A["s5_b"]).then_inc(maps_loaded, 16)
            e.dma_start(cn[:, :, :, :], A["s5_c"]).then_inc(maps_loaded, 16)
            e.wait_ge(maps_ready, 1)
            with e.Fori(0, S5_TILES) as c:
                e.wait_ge(u_read, c + 1)
                for st in range(4):
                    e.wait_ge(y_done, 4 * c + st + 1)
                    for d in range(4):
                        e.dma_start(taps[st][32 * d:32 * d + 32, d:], u[32 * st:32 * st + 32, bass.ds(c, 1), 0:S - d].rearrange("p o n -> p (o n)")).then_inc(taps_loaded[st], 16)

        def pool(e):
            o = steps_of(e, "pool")
            split_chunks(e, U, SLOTS)
            e.wait_ge(maps_ready, 1)

            def powers_of_b(c, st):
                n, b = 4 * c + st, st % 2
                e.wait_ge(near_done, n + 1)
                pr, pi = (pw[:, x, bass.ds(n, 1), 0:LC].rearrange("p o (d u) -> p (o d) u", u=1).broadcast_to([P, LC, 32]) for x in range(2))
                br, bi = (bn[:, bass.ds(n, 1), x, :].broadcast_to([P, LC, 32]) for x in range(2))
                o.step(e.tensor_tensor(pt[:, 0, :, :], pr, br, ALU.mult))
                a = o.step(e.tensor_tensor(pt[:, 1, :, :], pi, bi, ALU.mult))
                o.step(e.tensor_tensor(pt[:, 2, :, :], pr, bi, ALU.mult))
                d = o.step(e.tensor_tensor(pt[:, 3, :, :], pi, br, ALU.mult))
                o.after(a)
                o.step(e.tensor_tensor(aB[b][:, 0, :, :], pt[:, 0, :, :], pt[:, 1, :, :], ALU.subtract))
                o.after(d)
                e.tensor_tensor(aB[b][:, 1, :, :], pt[:, 2, :, :], pt[:, 3, :, :], ALU.add).then_inc(aB_ready, 1)
                e.wait_ge(aB_ready, n + 1)

            with e.Fori(0, S5_TILES) as c:
                o.enter(c, 4 * 5)
                for st in range(4):
                    powers_of_b(c, st)
            o.leave(S5_TILES)

        def pe(e):
            for c in range(S5_TILES):
                e.wait_ge(split, stream.number(U, c))
                columns(e, stream.slot(U, c), c, H_hi, H_lo, ready=h_ready if c == 0 else None).then_inc(multiplied, 1)
            e.wait_ge(u_read, S5_TILES)
            e.wait_ge(maps_ready, 1)

            def maps(c, st):
                n, b = 4 * c + st, st % 2
                e.wait_ge(aB_ready, n + 1)
                e.wait_ge(turned_ready, n + 1)
                for x in range(2):
                    for h in range(2):
                        ins = e.transpose(ps[:, turn_bank[b], (2 * x + h) * P:(2 * x + h + 1) * P],
                                          aB[b][:, x, 4 * h:4 * h + 4, :].rearrange("p d n -> p (d n)"), ident[:, :])
                ins.then_inc(transposed, 1)
                e.wait_ge(near_ready, n + 1)
                for h in range(2):
                    for x in range(2):
                        ins = e.matmul(ps[:, near_bank[b], 32 * h:32 * h + 32], aB[b][:, x, 4 * h:4 * h + 4, :].rearrange("p d n -> p (d n)"),
                                       cn[:, bass.ds(n, 1), x, :].rearrange("p o n -> p (o n)"), start=x == 0, stop=x == 1)
                ins.then_inc(near_done, 1)

            def inputs(c, st):
                n, b = 4 * c + st, st % 2
                e.wait_ge(turned_ready, n + 3)
                e.wait_ge(taps_loaded[st], 64 * c + 64)
                e.wait_ge(v_used, n + 1)
                for x in range(2):
                    for h in range(2):
                        ins = e.matmul(ps[:, v_bank[b], x * NC:(x + 1) * NC], turned[b][:, (2 * x + h) * P:(2 * x + h + 1) * P],
                                       chunked(taps[st][:, :])[:, LC - 1 - 4 * h, :], start=h == 0, stop=h == 1)
                ins.then_inc(v_done, 1)

            def outputs(c, st):
                n, b = 4 * c + st, st % 2
                e.wait_ge(s_ready, n + 1)
                if st == 0:
                    e.wait_ge(y_full, c + 1)
                for j in range(LC):
                    out = ps[32 * st:32 * st + 32, 6 + j // 4, (j % 4) * NC:(j % 4 + 1) * NC]
                    parts = [(Ca[b][:, x, j, :], s[b][:, x, 0:NC]) for x in range(2)]
                    parts.append((near[b][:, min(j, 3), 0:32], chunked(taps[st][:, :])[:, j, :]))
                    if j >= 4:
                        parts.append((near[b][:, j - 4, 32:64], chunked(taps[st][:, :])[:, j - 4, :]))
                    for x, (l, r) in enumerate(parts):
                        ins = e.matmul(out, l, r, start=j % 4 == 0 and x == 0, stop=j % 4 == 3 and x == len(parts) - 1)
                ins.then_inc(y_done, 1)

            def tile_of_channels(c, last):
                for st in range(4):
                    for step, ahead in ((maps, 2), (inputs, 1)):
                        if st + ahead < 4:
                            step(c, st + ahead)
                        elif not last:
                            step(c + 1, st + ahead - 4)
                    outputs(c, st)

            maps(0, 0)
            maps(0, 1)
            inputs(0, 0)
            with e.Fori(0, S5_TILES - 1) as c:
                tile_of_channels(c, False)
            tile_of_channels(S5_TILES - 1, True)

        def act(e):
            for w_, v in tmp_free:
                e.wait_ge(w_, v)
            for c in range(S5_TILES):
                e.wait_ge(multiplied, stream.number(U, c))
                e.activation(u[:, c, :], pair(c), ACT.Copy).then_inc(u_read, 1)

            def maps(c, st):
                n, b = 4 * c + st, st % 2
                e.wait_ge(transposed, n + 1)
                e.wait_ge(v_done, n + 1)
                e.activation(turned[b][:, :], ps[:, turn_bank[b], :], ACT.Copy).then_inc(turned_ready, 1)

            def tile_of_channels(c, last):
                each_tile(c, last, maps, 2)
                e.wait_ge(y_full, c + 2)
                e.activation(t[:, 1, :], t[:, 0, :], ACT.Square).then_inc(y_squared, 1)
                e.wait_ge(y_arg, c + 1)
                e.activation(t[:, 1, :], t[:, 1, :], ACT.Tanh, scale=GELU_C).then_inc(y_tanh, 1)
                e.wait_ge(y_gelu, c + 1)
                e.activation(tile(ys_hi, c), t[:, 1, :], ACT.Copy, scale=0.5).then_inc(y_hi, 1)

            maps(0, 0)
            maps(0, 1)
            with e.Fori(0, S5_TILES - 1) as c:
                tile_of_channels(c, False)
            tile_of_channels(S5_TILES - 1, True)

        def dve(e):
            o = dve_steps(e)
            for w_, v in tmp_free:
                e.wait_ge(w_, v)
            e.wait_ge(maps_loaded, 32)

            def over(ap, n):
                return ap.rearrange("p (s o) -> p s o", o=1).broadcast_to([P, STATE_TILES, n])

            x = [t[:, 0, k * 512:(k + 1) * 512].rearrange("p (s n) -> p s n", n=32) for k in range(2)] + \
                [t[:, 1, k * 512:(k + 1) * 512].rearrange("p (s n) -> p s n", n=32) for k in range(2)]
            for k, (qc, part) in enumerate(((q_re, 0), (q_im, 1), (q_re, 1), (q_im, 0))):
                o.step(e.tensor_tensor(x[k], over(qc[:, :], 32), bn[:, :, part, :], ALU.mult))
            o(e.tensor_scalar(cn[:, :, 1, :], cn[:, :, 1, :], -1.0, None, ALU.mult))
            o.step(e.tensor_tensor(bn[:, :, 0, :], x[0], x[1], ALU.subtract))
            o(e.tensor_tensor(bn[:, :, 1, :], x[2], x[3], ALU.add))
            o.step(e.memset(pw[:, 0, :, 0:1], 1.0))
            o.step(e.memset(pw[:, 1, :, 0:1], 0.0))
            power = [[pw[:, part, :, k:k + 1].rearrange("p s o -> p (s o)") for k in range(LC + 1)] for part in range(2)]
            o.step(e.tensor_tensor(power[0][1], mag[:, :], rot_re[:, 0, :], ALU.mult))
            o(e.tensor_tensor(power[1][1], mag[:, :], rot_im[:, 0, :], ALU.mult))
            y = [w[:, k, 0:STATE_TILES] for k in range(4)]
            for k in range(2, LC + 1):
                for z, (m, n) in enumerate(((0, 0), (1, 1), (0, 1), (1, 0))):
                    a = o.step(e.tensor_tensor(y[z], power[m][1], power[n][k - 1], ALU.mult))
                o.after(a)
                o.step(e.tensor_tensor(power[0][k], y[0], y[1], ALU.subtract))
                o(e.tensor_tensor(power[1][k], y[2], y[3], ALU.add))
            o(e.tensor_tensor(mag8[:, :], mag[:, :], mag[:, :], ALU.mult))
            o(e.tensor_tensor(mag8[:, :], mag8[:, :], mag8[:, :], ALU.mult))
            o(e.tensor_tensor(mag8[:, :], mag8[:, :], mag8[:, :], ALU.mult))
            o.step(e.memset(E[:, :, 0, 0:1], 1.0))
            o(e.memset(E[:, :, 1, 0:1], 0.0))
            for k in range(POWERS - 3):
                n = 1 << k
                re, im, re_up, im_up = (E[:, :, part, at:at + n] for at in (0, n) for part in range(2))
                a, b = (t[:, z, 0:STATE_TILES * n].rearrange("p (s n) -> p s n", n=n) for z in range(2))
                cr, ci = over(rot_re[:, 3 + k, :], n), over(rot_im[:, 3 + k, :], n)
                o.step(e.tensor_tensor(a, im, ci, ALU.mult))
                o.step(e.tensor_tensor(b, re, ci, ALU.mult))
                o.step(e.tensor_tensor(re_up, re, cr, ALU.mult))
                o(e.tensor_tensor(im_up, im, cr, ALU.mult))
                o.step(e.tensor_tensor(re_up, re_up, a, ALU.subtract))
                o(e.tensor_tensor(im_up, im_up, b, ALU.add))
            for b in range(2):
                o.step(e.memset(s[b][:, :, 0:1], 0.0))
            for st in range(3):
                o.step(e.memset(taps[st][:, 0:4], 0.0))
            e.memset(taps[3][:, 0:4], 0.0).then_inc(maps_ready, 1)
            e.wait_ge(maps_ready, 1)

            def states(c, st):
                n, b = 4 * c + st, st % 2
                e.wait_ge(y_done, n + 3)
                pr, pi = (pw[:, z, bass.ds(n, 1), 1:LC + 1].rearrange("p o (d u) -> p (o d) u", u=1).broadcast_to([P, LC, 32]) for z in range(2))
                cr, ci = (cn[:, bass.ds(n, 1), z, :].broadcast_to([P, LC, 32]) for z in range(2))
                x = [t[:, 1, k * 256:(k + 1) * 256].rearrange("p (d n) -> p d n", n=32) for k in range(4)]
                o.step(e.tensor_tensor(x[0], cr, pr, ALU.mult))
                a = o.step(e.tensor_tensor(x[1], ci, pi, ALU.mult))
                o.step(e.tensor_tensor(x[2], ci, pr, ALU.mult))
                d = o.step(e.tensor_tensor(x[3], cr, pi, ALU.mult))
                o.after(a)
                o.step(e.tensor_tensor(Ca[b][:, 0, :, :], x[0], x[1], ALU.add))
                o.after(d)
                o.step(e.tensor_tensor(Ca[b][:, 1, :, :], x[2], x[3], ALU.subtract))
                e.wait_ge(near_done, n + 3)
                e.tensor_tensor(near[b][:, :, :], ps[:, near_bank[b], 0:64].rearrange("p (o n) -> p o n", o=1).broadcast_to([P, 4, 64]),
                                up_to[:, :].rearrange("p (m o) -> p m o", o=1).broadcast_to([P, 4, 64]), ALU.mult).then_inc(near_ready, 1)
                e.wait_ge(v_done, n + 3)
                vr, vi = ps[:, v_bank[b], 0:NC], ps[:, v_bank[b], NC:2 * NC]
                Er, Ei = (E[:, bass.ds(n, 1), z, :].rearrange("p o n -> p (o n)") for z in range(2))
                w0, w1, w2, w3 = (w[:, z, :] for z in range(4))
                o.step(e.tensor_tensor(w0, Er, vr, ALU.mult))
                a = o.step(e.tensor_tensor(w1, Ei, vi, ALU.mult))
                o.step(e.tensor_tensor(w2, Er, vi, ALU.mult))
                e.tensor_tensor(w3, Ei, vr, ALU.mult).then_inc(v_used, 1)
                o.after(a)
                a = o.step(e.tensor_tensor(w0, w0, w1, ALU.add))
                e.wait_ge(v_used, n + 3)
                d = o.step(e.tensor_tensor(w2, w2, w3, ALU.subtract))
                decay = mag8[:, bass.ds(n, 1)].broadcast_to([P, NC])
                o.after(a)
                o.step(e.tensor_tensor_scan(w1, decay, w0, 0.0, ALU.mult, ALU.add))
                o.after(d)
                d = o.step(e.tensor_tensor_scan(w3, decay, w2, 0.0, ALU.mult, ALU.add))
                o.after(d)
                a = o.step(e.tensor_tensor(w2, Ei, w3, ALU.mult))
                o.step(e.tensor_tensor(w0, Er, w1, ALU.mult))
                o.after(a)
                o.step(e.tensor_tensor(w3, Er, w3, ALU.mult))
                d = o.n - 1
                o.after(d)
                a = o.step(e.tensor_tensor(w1, Ei, w1, ALU.mult))
                o.step(e.tensor_tensor(s[b][:, 0, 1:NC + 1], w0, w2, ALU.subtract))
                o.after(a)
                e.tensor_tensor(s[b][:, 1, 1:NC + 1], w3, w1, ALU.add).then_inc(s_ready, 1)
                e.wait_ge(s_ready, n + 1)

            def gelu(c):
                e.wait_ge(y_done, 4 * c + 8)
                e.scalar_tensor_tensor(chunked(t[:, 0, :]), chunked(tile(u, c)), col("d_skip", c), pair(3).rearrange("p (j k) -> p j k", j=LC),
                                       ALU.mult, ALU.add).then_inc(y_full, 1)
                e.wait_ge(y_squared, c + 1)
                o(e.tensor_scalar(t[:, 1, :], t[:, 1, :], GELU_A, 1.0, ALU.mult, ALU.add))
                e.tensor_tensor(t[:, 1, :], t[:, 1, :], t[:, 0, :], ALU.mult).then_inc(y_arg, 1)
                e.wait_ge(y_tanh, c + 1)
                e.scalar_tensor_tensor(t[:, 1, :], t[:, 1, :], 1.0, t[:, 0, :], ALU.add, ALU.mult).then_inc(y_gelu, 1)
                e.wait_ge(y_hi, c + 1)
                e.scalar_tensor_tensor(tile(ys_lo, c), t[:, 1, :], 0.5, f32(tile(ys_hi, c)), ALU.mult, ALU.subtract).then_inc(ys_ready, 1)
                e.wait_ge(ys_ready, c + 1)

            states(0, 0)
            with e.Fori(0, S5_TILES - 1) as c:
                o.enter(c, 4 * 18 + 1)
                each_tile(c, False, states, 1)
                gelu(c)
            o.leave(S5_TILES - 1)
            each_tile(S5_TILES - 1, True, states, 1)
            gelu(S5_TILES - 1)

        done = [(ys_ready, S5_TILES)]
        return dict(sp=sp, pool=pool, pe=pe, act=act, dve=dve, ys=(ys_hi, ys_lo), ready=done, tmp_free=done)

    def glu(ys, ready):
        ys_hi, ys_lo = ys
        yo_hi, yo_lo, th, tz, y0, y1 = carve(
            ("yo_hi", [P, 4, S], F32R), ("yo_lo", [P, 4, S], F32R), ("glu_th", [P, 4, S], F32), ("glu_tz", [P, 4, S], F32),
            ("glu_y0", [P, S], F32), ("glu_y1", [P, S], F32))
        y = (y0, y1)
        part, th_done, gated, tz_done, full, hi_done, yo_ready = (
            sem(f"glu_{n}") for n in ("part", "th", "gated", "tz", "full", "hi", "yo_ready"))
        G = "glu"

        def sp(e):
            load_chunks(e, G)

        def pool(e):
            split_chunks(e, G)

        def pe(e):
            for n in range(4):
                e.wait_ge(split, stream.number(G, n))
                if n == 3:
                    for w, v in ready:
                        e.wait_ge(w, v)
                columns(e, stream.slot(G, n), n, H_hi, H_lo).then_inc(multiplied, 1)
            for n in range(4):
                e.wait_ge(split, stream.number(G, 4 + n // 2))
                e.wait_ge(gated, n + 1)
                columns(e, stream.slot(G, 4 + n // 2), n, ys_hi, ys_lo, kt=4, at=(n % 2) * P, step=256).then_inc(multiplied if n % 2 else part, 1)

        def act(e):
            for w, v in ready:
                e.wait_ge(w, v)
            for n in range(4):
                e.wait_ge(multiplied, stream.number(G, n))
                e.activation(tz[:, n, :], pair(n), ACT.Tanh, scale=0.5).then_inc(tz_done, 1)
            for n in range(4):
                if n % 2:
                    e.wait_ge(multiplied, stream.number(G, 4 + n // 2))
                else:
                    e.wait_ge(part, n // 2 + 1)
                e.activation(th[:, n, :], pair(n), ACT.Tanh, scale=0.5, bias=half_bias[:, 16 + n:17 + n]).then_inc(th_done, 1)
                e.wait_ge(full, n + 1)
                e.activation(yo_hi[:, n, :], tz[:, n, :], ACT.Copy, scale=0.25).then_inc(hi_done, 1)

        def dve(e):
            o = dve_steps(e)
            for n in range(4):
                e.wait_ge(tz_done, n + 1)
                e.scalar_tensor_tensor(tz[:, n, :], tz[:, n, :], 1.0, pair(n), ALU.add, ALU.mult).then_inc(gated, 1)
            for n in range(4):
                if n >= 2:
                    e.wait_ge(gated, 4 + n - 1)
                o(e.tensor_tensor(y[n % 2][:, :], f32(ys_hi[:, n, :]), f32(ys_lo[:, n, :]), ALU.add))
                e.wait_ge(th_done, n + 1)
                e.scalar_tensor_tensor(th[:, n, :], th[:, n, :], 1.0, y[n % 2][:, :], ALU.add, ALU.mult).then_inc(gated, 1)
                e.wait_ge(gated, 4 + n + 1)
                e.tensor_tensor(tz[:, n, :], tz[:, n, :], th[:, n, :], ALU.mult).then_inc(full, 1)
                e.wait_ge(hi_done, n + 1)
                e.scalar_tensor_tensor(yo_lo[:, n, :], tz[:, n, :], 0.25, f32(yo_hi[:, n, :]), ALU.mult, ALU.subtract).then_inc(yo_ready, 1)

        return dict(sp=sp, pool=pool, pe=pe, act=act, dve=dve, yo=(yo_hi, yo_lo), ready=[(yo_ready, 4)], banks_free=[(th_done, 4)])

    def s5_out(yo, ready, banks_free):
        yo_hi, yo_lo = yo
        G0, G1, f_abs, f_min, i_row, sums, neg_max, neg_m, ones_rows = carve(
            ("s5_G0", [P, S], F32), ("s5_G1", [P, S], F32),
            *[(f"ml_{n}", [4, S], F32) for n in ("f_abs", "f_min", "i_row", "sums", "neg_max", "neg_m", "ones_rows")], keep=2 * 4 * S * 4)
        G = (G0, G1)
        g_read, parted, stored = (sem(f"s5_out_{n}") for n in ("g_read", "parted", "stored"))
        rows_ready, rows_stored, turned, cols_ready = (
            sem(f"ml_{n}") for n in ("rows_ready", "rows_stored", "turned", "cols_ready"))
        credits.extend([(parted, 2), (g_read, 2), (stored, 32)])
        M, O = "ml_pre", "s5_out"

        def sp(e):
            load_chunks(e, M)
            load_chunks(e, O)
            e.wait_ge(rows_ready, 1)
            e.dma_start(rows_dram[8:12, :], neg_max[:, :]).then_inc(rows_stored, 16)
            e.dma_start(rows_dram[12:16, :], neg_m[:, :]).then_inc(rows_stored, 16)

        def pool(e):
            split_chunks(e, M)
            split_chunks(e, O)

        def pe(e):
            for w, v in banks_free:
                e.wait_ge(w, v)
            for c in range(2):
                e.wait_ge(split, stream.number(M, c))
                columns(e, stream.slot(M, c), 2 + c, H_hi, H_lo).then_inc(multiplied, 1)
            for w, v in ready:
                e.wait_ge(w, v)
            with e.Fori(0, 4) as i:
                e.wait_ge(split, stream.number(O, 0, i))
                for t in range(2):
                    e.wait_ge(parted, 2 * i + t + 1)
                    ins = columns(e, stream.slot(O, 0), t, yo_hi, yo_lo, kt=4, at=t * P, step=256)
                ins.then_inc(multiplied, 1)
                for t in range(2):
                    e.wait_ge(split, stream.number(O, 1 + t, i))
                    e.wait_ge(rows_ready, 1)
                    e.wait_ge(g_read, 2 * i + t + 1)
                    columns(e, stream.slot(O, 1 + t), 2 + t, H_hi, H_lo).then_inc(multiplied, 1)
            e.wait_ge(parted, 10)
            for k in range(KT):
                ins = e.transpose(ps[:, 0, k * 4:(k + 1) * 4], i_row[:, k * P:(k + 1) * P], ident[0:4, 0:4])
            ins.then_inc(turned, 1)

        def act(e):
            a = steps_of(e, "act")
            bias = par[0:4, COLUMN["row_bias"] + 2:COLUMN["row_bias"] + 3]
            for w, v in ready:
                e.wait_ge(w, v)
            e.wait_ge(multiplied, stream.number(M, 1))
            a(e.activation(f_abs[:, :], pair(3)[0:4, :], ACT.Abs, bias=bias))
            a(e.activation(f_abs[:, :], f_abs[:, :], ACT.Exp, scale=-1.0))
            a.step(e.activation(f_abs[:, :], f_abs[:, :], ACT.Ln, bias=one_col[0:4, :]))
            with e.Fori(0, 4) as i:
                for t in range(2):
                    e.wait_ge(multiplied, stream.number(O, 1 + t, i))
                    if t == 0:
                        e.wait_ge(stored, 32 * i + 32)
                    e.activation(G[t][:, :], pair(2 + t), ACT.Tanh, scale=0.5).then_inc(g_read, 1)
                for t in range(2):
                    e.wait_ge(parted, 2 * i + t + 3)
                    e.dma_start(part_dram[bass.ds(2 * i + t, 1), :, :].rearrange("o p n -> p (o n)"), G[t][:, :]).then_inc(stored, 16)
            e.wait_ge(turned, 1)
            e.activation(gate_cols[:, :, :].rearrange("p k h -> p (k h)"), ps[:, 0, 0:4 * KT], ACT.Copy).then_inc(cols_ready, 1)

        def dve(e):
            o = dve_steps(e)
            col_i, col_f = (par[0:4, COLUMN["row_bias"] + n:COLUMN["row_bias"] + n + 1] for n in (1, 2))
            for w, v in ready:
                e.wait_ge(w, v)
            e.wait_ge(multiplied, stream.number(M, 0))
            o(e.memset(ones_rows[:, :], 1.0))
            o(e.tensor_scalar(i_row[:, :], pair(2)[0:4, :], col_i, None, ALU.add))
            e.wait_ge(sem("act_order"), PRELUDE_ACT + 4)
            o(e.tensor_scalar(f_min[:, :], pair(3)[0:4, :], col_f, 0.0, ALU.add, ALU.min))
            e.wait_ge(sem("act_order"), PRELUDE_ACT + 6)
            o(e.tensor_tensor(f_min[:, :], f_min[:, :], f_abs[:, :], ALU.subtract))
            o(e.tensor_tensor_scan(sums[:, :], ones_rows[:, :], f_min[:, :], 0.0, ALU.mult, ALU.add))
            o(e.tensor_tensor(i_row[:, :], i_row[:, :], sums[:, :], ALU.subtract))
            o(e.tensor_tensor_scan(f_abs[:, :], ones_rows[:, :], i_row[:, :], FILL, ALU.mult, ALU.max))
            o(e.tensor_scalar(neg_max[:, :], f_abs[:, :], -1.0, None, ALU.mult))
            e.scalar_tensor_tensor(neg_m[:, :], sums[:, :], -1.0, f_abs[:, :], ALU.mult, ALU.subtract).then_inc(rows_ready, 1)
            with e.Fori(0, 4) as i:
                for t in range(2):
                    e.wait_ge(g_read, 2 * i + t + 3)
                    e.scalar_tensor_tensor(G[t][:, :], G[t][:, :], 1.0, pair(t), ALU.add, ALU.mult).then_inc(parted, 1)

        return dict(sp=sp, pool=pool, pe=pe, act=act, dve=dve, part_stored=(stored, 160), rows_stored=(rows_stored, 32),
                    cols_ready=(cols_ready, 1), tmp_free=[(cols_ready, 1), (rows_stored, 32), (stored, 160)])

    def mlstm(h_ready, tmp_free, rows_stored):
        two_tiles, X = 2 * S * 4, 3
        (xpad,) = carve(("ml_xpad", [P, 2, X + S], F32))
        u_at = two_tiles + 32
        u_hi, u_lo, c_hi, c_lo, v_hi, v_lo, acc, so, negm_b, st_hi, st_lo, capped = carve(
            ("ml_u_hi", [P, 2, S], F32R), ("ml_u_lo", [P, 2, S], F32R), ("ml_c_hi", [P, 2, S], F32R),
            ("ml_c_lo", [P, 2, S], F32R), ("ml_v_hi", [P, KT, 256], F32R), ("ml_v_lo", [P, KT, 256], F32R), ("ml_acc", [P, 2, S], F32),
            ("ml_so", [P, 2, S], F32), ("ml_negm_b", [P, S], F32), ("ml_st_hi", [P, 2, HALF], F32R), ("ml_st_lo", [P, 2, HALF], F32R),
            ("ml_capped", [P, P], F32), keep=u_at)
        E, st, em = carve(("ml_E", [P, HALF], F32), ("ml_st", [P, HALF], F32), ("ml_em", [P, S], F32))
        (tz,) = carve(("ml_tz", [P, 2, S], F32))
        q, k_ = carve(("ml_q", [P, 2, S], F32), ("ml_k", [P, 2, S], F32), keep=u_at)
        out_hi, out_lo = carve(("ml_out_hi", [P, 2, S], F32R), ("ml_out_lo", [P, 2, S], F32R), keep=u_at)
        (c_full,) = carve(("ml_c_full", [P, 2, S], F32), keep=u_at + 5 * two_tiles)
        sq, rstd = so, negm_b
        (tc,) = carve(("ml_tc", [P, 2, S], F32), keep=u_at + 8 * two_tiles + S * 4)
        names = ("x_read", "u_hi", "u_ready", "conv", "c_tanh", "c_full", "c_hi", "c_ready", "o_read", "v_part", "v_hi", "v_ready",
                 "qk_part", "qk_read", "neg_loaded", "em_loaded", "em_ready", "capped", "E_ready", "scored", "st_full", "st_hi", "st_ready", "num_done",
                 "h_read", "gated", "squared", "summed", "rooted", "tz", "f_full", "out_hi", "out_ready", "out_part", "y_added")
        s = {n: sem(f"mlstm_{n}") for n in names}
        credits.extend([(s["y_added"], KT), (s["st_full"], 1)])
        N = "ml"
        pieces = [(hf, k, max(0, k * P - hf * HALF)) for hf in range(2) for k in range(4 * hf + 4)]
        M = len(pieces)
        diagonal = [m for m, (hf, k, off) in enumerate(pieces) if k * P >= hf * HALF]
        num_bank, den_bank = (2, 5), (4, 7)

        def sp(e):
            load_chunks(e, N)

        def pool(e):
            split_chunks(e, N)

        def pe(e):
            for w, v in tmp_free:
                e.wait_ge(w, v)

            def scores(j, m):
                hf, k, off = pieces[m]
                if m == 0:
                    e.wait_ge(s["qk_read"], 4 * j + 4)
                elif m >= 2:
                    e.wait_ge(s["st_full"], M * j + m)
                for d in range(2):
                    ins = e.matmul(ps[:, m % 2, 0:HALF - off], k_[:, d, k * P:(k + 1) * P], q[:, d, hf * HALF + off:(hf + 1) * HALF],
                                   start=d == 0, stop=d == 1)
                ins.then_inc(s["scored"], 1)

            def values(j, m):
                hf, k, off = pieces[m]
                first, last = k == 0, k == 4 * hf + 3
                e.wait_ge(s["st_ready"], M * j + m + 1)
                hi, lo = st_hi[:, m % 2, 0:HALF - off], st_lo[:, m % 2, 0:HALF - off]
                for d in range(2):
                    product(e, ps[:, num_bank[hf] + d, off:], v_hi[:, k, d * P:(d + 1) * P], v_lo[:, k, d * P:(d + 1) * P], hi, lo, first, last)
                e.matmul(ps[:, den_bank[hf], off:], ones_r[:, :], hi, start=first, stop=False)
                e.matmul(ps[:, den_bank[hf], off:], ones_r[:, :], lo, start=False, stop=last).then_inc(s["num_done"], 1)

            def sums(j, hf):
                e.wait_ge(s["squared"], 2 * j + hf + 1)
                for d in range(2):
                    ins = e.matmul(ps[:, 4 + hf, :], ones[:, :], sq[:, d, hf * HALF:(hf + 1) * HALF], start=d == 0, stop=d == 1)
                ins.then_inc(s["summed"], 1)

            with e.Fori(0, MLSTM_HEADS) as j:
                for c in range(4):
                    e.wait_ge(split, stream.number(N, c, j))
                    e.wait_ge(s["y_added"], 8 * j + 5 + c)
                    columns(e, stream.slot(N, c), c, H_hi, H_lo).then_inc(multiplied, 1)
                sl = stream.slot(N, 4)
                e.wait_ge(split, stream.number(N, 4, j))
                e.wait_ge(s["u_ready"], 2 * j + 2)
                for m in range(KT):
                    for t in range(2):
                        ins = product(e, ps[:, m // 2, (m % 2) * 256:(m % 2 + 1) * 256], u_hi[:, t, m * P:(m + 1) * P], u_lo[:, t, m * P:(m + 1) * P],
                                      w_hi[sl][:, t * 256:(t + 1) * 256], w_lo[sl][:, t * 256:(t + 1) * 256], t == 0, t == 1)
                    if m == 3:
                        ins.then_inc(s["v_part"], 1)
                ins.then_inc(multiplied, 1)
                sl = stream.slot(N, 5)
                e.wait_ge(split, stream.number(N, 5, j))
                e.wait_ge(s["c_ready"], 2 * j + 2)
                for n in range(4):
                    if n < 2:
                        e.wait_ge(s["o_read"], 2 * j + n + 1)
                    else:
                        e.wait_ge(s["v_ready"], 2 * j + n - 1)
                    columns(e, sl, (2, 3, 0, 1)[n], c_hi, c_lo, kt=2, at=HALF * (n // 2) + (n % 2) * P, step=256).then_inc(multiplied if n == 3 else s["qk_part"], 1)
                scores(j, 0)
                scores(j, 1)
                for m in range(M):
                    values(j, m)
                    if m + 2 < M:
                        scores(j, m + 2)
                sums(j, 0)
                for t in range(2):
                    e.wait_ge(split, stream.number(N, 6 + t, j))
                    if t == 0:
                        e.wait_ge(s["st_full"], M * j + M + 1)
                    else:
                        e.wait_ge(s["h_read"], 4 * j + 2)
                    columns(e, stream.slot(N, 6 + t), t, H_hi, H_lo, part=(0, 6))
                    if t == 0:
                        sums(j, 1)
                    columns(e, stream.slot(N, 6 + t), t, H_hi, H_lo, part=(6, KT)).then_inc(multiplied, 1)
                for c in range(2):
                    sl = stream.slot(N, 8 + c)
                    e.wait_ge(split, stream.number(N, 8 + c, j))
                    if c == 0:
                        e.wait_ge(s["out_ready"], 2 * j + 1)
                        for n in (0, 2, 3):
                            columns(e, sl, n, out_hi, out_lo, kt=2, at=n * P, step=HALF, part=(0, 1))
                    e.wait_ge(s["out_ready"], 2 * j + 2)
                    for n in range(4):
                        if c == 1:
                            e.wait_ge(s["y_added"], 8 * j + n + 1 + KT)
                        columns(e, sl, n, out_hi, out_lo, kt=2, at=n * P, step=HALF, part=None if c == 1 or n == 1 else (1, 2)).then_inc(multiplied if n == 3 else s["out_part"], 1)

        def act(e):
            for w, v in tmp_free + [rows_stored]:
                e.wait_ge(w, v)
            with e.Fori(0, MLSTM_HEADS) as j:
                e.wait_ge(s["y_added"], 8 * j + 8)
                e.dma_start(negm_b[:, :], rows_dram[bass.ds(8 + j, 1), :].broadcast_to([P, S])).then_inc(s["neg_loaded"], 16)
                for t in range(2):
                    e.wait_ge(multiplied, stream.number(N, t, j))
                    e.activation(xpad[:, t, X:], pair(t), ACT.Copy).then_inc(s["x_read"], 1)
                    e.activation(u_hi[:, t, :], pair(t), ACT.Copy).then_inc(s["u_hi"], 1)
                for t in range(2):
                    e.wait_ge(s["conv"], 2 * j + t + 1)
                    e.activation(tc[:, t, :], acc[:, t, :], ACT.Tanh, scale=0.5).then_inc(s["c_tanh"], 1)
                for t in range(2):
                    e.wait_ge(s["c_full"], 2 * j + t + 1)
                    e.activation(c_hi[:, t, :], acc[:, t, :], ACT.Copy, scale=0.5).then_inc(s["c_hi"], 1)
                e.wait_ge(s["u_ready"], 2 * j + 2)
                e.dma_start(em[:, :], rows_dram[bass.ds(12 + j, 1), :].broadcast_to([P, S])).then_inc(s["em_loaded"], 16)
                for t in range(2):
                    e.wait_ge(multiplied, stream.number(N, 2 + t, j))
                    e.activation(so[:, t, :], pair(2 + t), ACT.Tanh, scale=0.5).then_inc(s["o_read"], 1)
                e.wait_ge(s["em_loaded"], 16 * j + 16)
                e.activation(em[:, :], em[:, :], ACT.Exp).then_inc(s["em_ready"], 1)
                for t in range(2):
                    e.wait_ge(*((s["v_part"], j + 1) if t == 0 else (multiplied, stream.number(N, 4, j))))
                    e.activation(v_hi[:, 4 * t:4 * t + 4, :].rearrange("p k n -> p (k n)"), pair(t), ACT.Copy).then_inc(s["v_hi"], 1)
                for n in range(4):
                    e.wait_ge(*((multiplied, stream.number(N, 5, j)) if n == 3 else (s["qk_part"], 3 * j + n + 1)))
                    if n < 2:
                        e.activation(q[:, n, :], pair(2 + n), ACT.Copy, scale=256 ** -0.5).then_inc(s["qk_read"], 1)
                    else:
                        e.activation(k_[:, n - 2, :], pair(n - 2), ACT.Copy).then_inc(s["qk_read"], 1)
                e.wait_ge(s["neg_loaded"], 16 * j + 16)

                def weights(m):
                    hf, k, off = pieces[m]
                    t0, g = hf * HALF + off, gate_cols[:, k, bass.ds(j, 1)]
                    at = P if m in diagonal else 0
                    if at:
                        e.wait_ge(s["capped"], 8 * j + k + 1)
                        ins = e.activation(E[:, 0:P], capped[:, :], ACT.Exp)
                    if at < HALF - off:
                        ins = e.activation(E[:, at:HALF - off], negm_b[:, t0 + at:(hf + 1) * HALF], ACT.Exp, bias=g)
                    ins.then_inc(s["E_ready"], 1)

                e.wait_ge(s["st_full"], M * j + 1)
                weights(0)
                for m in range(M):
                    width = HALF - pieces[m][2]
                    e.wait_ge(s["st_full"], M * j + m + 2)
                    if m >= 2:
                        e.wait_ge(s["num_done"], M * j + m - 1)
                    e.activation(st_hi[:, m % 2, 0:width], st[:, 0:width], ACT.Copy).then_inc(s["st_hi"], 1)
                    if m + 1 < M:
                        weights(m + 1)

                def square(hf):
                    half = slice(hf * HALF, (hf + 1) * HALF)
                    e.wait_ge(s["gated"], 4 * j + 2 * hf + 2)
                    e.activation(sq[:, :, half], acc[:, :, half], ACT.Square).then_inc(s["squared"], 1)

                def root(hf):
                    half = slice(hf * HALF, (hf + 1) * HALF)
                    e.wait_ge(s["summed"], 2 * j + hf + 1)
                    e.activation(rstd[:, half], ps[:, 4 + hf, :], ACT.Sqrt, scale=1.0 / 256, bias=eps_col[:, :]).then_inc(s["rooted"], 1)

                square(0)
                root(0)
                square(1)
                root(1)
                for t in range(2):
                    e.wait_ge(multiplied, stream.number(N, 6 + t, j))
                    e.activation(tz[:, t, :], pair(t), ACT.Tanh, scale=0.5).then_inc(s["tz"], 1)
                for t in range(2):
                    e.wait_ge(s["f_full"], 2 * j + t + 1)
                    e.activation(out_hi[:, t, :], acc[:, t, :], ACT.Copy, scale=0.5).then_inc(s["out_hi"], 1)

        def dve(e):
            o = dve_steps(e)
            for w, v in tmp_free:
                e.wait_ge(w, v)
            o(e.memset(Y[:, :, :], 0.0))
            with e.Fori(0, MLSTM_HEADS) as j:
                o.enter(j, 25)
                o(e.memset(xpad[:, :, 0:X], 0.0))
                for t in range(2):
                    n = 2 * j + t
                    e.wait_ge(s["x_read"], n + 1)
                    o(e.tensor_scalar(acc[:, t, :], xpad[:, t, X:], col("ml_conv3", n), col("ml_conv_b", n), ALU.mult, ALU.add))
                    for back in (1, 2, 3):
                        ins = e.scalar_tensor_tensor(acc[:, t, :], xpad[:, t, X - back:X - back + S], col(f"ml_conv{3 - back}", n), acc[:, t, :], ALU.mult, ALU.add)
                        if back < 3:
                            o(ins)
                    ins.then_inc(s["conv"], 1)
                    e.wait_ge(s["u_hi"], n + 1)
                    e.tensor_tensor(u_lo[:, t, :], xpad[:, t, X:], f32(u_hi[:, t, :]), ALU.subtract).then_inc(s["u_ready"], 1)
                for t in range(2):
                    n = 2 * j + t
                    e.wait_ge(s["c_tanh"], n + 1)
                    e.scalar_tensor_tensor(acc[:, t, :], tc[:, t, :], 1.0, acc[:, t, :], ALU.add, ALU.mult).then_inc(s["c_full"], 1)
                    e.wait_ge(s["c_hi"], n + 1)
                    e.scalar_tensor_tensor(c_lo[:, t, :], acc[:, t, :], 0.5, f32(c_hi[:, t, :]), ALU.mult, ALU.subtract).then_inc(s["c_ready"], 1)
                for t in range(2):
                    e.wait_ge(s["o_read"], 2 * j + t + 1)
                    o(e.tensor_scalar(so[:, t, :], so[:, t, :], 1.0, 0.5, ALU.add, ALU.mult))
                for t in range(2):
                    e.wait_ge(s["v_hi"], 2 * j + t + 1)
                    half = slice(4 * t, 4 * t + 4)
                    e.tensor_tensor(v_lo[:, half, :].rearrange("p k n -> p (k n)"), pair(t), f32(v_hi[:, half, :].rearrange("p k n -> p (k n)")),
                                    ALU.subtract).then_inc(s["v_ready"], 1)

                def cap_weights(m):
                    hf, k, off = pieces[m]
                    if k:
                        e.wait_ge(s["E_ready"], M * j + diagonal[k - 1] + 1)
                    t0 = hf * HALF + off
                    e.scalar_tensor_tensor(capped[:, :], negm_b[:, t0:t0 + P], gate_cols[:, k, bass.ds(j, 1)], cap[:, :],
                                           ALU.add, ALU.min).then_inc(s["capped"], 1)

                def denominator(hf):
                    half = slice(hf * HALF, (hf + 1) * HALF)
                    e.wait_ge(s["num_done"], M * j + (M if hf else 4))
                    if hf == 0:
                        e.wait_ge(s["em_ready"], j + 1)
                    o(e.tensor_tensor(em[:, half], ps[:, den_bank[hf], :], em[:, half], ALU.max))
                    o(e.scalar_tensor_tensor(em[:, half], ps[:, den_bank[hf], :], -1.0, em[:, half], ALU.mult, ALU.max))

                def invert(hf, q0, q1):
                    t = slice(hf * HALF + q0 * P, hf * HALF + q1 * P)
                    o(e.reciprocal(em[:, t], em[:, t]))

                def divided(hf):
                    half = slice(hf * HALF, (hf + 1) * HALF)
                    for d in range(2):
                        e.tensor_tensor(acc[:, d, half], ps[:, num_bank[hf] + d, :], em[:, half], ALU.mult).then_inc(s["h_read"], 1)
                    e.wait_ge(s["h_read"], 4 * j + 2 * hf + 2)

                def gate(hf):
                    half = slice(hf * HALF, (hf + 1) * HALF)
                    for d in range(2):
                        e.tensor_tensor(acc[:, d, half], acc[:, d, half], so[:, d, half], ALU.mult).then_inc(s["gated"], 1)

                e.wait_ge(s["neg_loaded"], 16 * j + 16)
                cap_weights(0)
                for m in range(M):
                    width = HALF - pieces[m][2]
                    e.wait_ge(s["E_ready"], M * j + m + 1)
                    e.wait_ge(s["scored"], M * j + m + 1)
                    e.tensor_tensor(st[:, 0:width], ps[:, m % 2, 0:width], E[:, 0:width], ALU.mult).then_inc(s["st_full"], 1)
                    if m + 1 in diagonal:
                        cap_weights(m + 1)
                    e.wait_ge(s["st_hi"], M * j + m + 1)
                    e.tensor_tensor(st_lo[:, m % 2, 0:width], st[:, 0:width], f32(st_hi[:, m % 2, 0:width]), ALU.subtract).then_inc(s["st_ready"], 1)
                    e.wait_ge(s["st_ready"], M * j + m + 1)
                    if m == 4:
                        denominator(0)
                    elif m == 5:
                        invert(0, 0, 2)
                    elif m == 6:
                        invert(0, 2, 4)
                    elif m == 7:
                        divided(0)
                    elif m == 8:
                        gate(0)
                denominator(1)
                invert(1, 0, 4)
                divided(1)
                gate(1)
                o(e.tensor_tensor(c_full[:, :, :], f32(c_hi[:, :, :]), f32(c_lo[:, :, :]), ALU.add))
                for hf in range(2):
                    half = slice(hf * HALF, (hf + 1) * HALF)
                    e.wait_ge(s["rooted"], 2 * j + hf + 1)
                    o(e.reciprocal(rstd[:, half], rstd[:, half]))
                for t in range(2):
                    n = 2 * j + t
                    o(e.scalar_tensor_tensor(acc[:, t, :], acc[:, t, :], col("head_g", n), rstd[:, :], ALU.mult, ALU.mult))
                    o(e.scalar_tensor_tensor(acc[:, t, :], c_full[:, t, :], col("skip", n), acc[:, t, :], ALU.mult, ALU.add))
                    e.wait_ge(s["tz"], n + 1)
                    o(e.scalar_tensor_tensor(tz[:, t, :], tz[:, t, :], 1.0, pair(t), ALU.add, ALU.mult))
                    e.tensor_tensor(acc[:, t, :], acc[:, t, :], tz[:, t, :], ALU.mult).then_inc(s["f_full"], 1)
                    e.wait_ge(s["out_hi"], n + 1)
                    e.scalar_tensor_tensor(out_lo[:, t, :], acc[:, t, :], 0.5, f32(out_hi[:, t, :]), ALU.mult, ALU.subtract).then_inc(s["out_ready"], 1)
                for n in range(KT):
                    if n % 4 == 3:
                        e.wait_ge(multiplied, stream.number(N, 8 + n // 4, j))
                    else:
                        e.wait_ge(s["out_part"], 6 * j + 3 * (n // 4) + n % 4 + 1)
                    e.tensor_tensor(Y[:, n, :], Y[:, n, :], pair(n % 4), ALU.add).then_inc(s["y_added"], 1)
                e.wait_ge(s["y_added"], 8 * j + 2 * KT)
            o.leave(MLSTM_HEADS)

        return dict(sp=sp, pool=pool, pe=pe, act=act, dve=dve, ready=[(s["y_added"], KT * (MLSTM_HEADS + 1))])

    def merge(ready, part_stored):
        m_hi, m_lo, tg0, tg1, part0, part1 = carve(("m_hi", [P, KT, S], F32R), ("m_lo", [P, KT, S], F32R), *[(f"merge_{n}", [P, S], F32) for n in ("tg0", "tg1", "part0", "part1")])
        tg, part = (tg0, tg1), (part0, part1)
        part_loaded, g_read, full, hi_done, m_ready, out_ready = (
            sem(f"merge_{n}") for n in ("part_loaded", "g_read", "full", "hi", "m_ready", "out_ready"))
        credits.extend([(g_read, 4), (m_ready, 2), (full, 2), (out_ready, 4)])
        G, O = "merge", "final_out"

        def sp(e):
            load_chunks(e, G)
            load_chunks(e, O)

        def pool(e):
            split_chunks(e, G)
            split_chunks(e, O)

        def pe(e):
            for w, v in ready:
                e.wait_ge(w, v)
            with e.Fori(0, 2) as i:
                for c in range(4):
                    e.wait_ge(split, stream.number(G, c, i))
                    e.wait_ge(g_read, 4 * i + c + 1)
                    columns(e, stream.slot(G, c), c, H_hi, H_lo).then_inc(multiplied, 1)
            with e.Fori(0, 2) as i:
                for c in range(4):
                    e.wait_ge(split, stream.number(O, c, i))
                    e.wait_ge(g_read, 9 + c)
                    e.wait_ge(out_ready, 4 * i + c + 1)
                    columns(e, stream.slot(O, c), c, m_hi, m_lo, ready=[(m_ready, 2)] if c == 0 else None).then_inc(multiplied, 1)

        def act(e):
            for w, v in ready + [part_stored]:
                e.wait_ge(w, v)
            with e.Fori(0, 2) as i:
                for c in range(4):
                    n = 4 * i + c
                    e.wait_ge(full, n + 1)
                    e.dma_start(part[c % 2][:, :], part_dram[bass.ds(n, 1), :, :].rearrange("o p n -> p (o n)")).then_inc(part_loaded, 16)
                    e.wait_ge(multiplied, stream.number(G, c, i))
                    e.wait_ge(m_ready, n + 1)
                    e.activation(tg[c % 2][:, :], pair(c), ACT.Tanh, scale=0.5).then_inc(g_read, 1)
                    e.wait_ge(full, n + 3)
                    e.activation(tile(m_hi, n), tg[c % 2][:, :], ACT.Copy, scale=0.5).then_inc(hi_done, 1)

        def dve(e):
            o = dve_steps(e)
            for w, v in ready:
                e.wait_ge(w, v)
            with e.Fori(0, 2) as i:
                o.enter(i, 4)
                for c in range(4):
                    n = 4 * i + c
                    b = c % 2
                    e.wait_ge(g_read, n + 5)
                    o(e.scalar_tensor_tensor(tg[b][:, :], tg[b][:, :], 1.0, tile(Y, n), ALU.add, ALU.mult))
                    e.wait_ge(part_loaded, 16 * n + 16)
                    e.tensor_tensor(tg[b][:, :], tg[b][:, :], part[b][:, :], ALU.add).then_inc(full, 1)
                    e.wait_ge(hi_done, n + 1)
                    e.scalar_tensor_tensor(tile(m_lo, n), tg[b][:, :], 0.5, f32(tile(m_hi, n)), ALU.mult, ALU.subtract).then_inc(m_ready, 1)
                e.wait_ge(m_ready, 4 * i + 6)
            o.leave(2)
            with e.Fori(0, 2) as i:
                for c in range(4):
                    e.wait_ge(multiplied, stream.number(O, c, i))
                    e.tensor_copy(tile(Y, 4 * i + c), pair(c)).then_inc(out_ready, 1)

        return dict(sp=sp, pool=pool, pe=pe, act=act, dve=dve, y_ready=(out_ready, 4),
                    x_free=[(multiplied, stream.number(G, 3, 1))], sq_free=[(m_ready, KT + 2)])


    def constants(e):
        o = steps_of(e, "pool")
        o.step(e.memset(ident[:, :], 0.0))
        o.step(e.memset(causal_b[:, :], 0.0))
        o.step(e.memset(cap[:, :], 0.0))
        o.step(e.memset(eps_col[:, :], EPS))
        o.step(e.memset(one_col[:, :], 1.0))
        o.step(e.memset(ones[:, :], 1.0))
        o.step(e.memset(up_to[:, :], 1.0))
        o.step(e.memset(pick[:, :], 0.0))
        o.after(o.n)
        o(e.memset(pick[:, 0:KT * KT:KT + 1], 1.0))
        o(e.affine_select(out=ident[:, :], in_=ident[:, :], compare_op=ALU.not_equal, fill=1.0, base=0, pattern=[[-1, P]], channel_multiplier=1))
        o(e.affine_select(out=causal_b[:, :], in_=causal_b[:, :], compare_op=ALU.is_ge, fill=FILL, base=0, pattern=[[-1, P]], channel_multiplier=1))
        o(e.affine_select(out=cap[:, :], in_=cap[:, :], compare_op=ALU.is_ge, fill=FILL, base=0, pattern=[[1, P]], channel_multiplier=-1))
        o(e.affine_select(out=up_to[:, :], in_=up_to[:, :], compare_op=ALU.is_ge, fill=0.0, base=31, pattern=[[32, 4]], channel_multiplier=-1))
        o(e.tensor_copy(ones_r[:, :], ones[:, :]))
        e.tensor_copy(ident_b[:, :], ident[:, :]).then_inc(consts, 1)

    steps = []
    steps = []
    pl = prelude()
    b0 = boundary("b0", None, "mix_pre0", A["x_t"], None, [], pl["tmp_free"], "fox_pre")
    fx = fox(b0["h_ready"], b0["tmp_free"])
    b1 = boundary("b1", "mix_post0", "ffn_pre0", A["x_t"], fx["y_ready"], fx["x_free"], fx["sq_free"], "ffn0_first", x_at=tmp_at)
    f0 = ffn(0, b1["h_ready"], b1["tmp_free"])
    b2 = boundary("b2", "ffn_post0", "mix_pre1", x_dram, f0["y_ready"], f0["x_free"], f0["sq_free"], "lru_first")
    lr = lru(b2["h_ready"], b2["tmp_free"])
    b3 = boundary("b3", "mix_post1", "ffn_pre1", x_dram, lr["y_ready"], lr["x_free"], lr["sq_free"], "ffn1_first")
    f1 = ffn(1, b3["h_ready"], b3["tmp_free"])
    b4 = boundary("b4", "ffn_post1", "norm_pre", x_dram, f1["y_ready"], f1["x_free"], f1["sq_free"], "s5_u")
    s5_ = s5(b4["h_ready"], b4["tmp_free"])
    gl = glu(s5_["ys"], s5_["ready"])
    so = s5_out(gl["yo"], gl["ready"], gl["banks_free"])
    ml = mlstm(b4["h_ready"], so["tmp_free"], so["rows_stored"])
    mg = merge(ml["ready"], so["part_stored"])
    b5 = boundary("b5", "norm_post", None, x_dram, mg["y_ready"], mg["x_free"], mg["sq_free"])
    steps += [pl, b0, fx, b1, f0, b2, lr, b3, f1, b4, s5_, gl, so, ml, mg, b5]

    def run(engine, which):
        for step in steps:
            if which in step:
                step[which](engine)

    with nc.Block() as block:
        @block.sync
        def _(e):
            for s, n in credits:
                e.sem_inc(s, n)
            e.dma_start(par[:, :], A["params"]).then_inc(params_loaded, 16)
            run(e, "sp")

        @block.gpsimd
        def _(e):
            constants(e)
            run(e, "pool")

        @block.tensor
        def _(e):
            e.wait_ge(consts, 1)
            run(e, "pe")

        @block.scalar
        def _(e):
            e.wait_ge(consts, 1)
            e.wait_ge(params_loaded, 16)
            run(e, "act")

        @block.vector
        def _(e):
            e.wait_ge(consts, 1)
            e.wait_ge(params_loaded, 16)
            run(e, "dve")


def kernel(**inputs):
    import concourse.bacc as bacc
    from concourse.bass_utils import run_bass_kernel_spmd

    v = {k: np.asarray(a) for k, a in inputs.items()}

    def columns_of(a):
        return np.ascontiguousarray(a.reshape(-1, P).T)

    packed = {"od_conv_b": v["od_conv_b"], "od_b_a": v["od_b_a"], "od_b_x": v["od_b_x"], "od_lam": v["od_lam"],
              "norm_pre": v["norm_pre_g_2"], "ml_conv_b": v["conv_b_2"], "head_g": v["head_g_2"], "skip": v["skip_a_2"],
              "norm_post": v["norm_post_g_2"], "pool_scale": v["ev_pool_scale"], "d_skip": v["D_skip_2"], "b_glu": v["b_glu_2"],
              "lam_re": v["lam_re_2"], "lam_im": v["lam_im_2"], "log_dt": np.repeat(v["log_dt_2"].reshape(-1, 1), 64, axis=1)}
    for l in range(2):
        packed |= {f"mix_pre{l}": v["mix_pre_g"][l], f"mix_post{l}": v["mix_post_g"][l],
                   f"ffn_pre{l}": v["ffn_pre_g"][l], f"ffn_post{l}": v["ffn_post_g"][l]}
    for t in range(4):
        packed |= {f"od_conv{t}": v["od_conv_w"][0, t], f"ml_conv{t}": v["conv_w_2"][0, t]}
    params = np.zeros((P, n_columns), np.float32)
    for name, n in VECTORS:
        if name in packed:
            params[:, COLUMN[name]:COLUMN[name] + n] = columns_of(packed[name])
    params[0:8, COLUMN["row_bias"]] = v["ev_b_f"][0]
    params[0:4, COLUMN["row_bias"] + 1] = v["b_i_2"][0]
    params[0:4, COLUMN["row_bias"] + 2] = v["b_f_2"][0]
    for g, w in enumerate(POOL_WINDOWS):
        at = COLUMN["inv_count"] + PAD * g
        params[:, at:at + PAD] = [1.0 / min(t + 1, w) for t in range(PAD)]
    s5_b = np.zeros((P, STATE_TILES, 2, 32), np.float32)
    s5_c = np.zeros((P, STATE_TILES, 2, 32), np.float32)
    for g in range(32):
        n, at, ch = g // 2, 64 * (g % 2), 16 * (g % 2)
        for part, (b, c) in enumerate(((v["B_re_2"], v["C_re_2"]), (v["B_im_2"], v["C_im_2"]))):
            s5_b[at:at + 64, n, part, ch:ch + 16] = b[0, g]
            s5_c[at:at + 64, n, part, ch:ch + 16] = c[0, g].T
    arrays = {
        "x_t": np.ascontiguousarray(v["x"][0].T).reshape(KT, P, S), "params": params,
        "s5_b": s5_b, "s5_c": s5_c,
        "ev_w_in": v["ev_w_in"][0], "ev_pool_w": v["ev_pool_w"].reshape(512, P), "ev_w_out": v["ev_w_out"][0],
        "ffn_w_gate": v["ffn_w_gate"], "ffn_w_up": v["ffn_w_up"], "ffn_w_down": v["ffn_w_down"],
        "od_w_in": v["od_w_in"][0], "od_w_a": v["od_w_a"].reshape(D, 256), "od_w_x": v["od_w_x"].reshape(D, 256), "od_w_out": v["od_w_out"][0],
        "w_in_2": v["w_in_2"][0], "w_q_2": v["w_q_2"].reshape(D, 256), "w_k_2": v["w_k_2"].reshape(D, 256), "w_v_2": v["w_v_2"].reshape(D, 256),
        "w_a_out_2": v["w_a_out_2"][0], "w_glu_2": v["w_glu_2"][0], "w_b_out_2": v["w_b_out_2"][0], "w_o_2": v["w_o_2"][0],
    }
    nc = bacc.Bacc("TRN2", target_bir_lowering=False, num_devices=1, dynamic_dma_scratch_size=1024)
    maps, handles = {}, {}
    for name, a in arrays.items():
        maps[f"in_{name}"] = np.ascontiguousarray(a)
        handles[name] = nc.dram_tensor(f"in_{name}", a.shape, F32, kind="ExternalInput").ap()
    out = nc.dram_tensor("out", (KT, P, S), F32, kind="ExternalOutput").ap()
    block_program(nc, handles, out)
    r = run_bass_kernel_spmd(nc, [maps], core_ids=[0])
    return np.ascontiguousarray(np.asarray(r.results[0]["out"]).reshape(D, S).T).reshape(1, S, D)
```
